# Optimizing a Trainium2 kernel written in Bass

```python
import math
import jax, jax.numpy as jnp
from jax import lax
import numpy as np

'''
One inference step of a 4-layer hybrid autoregressive decoder trunk built from
parallel head groups (Hymba-style). Each layer:
  h = RMSNorm(x)
  z = h @ W_in        (one combined projection; columns split among all head groups)
  group A: DSA sparse attention. Indexer I[t,s] = sum_h w[t,h] relu(q_idx[t,h].k_idx[s]),
           each query keeps top-k admissible keys (k = min(256, L/4)), gathers those K/V rows,
           GQA softmax attention (8 q heads / 2 kv heads) + shared T5 relative bias.
  group B: GLA gated linear attention, 4 heads, low-rank sigmoid^(1/16) forget gate,
           chunked exact form of S_t = diag(a_t) S_{t-1} + k_t^T v_t, o_t = q_t S_t,
           per-head RMSNorm and swish output gate.
  x = x + concat(A, B) @ W_out ;  x = x + SwiGLU(RMSNorm(x)).
Final RMSNorm.

Inputs
  x_prompt   (BATCH, SEQ, D_MODEL)          positions 0..SEQ-1
  x_sample   (DEC_BATCH, DEC_SEQ, D_MODEL)  positions PAST_LEN..PAST_LEN+DEC_SEQ-1
  cache_k    (DEPTH, N_POOL, PAGE_SIZE, ATTN_KV_HEADS, HEAD_DIM)  paged
  cache_v    (DEPTH, N_POOL, PAGE_SIZE, ATTN_KV_HEADS, HEAD_DIM)  paged
  cache_idx_k(DEPTH, N_POOL, PAGE_SIZE, IDX_DIM)                  paged indexer keys
  state_gla  (DEPTH, DEC_BATCH, GLA_HEADS, GLA_DK, GLA_DV)        recurrent state
  page_table (DEC_BATCH, N_PAGES) int32, N_PAGES = PAST_LEN // PAGE_SIZE
  weights (stacked over DEPTH) and the shared rel_bias (REL_BUCKETS, ATTN_HEADS).

Returns tuple
  y_prompt         (BATCH, SEQ, D_MODEL)
  y_sample         (DEC_BATCH, DEC_SEQ, D_MODEL)
  new_k_prompt     (DEPTH, BATCH, SEQ, ATTN_KV_HEADS, HEAD_DIM)
  new_v_prompt     (DEPTH, BATCH, SEQ, ATTN_KV_HEADS, HEAD_DIM)
  new_idx_k_prompt (DEPTH, BATCH, SEQ, IDX_DIM)
  new_gla_prompt   (DEPTH, BATCH, GLA_HEADS, GLA_DK, GLA_DV)
  new_k_sample     (DEPTH, DEC_BATCH, DEC_SEQ, ATTN_KV_HEADS, HEAD_DIM)
  new_v_sample     (DEPTH, DEC_BATCH, DEC_SEQ, ATTN_KV_HEADS, HEAD_DIM)
  new_idx_k_sample (DEPTH, DEC_BATCH, DEC_SEQ, IDX_DIM)
  new_gla_sample   (DEPTH, DEC_BATCH, GLA_HEADS, GLA_DK, GLA_DV)
'''

D_MODEL = 1024
BATCH = 1
SEQ = 2048
DEPTH = 1
DEC_BATCH = 8
DEC_SEQ = 8
PAST_LEN = 512
PAGE_SIZE = 128

ATTN_HEADS = 8
ATTN_KV_HEADS = 2
HEAD_DIM = 64
ATTN_REP = ATTN_HEADS // ATTN_KV_HEADS
ATTN_WIDTH = ATTN_HEADS * HEAD_DIM
KV_WIDTH = ATTN_KV_HEADS * HEAD_DIM
IDX_HEADS = 8
IDX_DIM = 64
IDX_TOPK_MAX = 256
Q_BLOCK = 128
GLA_HEADS = 4
GLA_DK = 64
GLA_DV = 128
GLA_K_WIDTH = GLA_HEADS * GLA_DK
GLA_V_WIDTH = GLA_HEADS * GLA_DV
GLA_GATE_RANK = 16
GLA_GATE_TAU = 16.0
GLA_CHUNK = 64
MIX_WIDTH = ATTN_WIDTH + GLA_V_WIDTH
D_FF = -(-8 * D_MODEL // (3 * 256)) * 256
REL_BUCKETS = 32
REL_MAX_DIST = 128
RMS_EPS = 1e-6
LN_EPS = 1e-5
PROJ_SPLIT = (ATTN_WIDTH, KV_WIDTH, KV_WIDTH, IDX_HEADS * IDX_DIM, IDX_DIM, IDX_HEADS,
              GLA_K_WIDTH, GLA_K_WIDTH, GLA_V_WIDTH, GLA_V_WIDTH, GLA_GATE_RANK)
IN_COLS = sum(PROJ_SPLIT)

kernel_name = 'hymba_dsa_gla_decoder_step'

def rmsnorm(x, g):
    x32 = x.astype(jnp.float32)
    y = x32 * lax.rsqrt(jnp.mean(x32 * x32, axis=-1, keepdims=True) + RMS_EPS)
    return (y * g.astype(jnp.float32)).astype(x.dtype)

def layernorm(x, g, b):
    x32 = x.astype(jnp.float32)
    xc = x32 - jnp.mean(x32, axis=-1, keepdims=True)
    y = xc * lax.rsqrt(jnp.mean(xc * xc, axis=-1, keepdims=True) + LN_EPS)
    return (y * g.astype(jnp.float32) + b.astype(jnp.float32)).astype(x.dtype)

def split_points():
    return tuple(int(c) for c in np.cumsum(PROJ_SPLIT)[:-1])

def rel_bucket(dist):
    n = jnp.maximum(dist, 0)
    max_exact = REL_BUCKETS // 2
    large = max_exact + (jnp.log(jnp.maximum(n, 1).astype(jnp.float32) / max_exact)
                         / math.log(REL_MAX_DIST / max_exact)
                         * (REL_BUCKETS - max_exact)).astype(jnp.int32)
    large = jnp.minimum(large, REL_BUCKETS - 1)
    return jnp.where(n < max_exact, n, large)

def project(h, w_in_l, kn_g, kn_b, gate_up_l, gate_b_l):
    B, T = h.shape[:2]
    z = jnp.einsum('btd,dc->btc', h, w_in_l)
    q, k, v, iq, ik, iw, gq, gk, gv, gr, glr = jnp.split(z, split_points(), axis=-1)
    q = q.reshape(B, T, ATTN_HEADS, HEAD_DIM)
    k = k.reshape(B, T, ATTN_KV_HEADS, HEAD_DIM)
    v = v.reshape(B, T, ATTN_KV_HEADS, HEAD_DIM)
    iq = iq.reshape(B, T, IDX_HEADS, IDX_DIM)
    ik = layernorm(ik, kn_g, kn_b)
    iw = iw * (IDX_HEADS ** -0.5 * IDX_DIM ** -0.5)
    gq = gq.reshape(B, T, GLA_HEADS, GLA_DK) * (GLA_DK ** -0.5)
    gk = gk.reshape(B, T, GLA_HEADS, GLA_DK)
    gv = gv.reshape(B, T, GLA_HEADS, GLA_DV)
    gate = jnp.einsum('btr,rc->btc', glr, gate_up_l) + gate_b_l
    log_a = (jax.nn.log_sigmoid(gate.astype(jnp.float32)) / GLA_GATE_TAU).reshape(B, T, GLA_HEADS, GLA_DK)
    return q, k, v, iq, ik, iw, gq, gk, gv, gr, log_a

def dsa_attention(q, iq, iw, t_pos, idx_keys, gather_kv, topk, rel_bias):
    B, T = q.shape[:2]
    L = idx_keys.shape[1]
    qb = math.gcd(T, Q_BLOCK)
    nb = T // qb
    key_pos = jnp.arange(L, dtype=jnp.int32)

    def blockify(a):
        return jnp.moveaxis(a.reshape((B, nb, qb) + a.shape[2:]), 1, 0)

    def one_block(args):
        qs, iqs, iws, tp = args
        dots = jnp.einsum('bqhd,bsd->bqhs', iqs, idx_keys)
        score = jnp.einsum('bqh,bqhs->bqs', iws, jax.nn.relu(dots)).astype(jnp.float32)
        admissible = key_pos[None, :] <= tp[:, None]
        score = jnp.where(admissible[None], score, -jnp.inf)
        _, sel = lax.top_k(score, topk)
        valid = sel <= tp[None, :, None]
        kg, vg = gather_kv(sel)
        qg = qs.reshape(B, qb, ATTN_KV_HEADS, ATTN_REP, HEAD_DIM)
        logits = jnp.einsum('bqgrd,bqkgd->bqgrk', qg, kg).astype(jnp.float32) * (HEAD_DIM ** -0.5)
        bias = rel_bias[rel_bucket(tp[None, :, None] - sel)]
        bias = jnp.moveaxis(bias, -1, 2).reshape(B, qb, ATTN_KV_HEADS, ATTN_REP, topk)
        logits = jnp.where(valid[:, :, None, None, :], logits + bias.astype(jnp.float32), -jnp.inf)
        p = jax.nn.softmax(logits, axis=-1).astype(vg.dtype)
        o = jnp.einsum('bqgrk,bqkgd->bqgrd', p, vg)
        return o.reshape(B, qb, ATTN_WIDTH)

    out = lax.map(one_block, (blockify(q), blockify(iq), blockify(iw), t_pos.reshape(nb, qb)))
    return jnp.moveaxis(out, 0, 1).reshape(B, T, ATTN_WIDTH)

def gla_chunked(q, k, v, log_a, s0):
    B, T, H, _ = q.shape
    C = min(GLA_CHUNK, T)
    pad = (-T) % C
    nc = (T + pad) // C

    def chunks(a):
        a = jnp.pad(a.astype(jnp.float32), ((0, 0), (0, pad), (0, 0), (0, 0)))
        return a.reshape(B, nc, C, H, a.shape[-1]).transpose(1, 0, 3, 2, 4)

    causal = jnp.tril(jnp.ones((C, C), dtype=bool))

    def step(S, xs):
        qc, kc, vc, gc = xs
        b = jnp.cumsum(gc, axis=2)
        o_inter = jnp.einsum('bhtd,bhde->bhte', qc * jnp.exp(b), S)
        diff = b[:, :, :, None, :] - b[:, :, None, :, :]
        decay = jnp.exp(jnp.where(causal[:, :, None], diff, -jnp.inf))
        A = jnp.einsum('bhtd,bhsd,bhtsd->bhts', qc, kc, decay)
        o_intra = jnp.einsum('bhts,bhse->bhte', A, vc)
        b_last = b[:, :, -1:, :]
        S_new = jnp.exp(b_last[:, :, 0, :])[..., None] * S + jnp.einsum('bhsd,bhse->bhde', kc * jnp.exp(b_last - b), vc)
        return S_new, o_inter + o_intra

    S_fin, o = lax.scan(step, s0.astype(jnp.float32), (chunks(q), chunks(k), chunks(v), chunks(log_a)))
    o = o.transpose(1, 0, 3, 2, 4).reshape(B, nc * C, H, GLA_DV)[:, :T]
    return o, S_fin

def gla_readout(o, r, g):
    B, T = o.shape[:2]
    y = o * lax.rsqrt(jnp.mean(o * o, axis=-1, keepdims=True) + RMS_EPS) * g.astype(jnp.float32)
    return y.reshape(B, T, GLA_V_WIDTH) * jax.nn.silu(r.astype(jnp.float32))

def residual_block(x, attn_o, gla_o, w_out_l, ffn_g, wg, wu, wd):
    mix = jnp.concatenate([attn_o.astype(x.dtype), gla_o.astype(x.dtype)], axis=-1)
    x = x + jnp.einsum('btc,cd->btd', mix, w_out_l)
    h = rmsnorm(x, ffn_g)
    u = jax.nn.silu(jnp.einsum('btd,df->btf', h, wg)) * jnp.einsum('btd,df->btf', h, wu)
    return x + jnp.einsum('btf,fd->btd', u, wd)

def setup_inputs(seed: int = 0) -> dict:
    key = jax.random.key(seed)
    ks = jax.random.split(key, 24)
    f32 = jnp.float32
    n_pages = PAST_LEN // PAGE_SIZE
    n_used = DEC_BATCH * n_pages
    n_pool = n_used + max(1, n_used // 4)

    def nrm(k, shape, s):
        return jax.random.normal(k, shape, f32) * s

    page_table = jax.random.permutation(ks[0], n_pool)[:n_used].reshape(DEC_BATCH, n_pages).astype(jnp.int32)
    return {
        'x_prompt': nrm(ks[1], (BATCH, SEQ, D_MODEL), 1.0),
        'x_sample': nrm(ks[2], (DEC_BATCH, DEC_SEQ, D_MODEL), 1.0),
        'cache_k': nrm(ks[3], (DEPTH, n_pool, PAGE_SIZE, ATTN_KV_HEADS, HEAD_DIM), 1.0),
        'cache_v': nrm(ks[4], (DEPTH, n_pool, PAGE_SIZE, ATTN_KV_HEADS, HEAD_DIM), 1.0),
        'cache_idx_k': nrm(ks[5], (DEPTH, n_pool, PAGE_SIZE, IDX_DIM), 1.0),
        'state_gla': nrm(ks[6], (DEPTH, DEC_BATCH, GLA_HEADS, GLA_DK, GLA_DV), 1.0),
        'page_table': page_table,
        'attn_norm_g': 1.0 + nrm(ks[7], (DEPTH, D_MODEL), 0.02),
        'w_in': nrm(ks[8], (DEPTH, D_MODEL, IN_COLS), D_MODEL ** -0.5),
        'idx_knorm_g': 1.0 + nrm(ks[9], (DEPTH, IDX_DIM), 0.02),
        'idx_knorm_b': nrm(ks[10], (DEPTH, IDX_DIM), 0.02),
        'gla_gate_up': nrm(ks[11], (DEPTH, GLA_GATE_RANK, GLA_K_WIDTH), GLA_GATE_RANK ** -0.5),
        'gla_gate_b': nrm(ks[12], (DEPTH, GLA_K_WIDTH), 0.1),
        'gla_onorm_g': 1.0 + nrm(ks[13], (DEPTH, GLA_DV), 0.02),
        'w_out': nrm(ks[14], (DEPTH, MIX_WIDTH, D_MODEL), MIX_WIDTH ** -0.5),
        'ffn_norm_g': 1.0 + nrm(ks[15], (DEPTH, D_MODEL), 0.02),
        'w_gate': nrm(ks[16], (DEPTH, D_MODEL, D_FF), D_MODEL ** -0.5),
        'w_up': nrm(ks[17], (DEPTH, D_MODEL, D_FF), D_MODEL ** -0.5),
        'w_down': nrm(ks[18], (DEPTH, D_FF, D_MODEL), D_FF ** -0.5),
        'rel_bias': nrm(ks[19], (REL_BUCKETS, ATTN_HEADS), 0.5),
        'final_norm_g': 1.0 + nrm(ks[20], (D_MODEL,), 0.02),
    }

def reference(x_prompt, x_sample, cache_k, cache_v, cache_idx_k, state_gla, page_table,
              attn_norm_g, w_in, idx_knorm_g, idx_knorm_b, gla_gate_up, gla_gate_b, gla_onorm_g,
              w_out, ffn_norm_g, w_gate, w_up, w_down, rel_bias, final_norm_g):
    B, T = x_prompt.shape[:2]
    DB, TS = x_sample.shape[:2]
    page = cache_k.shape[2]
    past_len = page_table.shape[1] * page
    topk_p = min(IDX_TOPK_MAX, T // 4)
    topk_s = min(IDX_TOPK_MAX, (past_len + TS) // 4)
    pos_p = jnp.arange(T, dtype=jnp.int32)
    pos_s = past_len + jnp.arange(TS, dtype=jnp.int32)
    seq_ids = jnp.arange(DB)[:, None, None]
    take = jax.vmap(lambda rows, i: rows[i])

    xp, xs = x_prompt, x_sample
    kp_l, vp_l, ikp_l, sp_l = [], [], [], []
    ks_l, vs_l, iks_l, ss_l = [], [], [], []
    for l in range(DEPTH):
        h = rmsnorm(xp, attn_norm_g[l])
        q, k, v, iq, ik, iw, gq, gk, gv, gr, la = project(h, w_in[l], idx_knorm_g[l], idx_knorm_b[l], gla_gate_up[l], gla_gate_b[l])

        def gather_p(sel, k=k, v=v):
            return take(k, sel), take(v, sel)

        a_o = dsa_attention(q, iq, iw, pos_p, ik, gather_p, topk_p, rel_bias)
        g_o, S = gla_chunked(gq, gk, gv, la, jnp.zeros((B, GLA_HEADS, GLA_DK, GLA_DV), jnp.float32))
        g_o = gla_readout(g_o, gr, gla_onorm_g[l])
        xp = residual_block(xp, a_o, g_o, w_out[l], ffn_norm_g[l], w_gate[l], w_up[l], w_down[l])
        kp_l.append(k); vp_l.append(v); ikp_l.append(ik); sp_l.append(S.astype(state_gla.dtype))

        h = rmsnorm(xs, attn_norm_g[l])
        q, k, v, iq, ik, iw, gq, gk, gv, gr, la = project(h, w_in[l], idx_knorm_g[l], idx_knorm_b[l], gla_gate_up[l], gla_gate_b[l])
        ck, cv = cache_k[l], cache_v[l]
        past_ik = cache_idx_k[l][page_table].reshape(DB, past_len, IDX_DIM)
        keys_idx = jnp.concatenate([past_ik, ik.astype(past_ik.dtype)], axis=1)

        def gather_s(sel, ck=ck, cv=cv, k=k, v=v):
            is_new = (sel >= past_len)[..., None, None]
            sp = jnp.minimum(sel, past_len - 1)
            phys = page_table[seq_ids, sp // page]
            off = sp % page
            sn = jnp.clip(sel - past_len, 0, TS - 1)
            kg = jnp.where(is_new, take(k, sn).astype(ck.dtype), ck[phys, off])
            vg = jnp.where(is_new, take(v, sn).astype(cv.dtype), cv[phys, off])
            return kg, vg

        a_o = dsa_attention(q, iq, iw, pos_s, keys_idx, gather_s, topk_s, rel_bias)
        g_o, S = gla_chunked(gq, gk, gv, la, state_gla[l])
        g_o = gla_readout(g_o, gr, gla_onorm_g[l])
        xs = residual_block(xs, a_o, g_o, w_out[l], ffn_norm_g[l], w_gate[l], w_up[l], w_down[l])
        ks_l.append(k); vs_l.append(v); iks_l.append(ik); ss_l.append(S.astype(state_gla.dtype))

    y_prompt = rmsnorm(xp, final_norm_g)
    y_sample = rmsnorm(xs, final_norm_g)
    new_k_prompt = jnp.stack(kp_l)
    new_v_prompt = jnp.stack(vp_l)
    new_idx_k_prompt = jnp.stack(ikp_l)
    new_gla_prompt = jnp.stack(sp_l)
    new_k_sample = jnp.stack(ks_l)
    new_v_sample = jnp.stack(vs_l)
    new_idx_k_sample = jnp.stack(iks_l)
    new_gla_sample = jnp.stack(ss_l)
    return (y_prompt, y_sample, new_k_prompt, new_v_prompt, new_idx_k_prompt, new_gla_prompt,
            new_k_sample, new_v_sample, new_idx_k_sample, new_gla_sample)


_drawn_inputs = setup_inputs


def setup_inputs(seed=0):
    import zlib

    import numpy as np

    out = dict(_drawn_inputs(seed))
    spreads = {}
    factors = {'gla_onorm_g': 6.374, 'ffn_norm_g': 4.097, 'final_norm_g': 8.732, 'rel_bias': 3.58}
    for name, (base, spread) in spreads.items():
        noise = np.random.default_rng([zlib.crc32(name.encode()), seed]).standard_normal(out[name].shape)
        drawn = base * np.exp(spread * noise) if base else spread * noise
        out[name] = __import__('jax').numpy.asarray(drawn.astype(out[name].dtype))
    for name, factor in factors.items():
        out[name] = (out[name] * factor).astype(out[name].dtype)
    return out
```

```python
from contextlib import ExitStack

import numpy as np

import concourse.bass as bass
from concourse import mybir

F32 = mybir.dt.float32
I32 = mybir.dt.int32
ALU = mybir.AluOpType
ACT = mybir.ActivationFunctionType
AX = mybir.AxisListType

D = 1024
KT = D // 128
SEQ = 2048
TOK = 512
NBLK = SEQ // TOK
DB, TS = 8, 8
NS = DB * TS
ALLT = SEQ + NS
PAST = 512
PAGE = 128
NPG = PAST // PAGE
NPOOL = 40
LS = PAST + NS
HEADS, KVH, HD = 8, 2, 64
GH, DK, DV = 4, 64, 128
CH = 64
RANK = 16
FF = 2816
NF = FF // 128
TOPK = 256
TOPK_S = (PAST + TS) // 4
RB, RD = 32, 128
EPS, LN_EPS = 1e-6, 1e-5
OUTSIDE = -1e30
TAKEN = -3e38
TAKEN_CUT = -2e38
W1, W2 = 384, 528

FEATURE_TILES = ([("iq", j) for j in range(4)] + [("ik", 0)] + [("k", g) for g in range(2)]
                 + [("q", j) for j in range(4)] + [("gq", j) for j in range(2)]
                 + [("gk", j) for j in range(2)] + [("gr", j) for j in range(4)])
TOKEN_TILES = [("v", 0)] + [("gv", j) for j in range(4)]
TILES = FEATURE_TILES + TOKEN_TILES + [("glr", 0)]
P_UNITS = TILES + [("iw", 0)]
NP_SLOT = 14
SLOT_TILES = [(2 * s, 2 * s + 1) for s in range(11)] + [(22,), (23,), (24,)]
SLOT_OF = {t: s for s, ts in enumerate(SLOT_TILES) for t in ts}

C_ID, C_ONE, C_TRI, C_TRI8, C_ROW, C_SEQ, C_RST, C_RST8, C_EPS, C_LNEPS = (
    0, 128, 256, 320, 384, 392, 456, 968, 1032, 1033)
NC_COLS = 1034


def bucket_table():
    n = np.arange(1024)
    f = np.log(np.maximum(n, 1).astype(np.float32) / np.float32(RB // 2)) / np.float32(np.log(RD / (RB // 2)))
    large = np.minimum(RB // 2 + (f * np.float32(RB - RB // 2)).astype(np.int32), RB - 1)
    return np.where(n < RB // 2, n, large)


def constants():
    c = np.zeros((128, NC_COLS), np.float32)
    p = np.arange(128)[:, None]
    t64 = np.arange(64)[None, :]
    c[:, C_ID:C_ID + 128] = np.eye(128)
    c[:, C_ONE:C_ONE + 128] = 1.0
    c[:, C_TRI:C_TRI + 64] = (p % 64) <= t64
    same = (p // TS == t64 // TS) & (p <= t64)
    c[:, C_TRI8:C_TRI8 + 64] = same
    c[:, C_ROW:C_ROW + 8] = (p // TS) == np.arange(8)[None, :]
    c[:, C_SEQ:C_SEQ + 64] = np.where((p // TS == t64 // TS) & (p >= t64), 0.0, OUTSIDE)
    c[:, C_RST:C_RST + TOK] = (np.arange(TOK) % CH) != 0
    c[:, C_RST8:C_RST8 + NS] = (np.arange(NS) % TS) != 0
    c[:, C_EPS] = EPS
    c[:, C_LNEPS] = LN_EPS
    rep = np.zeros((64, DB, HEADS * TS), np.float32)
    for b in range(DB):
        for m in range(HEADS * TS):
            rep[b * TS + m % TS, b, m] = 1.0
    bucket = bucket_table()
    far = bucket == RB - 1
    assert far[RD:].all()
    hot1 = np.zeros((RB, W1), np.float32)
    hot2 = np.zeros((RB, W2), np.float32)
    for u in range(W1):
        hot1[bucket[max(255 - u, 0)], u] += 1.0
    for u in range(W2):
        hot2[bucket[max(PAST + TS - 1 - u, 0)], u] += 1.0
    hot1[RB - 1] -= 1.0
    hot2[RB - 1] -= 1.0
    return c, rep.reshape(64, -1), np.concatenate([hot1, hot2], 1)


def near_chunks(i):
    keys = 128 * (i + 1)
    near = min(256, keys)
    far = keys - near
    out = [(a, min(512, far - a), False) for a in range(0, far, 512)]
    return out + [(far, near, True)]


def score_chunks(i):
    keys = 128 * (i + 1)
    return [(a, min(512, keys - a)) for a in range(0, keys, 512)]


def layer(nc, a):
    with ExitStack() as ctx:
        def sb(name, shape, dt=F32):
            return ctx.enter_context(nc.sbuf_tensor(name, shape, dt))

        bank = [ctx.enter_context(nc.psum_tensor(f"bank{i}", [128, 512], F32)) for i in range(8)]
        skew1 = nc.dram_tensor("skew1", (HEADS, 128, W1), F32, kind="Internal").ap()
        skew2 = nc.dram_tensor("skew2", (HEADS, TS, W2), F32, kind="Internal").ap()

        cst = sb("cst", [128, NC_COLS])
        kT = sb("kT", [128, KVH, ALLT])
        ikT = sb("ikT", [128, ALLT])
        vtok = sb("vtok", [128, SEQ // 128, 128])
        vnew = sb("vnew", [NS, 128])
        near_bias = sb("near_bias", [128, HEADS, 256])
        sbias = sb("sbias", [HEADS * TS, PAST + TS])
        gvec = sb("gvec", [128, 3 * KT])
        gates = sb("gates", [128, 5])
        gate_up = sb("gate_up", [RANK, 2 * 128])
        state = sb("state", [128, 2, DV])
        X = sb("X", [128, KT, TOK])
        H = sb("H", [128, KT, TOK])
        q = sb("q", [128, 4, TOK])
        iw = sb("iw", [128, TOK // 128, 8])
        scores = sb("scores", [128, 4 * SEQ])
        R = sb("R", [128, NF * TOK])
        mixA = sb("mixA", [128, 4, TOK])
        mixG = sb("mixG", [128, 2, GH, TOK])
        ring = sb("ring", [128, 2, 2 * KT * 128])
        top8 = sb("top8", [128, 8])
        mx = sb("mx", [128, 2, 8])
        nmax = sb("nmax", [128, 2])
        den = sb("den", [128, 2])
        rden = sb("rden", [128, 2])
        pages = sb("pages", [1, DB * NPG], I32)

        ident = cst[:, C_ID:C_ID + 128]
        ones = cst[:, C_ONE:C_ONE + 128]
        eps = cst[:, C_EPS:C_EPS + 1]
        lneps = cst[:, C_LNEPS:C_LNEPS + 1]

        def cut(t, at, *dims):
            n = int(np.prod(dims))
            v = t[:, at:at + n]
            if len(dims) == 1:
                return v
            if len(dims) == 2:
                return v.rearrange("p (a b) -> p a b", b=dims[1])
            return v.rearrange("p (a b c) -> p a b c", b=dims[1], c=dims[2])

        Xf = X[:, :, :].rearrange("p k n -> p (k n)")
        Hf = H[:, :, :].rearrange("p k n -> p (k n)")
        Sf = scores[:, :]
        Rf = R[:, :]
        hots = cut(Rf, 0, W1 + W2)
        relb = cut(Rf, 1024, HEADS)
        relw = cut(Rf, 1032, HEADS, 128)
        row1 = cut(Rf, 2056, HEADS, W1)
        row2 = cut(Rf, 2056 + HEADS * W1, HEADS, W2)
        sq = cut(Rf, 0, KT, TOK)
        iq = cut(Rf, 0, 4, TOK)
        gq = cut(Rf, 2048, 2, TOK)
        gk = cut(Rf, 3072, 2, TOK)
        gr = cut(Rf, 4096, 4, TOK)
        la = cut(Rf, 6144, 2, TOK)
        gv = cut(Rf, 7168, 4, TOK)
        glr = cut(Rf, 9216, TOK)
        att = cut(Rf, 9728, 2, 4, 128)
        khs = cut(Rf, 9728, 256)
        atts = cut(Rf, 9984, 4, 64)
        cum = cut(Sf, 0, 2, TOK)
        exa = cut(Sf, 1024, 2, TOK)
        exb = cut(Sf, 2048, 2, TOK)
        qgz = cut(Sf, 3072, 4, TOK)
        qiz = cut(Sf, 5120, 4, TOK)
        ikx = cut(Sf, 7168, TOK)
        ikc = cut(Sf, 7680, TOK)
        exe = cut(Sf, 7168, 2, TOK)
        gvz = cut(Sf, 2048, 2, 512)
        nG = [cut(Xf, 512 * j, TOK) for j in range(4)]
        kg = cut(Xf, 0, 2, TOK)
        kh = cut(Xf, 1024, 2, TOK)
        khz = cut(Xf, 2048, 4, 2, 256)
        sin = cut(Xf, 2048, DB, 2, DV)
        oT = cut(Hf, 0, GH, TOK)
        o2 = cut(Hf, 2048, GH, TOK)
        nP = [cut(Sf, 512 * j, TOK) for j in range(4)]
        nF = [cut(Rf, 4096 + 512 * j, TOK) for j in range(4)]
        relu = cut(Rf, 2048, 4, 512)
        lg = cut(Rf, 0, 2, 2048)
        pT = cut(Rf, 4096, 2, 16, 128)
        nearm = cut(Rf, 8192, 2, 256)
        osb = cut(Rf, 8704, 2, 512)
        iqz = cut(Rf, 2048, DB, 64)
        rep = cut(Rf, 2560, DB, 64)
        cache = cut(Rf, 4096, 2, NPG, 512)
        srelu = cut(Rf, 8192, 2, LS)
        wrow = cut(Rf, 9344, DB, 64)
        wsel = cut(Rf, 9856, DB, 64)
        qz = cut(Rf, 2048, DB, 64)
        slg = cut(Rf, 8192, 2, LS)
        spT = cut(Rf, 9344, 2, 5, 64)
        sscore = Sf[0:64, 0:LS + 6]
        outev = cut(Rf, 6144, 4, 512)
        U = cut(Rf, 0, NF, TOK)
        ffev = mixA

        sems = {}

        def S(name):
            if name not in sems:
                sems[name] = ctx.enter_context(nc.semaphore(name))
            return sems[name]

        SCHED = [("B", 0), ("P", 0), ("G", 0), ("I", 0), ("T", 0), ("A", 0)]
        for b in range(1, NBLK + 1):
            SCHED += [("P", b), ("G", b), ("I", b), ("F", b - 1), ("A", b)]
        SCHED += [("F", NBLK)]

        def ntok(b):
            return TOK if b < NBLK else NS

        ENG = ("pe", "act", "dve", "pool")

        def phase_start(eng, n):
            if n:
                for who in ENG:
                    eng.wait_ge(S("end_" + who), n)

        ring_base, at = {}, 0
        for kind, b in SCHED:
            if kind == "P":
                ring_base["P", b] = at
                at += NP_SLOT
            if kind == "F":
                ring_base["O", b] = at
                ring_base["U", b] = at + 4
                ring_base["D", b] = at + 4 + NF
                at += 4 + NF + 16

        IU = [(i, c, h) for i in range(2, 16) for c in range(len(score_chunks(i))) for h in range(HEADS)]
        IN = {u: n for n, u in enumerate(IU)}
        AU = [(i, h) for i in range(16) for h in range(HEADS)]
        QU = [(i, h, c) for i, h in AU for c in range(len(near_chunks(i)))]
        QN = {u: n for n, u in enumerate(QU)}
        TU = [(i, h, g) for i, h in AU for g in range(-(-(i + 1) // 4))]
        TN = {u: n for n, u in enumerate(TU)}

        def x_loads(nph):
            return 1 + sum(k in "PF" for k, _ in SCHED[:nph])

        def tiles_of(b):
            return range(4 * b, 4 * b + 4)

        block = ctx.enter_context(nc.Block())

        @block.sync
        def _(sp):
            sp.dma_start(cst[:, :], a["consts"]).then_inc(S("consts_in"), 16)
            sp.dma_start(hots[0:RB], a["hots"]).then_inc(S("consts_in"), 16)
            sp.dma_start(relb[0:RB], a["rel_bias"]).then_inc(S("consts_in"), 16)
            sp.dma_start(gvec[:, :], a["gains"]).then_inc(S("consts_in"), 16)
            sp.dma_start(gates[:, :], a["gates"]).then_inc(S("consts_in"), 16)
            sp.dma_start(gate_up[:, :], a["gate_up"]).then_inc(S("consts_in"), 16)
            sp.dma_start(pages[:, :], a["pages"]).then_inc(S("pages_in"), 16)
            stores = 0

            def weights(n, dst, src):
                sp.dma_start(dst, src).then_inc(S(f"weights_in{n % 2}"), 16)

            def load_cache(n, s):
                for p in range(NPG):
                    at = sp.value_load(pages[0:1, s * NPG + p:s * NPG + p + 1], min_val=0, max_val=NPOOL - 1)
                    sp.dma_start(cache[:, n % 2, p, :],
                                 a["cache"][bass.ds(at, 1)].rearrange("o p n -> p (o n)")
                                 ).then_inc(S(f"cache_in{n % 2}"), 16)

            for nph, (kind, b) in enumerate(SCHED):
                NT = ntok(b)
                t0 = TOK * b
                if kind == "B":
                    sp.wait_ge(S("pages_in"), 16)
                    sp.wait_ge(S("bias_rows"), 1)
                    sp.dma_start(skew1.rearrange("h p w -> p h w"), row1).then_inc(S("skew_dma"), 16)
                    sp.dma_start(skew2.rearrange("h p w -> p h w"), row2[0:TS]).then_inc(S("skew_dma"), 16)
                    sp.wait_ge(S("skew_dma"), 32)
                    sp.dma_start(near_bias[:, :, :],
                                 bass.AP(skew1.tensor, 127, [[W1 - 1, 128], [128 * W1, HEADS], [1, 256]])
                                 ).then_inc(S("skew_dma"), 16)
                    for h in range(HEADS):
                        sp.dma_start(sbias[h * TS:(h + 1) * TS, :],
                                     bass.AP(skew2.tensor, h * TS * W2 + TS - 1, [[W2 - 1, TS], [1, PAST + TS]])
                                     ).then_inc(S("skew_dma"), 16)
                if kind == "P":
                    phase_start(sp, nph)
                    sp.dma_start(X[:, :, 0:NT], a["xT"][:, :, t0:t0 + NT]).then_inc(S("x_in"), 16)
                    for s, ts in enumerate(SLOT_TILES):
                        n = ring_base["P", b] + s
                        if s >= 2:
                            sp.wait_ge(S("p_mm"), len(P_UNITS) * b + SLOT_TILES[s - 2][-1] + 1)
                        weights(n, ring[:, n % 2, 0:len(ts) * 1024].rearrange("p (t m) -> p t m", m=1024),
                                a["w_in"][ts[0]:ts[0] + len(ts)].rearrange("t p m -> p t m"))
                if kind == "G" and b == NBLK:
                    phase_start(sp, nph)
                    for e in range(2):
                        for j in range(2):
                            sp.dma_start(sin[64 * e:64 * e + 64, :, j, :],
                                         a["state"][:, 2 * j + e].rearrange("b k v -> k b v")
                                         ).then_inc(S("state_in"), 16)
                if kind == "I":
                    phase_start(sp, nph)
                    pairs = [(a["o_k"][:, :, t0:t0 + NT], kT[0:64, :, t0:t0 + NT]),
                             (a["o_ik"][:, t0:t0 + NT], ikT[0:64, t0:t0 + NT])]
                    if b < NBLK:
                        pairs.append((a["o_v"][t0:t0 + NT].rearrange("(t p) n -> p t n", p=128),
                                      vtok[:, 4 * b:4 * b + 4, :]))
                    else:
                        pairs += [(a["o_v"][t0:t0 + NT], vnew[:, :]), (a["o_gs"], sin)]
                    if b == NBLK - 1:
                        pairs.append((a["o_gp"], state[:, :, :]))
                    for dst, src in pairs:
                        sp.dma_start(dst, src).then_inc(S("outputs"), 16)
                        stores += 16
                    sp.wait_ge(S("outputs"), stores)
                    sp.sem_inc(S("stored"), 1)
                    if b == NBLK:
                        sp.dma_start(rep[0:64], a["rep"].rearrange("p (a b) -> p a b", b=64)
                                     ).then_inc(S("rep_in"), 16)
                        for s in range(DB):
                            if s >= 2:
                                sp.wait_ge(S("si_dots"), s - 1)
                            load_cache(s, s)
                if kind == "A" and b == NBLK:
                    phase_start(sp, nph)
                    sp.dma_start(rep[0:64], a["rep"].rearrange("p (a b) -> p a b", b=64)
                                 ).then_inc(S("rep_in"), 16)
                    for s in range(DB):
                        if s >= 2:
                            sp.wait_ge(S("sa_pv"), s - 1)
                        load_cache(s, s)
                if kind == "F":
                    phase_start(sp, nph)
                    sp.dma_start(X[:, :, 0:NT], a["xT"][:, :, t0:t0 + NT]).then_inc(S("x_in"), 16)
                    for s in range(4):
                        n = ring_base["O", b] + s
                        if s >= 2:
                            sp.wait_ge(S("o_mm"), KT * b + 2 * s - 2)
                        weights(n, ring[:, n % 2, :].rearrange("p (t m) -> p t m", m=1024),
                                a["w_out"][2 * s:2 * s + 2].rearrange("t p m -> p t m"))
                    def row(src, n, s, cols):
                        sp.dma_start(ring[:, s, 0:cols], src[bass.ds(n, 1)].rearrange("t p m -> p (t m)")
                                     ).then_inc(S(f"weights_in{s}"), 16)

                    u0 = 2 * NF * b
                    for s in range(2):
                        sp.wait_ge(S("o_mm"), KT * b + 2 * s + 6)
                        row(a["w_gu"], s, s, 2048)
                    with sp.Fori(1, NF // 2) as i:
                        for s in range(2):
                            sp.wait_ge(S("u_mm"), i * 4 + (u0 + 2 * s - 2))
                            row(a["w_gu"], i * 2 + s, s, 2048)
                    for s in range(2):
                        sp.wait_ge(S("u_mm"), u0 + 2 * NF + 2 * s - 2)
                        row(a["w_d"], s, s, 1408)
                    with sp.Fori(1, KT) as i:
                        for s in range(2):
                            sp.wait_ge(S("d_half"), i * 2 + (2 * KT * b + s - 1))
                            row(a["w_d"], i * 2 + s, s, 1408)
                    sp.wait_ge(S("f_y"), b + 1)
                    sp.dma_start(a["o_y"][:, :, t0:t0 + NT], H[:, :, 0:NT]).then_inc(S("outputs"), 16)
                    stores += 16
                    sp.wait_ge(S("outputs"), stores)
                    sp.sem_inc(S("stored"), 1)

        def stored_before(eng, nph):
            n = sum(1 for k, _ in SCHED[:nph] if k in "IF")
            if n:
                eng.wait_ge(S("stored"), n)

        @block.tensor
        def _(pe):
            mm = nc.tensor.matmul

            def weights_at(n):
                pe.wait_ge(S(f"weights_in{n % 2}"), 16 * (n // 2 + 1))
                return n % 2

            for nph, (kind, b) in enumerate(SCHED):
                NT = ntok(b)
                t0 = TOK * b
                ntile = NT // 128 if b < NBLK else 1
                tw = min(NT, 128)
                phase_start(pe, nph)
                if kind == "B":
                    pe.wait_ge(S("bias_wide"), 1)
                    for h in range(HEADS):
                        if h >= 2:
                            pe.wait_ge(S("bias_copied"), h - 1)
                        k = 3 * (h % 2)
                        mm(bank[k][:, 0:W1], relw[0:RB, h, :], hots[0:RB, 0:W1], start=True, stop=True)
                        mm(bank[k + 1][:, 0:512], relw[0:RB, h, :], hots[0:RB, W1:W1 + 512], start=True, stop=True)
                        mm(bank[k + 2][:, 0:W2 - 512], relw[0:RB, h, :], hots[0:RB, W1 + 512:W1 + W2],
                           start=True, stop=True).then_inc(S("bias_mm"), 1)
                if kind == "P":
                    pe.wait_ge(S("p_sq"), b + 1)
                    for k in range(KT):
                        last = mm(bank[7][:, 0:NT], ones, sq[:, k, 0:NT], start=(k == 0), stop=(k == KT - 1))
                    last.then_inc(S("p_ss"), 1)
                    pe.wait_ge(S("p_h"), b + 1)
                    for u, (what, j) in enumerate(P_UNITS):
                        n = len(P_UNITS) * b + u
                        t = min(u, len(TILES) - 1)
                        slot = weights_at(ring_base["P", b] + SLOT_OF[t])
                        w = ring[:, slot, 1024 * SLOT_TILES[SLOT_OF[t]].index(t):][:, 0:1024].rearrange(
                            "p (k c) -> p k c", c=128)
                        if u >= 4:
                            pe.wait_ge(S("p_copied"), n - 3)
                        o = bank[u % 4]
                        if what in ("v", "gv", "iw"):
                            lo, hi = (RANK, RANK + 8) if what == "iw" else (0, 128)
                            for t in range(ntile):
                                for k in range(KT):
                                    last = mm(o[0:tw, t * (hi - lo):(t + 1) * (hi - lo)],
                                              H[:, k, t * 128:t * 128 + tw], w[:, k, lo:hi],
                                              start=(k == 0), stop=(k == KT - 1))
                        else:
                            hi = RANK if what == "glr" else 128
                            for k in range(KT):
                                last = mm(o[0:hi, 0:NT], w[:, k, 0:hi], H[:, k, 0:NT],
                                          start=(k == 0), stop=(k == KT - 1))
                        last.then_inc(S("p_mm"), 1)
                if kind == "G":
                    mm(bank[0][:, 0:NT], ones, ikx[:, 0:NT], start=True, stop=True).then_inc(S("g_mean"), 1)
                    for j in range(2):
                        last = mm(bank[2 + j][:, 0:NT], gate_up[:, j * 128:(j + 1) * 128], glr[0:RANK, 0:NT],
                                  start=True, stop=True)
                    last.then_inc(S("g_gate"), 1)
                    pe.wait_ge(S("g_ikc"), b + 1)
                    mm(bank[1][:, 0:NT], ones, ikx[:, 0:NT], start=True, stop=True).then_inc(S("g_var"), 1)
                    pe.wait_ge(S("g_k"), b + 1)
                    pe.wait_ge(S("g_q"), b + 1)
                    if b < NBLK:
                        for t in range(4):
                            T = 4 * b + t
                            c0 = 128 * t
                            if t >= 2:
                                pe.wait_ge(S("g_khz"), T - 1)
                            for j in range(2):
                                last = nc.tensor.transpose(bank[t % 2][:, j * 128:(j + 1) * 128],
                                                           kh[:, j, c0:c0 + 128], ident)
                            last.then_inc(S("g_kt"), 1)
                            if t >= 2:
                                pe.wait_ge(S("g_atm"), T - 1)
                            for c in range(2):
                                for h in range(GH):
                                    cc = c0 + CH * c
                                    last = mm(bank[2 + t % 2][64 * c:64 * c + 64, h * 64:(h + 1) * 64],
                                              kg[:, h // 2, cc:cc + CH], qgz[:, h, cc:cc + CH],
                                              start=True, stop=True)
                            last.then_inc(S("g_at"), 1)
                            pe.wait_ge(S("g_atm"), T + 1)
                            pe.wait_ge(S("g_khz"), T + 1)
                            if t >= 2:
                                pe.wait_ge(S("g_oc"), T - 1)
                            for h in range(GH):
                                mm(bank[6 + t % 2][:, h * 128:(h + 1) * 128], gv[:, t, h * 128:(h + 1) * 128],
                                   att[:, t % 2, h, :], start=(h == 0), stop=False, skip_group_check=True)
                            for c in range(2):
                                cc = c0 + CH * c
                                n = 2 * T + c
                                if n:
                                    pe.wait_ge(S("g_state"), n)
                                for h in range(GH):
                                    mm(bank[6 + t % 2][:, h * 128 + CH * c:h * 128 + CH * c + CH],
                                       state[:, h // 2, :], qiz[:, h, cc:cc + CH],
                                       start=False, stop=(c == 1), skip_group_check=True)
                                for j in range(2):
                                    last = mm(bank[4 + c][:, j * 256:(j + 1) * 256],
                                              khz[:, t, c, j * 128:(j + 1) * 128],
                                              gv[:, t, j * 256:(j + 1) * 256], start=True, stop=True)
                                last.then_inc(S("g_o"), 1)
                    else:
                        for j in range(2):
                            last = nc.tensor.transpose(bank[0][0:NS, j * 128:(j + 1) * 128], kh[:, j, 0:NS], ident)
                        last.then_inc(S("g_kt"), 1)
                        for h in range(GH):
                            last = mm(bank[2][0:NS, h * 64:(h + 1) * 64], kg[:, h // 2, 0:NS], qgz[:, h, 0:NS],
                                      start=True, stop=True)
                        last.then_inc(S("g_at"), 1)
                        pe.wait_ge(S("g_atm"), 4 * NBLK + 1)
                        pe.wait_ge(S("state_in"), 64)
                        for h in range(GH):
                            mm(bank[6][:, h * 64:(h + 1) * 64], gv[0:NS, 0, h * 128:(h + 1) * 128],
                               atts[0:NS, h, :], start=(h == 0), stop=False, skip_group_check=True)
                        for s in range(DB):
                            for h in range(GH):
                                last = mm(bank[6][:, h * 64 + TS * s:h * 64 + TS * s + TS], sin[:, s, h // 2, :],
                                          qiz[:, h, TS * s:TS * s + TS], start=False, stop=True,
                                          skip_group_check=True)
                        last.then_inc(S("g_o"), 1)
                        pe.wait_ge(S("g_khz"), 4 * NBLK + 1)
                        for s in range(DB):
                            pe.wait_ge(S("gs_gvz"), s + 1)
                            if s >= 2:
                                pe.wait_ge(S("gs_new"), s - 1)
                            for j in range(2):
                                last = mm(bank[4 + s % 2][:, j * 256:(j + 1) * 256], khs[0:NS, j * 128:(j + 1) * 128],
                                          gvz[0:NS, s % 2, j * 256:(j + 1) * 256], start=True, stop=True)
                            last.then_inc(S("gs_u"), 1)
                    pe.wait_ge(S("g_o2"), b + 1)
                    for h in range(GH):
                        last = mm(bank[h][:, 0:NT], ones, o2[:, h, 0:NT], start=True, stop=True)
                    last.then_inc(S("g_oss"), 1)
                if kind == "I" and b < NBLK:
                    for i in tiles_of(b):
                        if i < 2:
                            continue
                        cq = 128 * (i % 4)
                        for c, (k0, kn) in enumerate(score_chunks(i)):
                            for h in range(HEADS):
                                n = IN[i, c, h]
                                if n >= 8:
                                    pe.wait_ge(S("i_relu"), n - 7)
                                e = 64 * (h % 2)
                                mm(bank[n % 8][:, 0:kn], iq[e:e + 64, h // 2, cq:cq + 128],
                                   ikT[e:e + 64, k0:k0 + kn], start=True, stop=True).then_inc(S("i_dots"), 1)
                if kind == "I" and b == NBLK:
                    pe.wait_ge(S("si_wrow"), 1)
                    for s in range(DB):
                        last = mm(bank[0][0:64, s * 64:(s + 1) * 64], wrow[0:64, s, :], ident[0:64, 0:64],
                                  start=True, stop=True)
                    last.then_inc(S("si_wt"), 1)
                    pe.wait_ge(S("si_iqz"), 1)
                    for s in range(DB):
                        pe.wait_ge(S(f"cache_in{s % 2}"), 16 * NPG * (s // 2 + 1))
                        if s >= 2:
                            pe.wait_ge(S("si_relu"), s - 1)
                        mm(bank[2 + 2 * (s % 2)][0:64, :], iqz[:, s, :], cache[:, s % 2, :, 256:384],
                           start=True, stop=True)
                        mm(bank[3 + 2 * (s % 2)][0:64, 0:NS], iqz[:, s, :], ikT[:, SEQ:ALLT],
                           start=True, stop=True).then_inc(S("si_dots"), 1)
                        pe.wait_ge(S("si_wsel"), 1)
                        pe.wait_ge(S("si_relu"), s + 1)
                        mm(bank[6][0:64, :], wsel[0:64, s, :], srelu[0:64, s % 2, 0:PAST],
                           start=(s == 0), stop=(s == DB - 1))
                        mm(bank[7][0:64, 0:NS], wsel[0:64, s, :], srelu[0:64, s % 2, PAST:LS],
                           start=(s == 0), stop=(s == DB - 1)).then_inc(S("si_sum"), 1)
                if kind == "A" and b < NBLK:
                    def logits(i, h):
                        e = 64 * (h % 2)
                        cq = 128 * (i % 4)
                        for c, (k0, kn, near) in enumerate(near_chunks(i)):
                            n = QN[i, h, c]
                            if n >= 3:
                                pe.wait_ge(S("a_masked"), n - 2)
                            mm(bank[n % 3][:, 0:kn], q[e:e + 64, h // 2, cq:cq + 128],
                               kT[e:e + 64, h // 4, k0:k0 + kn], start=True, stop=True).then_inc(S("a_logits"), 1)

                    def turn(i, h):
                        u = 8 * i + h
                        pe.wait_ge(S("a_exp"), u + 1)
                        for g in range(-(-(i + 1) // 4)):
                            n = TN[i, h, g]
                            if n >= 2:
                                pe.wait_ge(S("a_pTc"), n - 1)
                            for t in range(4 * g, min(4 * g + 4, i + 1)):
                                last = nc.tensor.transpose(bank[3 + n % 2][:, 128 * (t % 4):128 * (t % 4) + 128],
                                                           lg[:, u % 2, 128 * t:128 * t + 128], ident)
                            last.then_inc(S("a_pT"), 1)

                    def values(i, h):
                        u = 8 * i + h
                        pe.wait_ge(S("a_pTc"), TN[i, h, -(-(i + 1) // 4) - 1] + 1)
                        if u >= 2:
                            pe.wait_ge(S("a_scaled"), u - 1)
                        for t in range(i + 1):
                            last = mm(bank[5 + u % 2][:, 0:64], pT[:, u % 2, t, :],
                                      vtok[:, t, (h // 4) * 64:(h // 4) * 64 + 64],
                                      start=(t == 0), stop=(t == i))
                        last.then_inc(S("a_pv"), 1)

                    def turn_out(i):
                        pe.wait_ge(S("a_scaled"), 8 * i + 8)
                        if i:
                            pe.wait_ge(S("a_mix"), i)
                        for j in range(4):
                            last = nc.tensor.transpose(bank[7][:, 128 * j:128 * j + 128],
                                                       osb[:, i % 2, 128 * j:128 * j + 128], ident)
                        last.then_inc(S("a_oT"), 1)

                    units = [(i, h) for i in tiles_of(b) for h in range(HEADS)]
                    logits(*units[0])
                    for n, (i, h) in enumerate(units):
                        if n + 1 < len(units):
                            logits(*units[n + 1])
                        turn(i, h)
                        if n:
                            values(*units[n - 1])
                            if units[n - 1][1] == HEADS - 1:
                                turn_out(units[n - 1][0])
                    values(*units[-1])
                    turn_out(units[-1][0])
                if kind == "A" and b == NBLK:
                    pe.wait_ge(S("sa_qz"), 1)
                    pe.wait_ge(S("rep_in"), 32)
                    for s in range(DB):
                        pe.wait_ge(S(f"cache_in{s % 2}"), 16 * NPG * ((DB + s) // 2 + 1))
                        if s:
                            pe.wait_ge(S("sa_added"), s)
                        mm(bank[0][0:64, :], rep[0:64, s, :], sscore[:, 0:PAST], start=True, stop=False,
                           skip_group_check=True)
                        mm(bank[1][0:64, 0:NS], rep[0:64, s, :], sscore[:, PAST:LS], start=True, stop=False,
                           skip_group_check=True)
                        for g in range(KVH):
                            mm(bank[0][32 * g:32 * g + 32, :], qz[:, s, 32 * g:32 * g + 32],
                               cache[:, s % 2, :, 128 * g:128 * g + 128], start=False, stop=True,
                               skip_group_check=True)
                            last = mm(bank[1][32 * g:32 * g + 32, 0:NS], qz[:, s, 32 * g:32 * g + 32],
                                      kT[:, g, SEQ:ALLT], start=False, stop=True, skip_group_check=True)
                        last.then_inc(S("sa_logits"), 1)
                        pe.wait_ge(S("sa_probs"), s + 1)
                        if s >= 2:
                            pe.wait_ge(S("sa_pTc"), s - 1)
                        for p in range(NPG):
                            nc.tensor.transpose(bank[2 + s % 2][:, 64 * p:64 * p + 64],
                                                slg[0:64, s % 2, 128 * p:128 * p + 128], ident[0:64, 0:64])
                        nc.tensor.transpose(bank[4 + s % 2][0:64, 0:64], slg[0:64, s % 2, PAST:LS],
                                            ident[0:64, 0:64]).then_inc(S("sa_pT"), 1)
                        pe.wait_ge(S("sa_pTc"), s + 1)
                        for g in range(KVH):
                            o = bank[6][0:64, s * 64 + 32 * g:s * 64 + 32 * g + 32]
                            for p in range(NPG):
                                mm(o, cache[:, s % 2, p, 384 + 64 * g:384 + 64 * g + 64],
                                   spT[:, s % 2, p, 32 * g:32 * g + 32], start=(p == 0), stop=False)
                            last = mm(o, vnew[:, 64 * g:64 * g + 64], spT[0:64, s % 2, 4, 32 * g:32 * g + 32],
                                      start=False, stop=True)
                        last.then_inc(S("sa_pv"), 1)
                if kind == "F":
                    par = b % 2
                    for dt in range(KT):
                        n = ring_base["O", b] + dt // 2
                        slot = weights_at(n)
                        if dt >= 2:
                            pe.wait_ge(S("o_copied"), KT * b + dt - 1)
                        for k in range(KT):
                            w = ring[:, slot, 1024 * (dt % 2) + 128 * k:1024 * (dt % 2) + 128 * k + 128]
                            src = mixA[:, k, 0:NT] if k < 4 else mixG[:, par, k - 4, 0:NT]
                            last = mm(bank[dt % 2][:, 0:NT], w, src, start=(k == 0), stop=(k == KT - 1))
                        last.then_inc(S("o_mm"), 1)
                    pe.wait_ge(S("f_sq"), b + 1)
                    for k in range(KT):
                        last = mm(bank[2][:, 0:NT], ones, sq[:, k, 0:NT], start=(k == 0), stop=(k == KT - 1))
                    last.then_inc(S("f_ss"), 1)
                    pe.wait_ge(S("f_h"), b + 1)
                    n0 = ring_base["U", b]
                    u0 = 2 * NF * b
                    with pe.Fori(0, NF // 2) as i:
                        for s in range(2):
                            pe.wait_ge(S(f"weights_in{s}"), i * 16 + 16 * (n0 // 2 + 1))
                            for m in range(2):
                                r = 2 * s + m
                                pe.wait_ge(S("u_bank_free"), i * 4 + (u0 + r + 1))
                                for k in range(KT):
                                    last = mm(bank[4 + r][:, 0:NT],
                                              ring[:, s, 1024 * m + 128 * k:1024 * m + 128 * k + 128],
                                              H[:, k, 0:NT], start=(k == 0), stop=(k == KT - 1))
                                last.then_inc(S("u_mm"), 1)
                    pe.wait_ge(S("u_pair_free"), 2 + NF * (b + 1))
                    n0 = ring_base["D", b]
                    with pe.Fori(0, KT // 2) as i:
                        for dt in range(2):
                            pe.wait_ge(S("d_bank_free"), i * 2 + (KT * b + dt + 1))
                            for s in range(2):
                                pe.wait_ge(S(f"weights_in{s}"), i * 32 + 16 * (n0 // 2 + dt + 1))
                                for k in range(NF // 2):
                                    last = mm(bank[dt][:, 0:NT], ring[:, s, 128 * k:128 * k + 128],
                                              U[:, 11 * s + k, 0:NT], start=(s == 0 and k == 0),
                                              stop=(s == 1 and k == NF // 2 - 1))
                                last.then_inc(S("d_half"), 1)
                    pe.wait_ge(S("y_sq"), b + 1)
                    for k in range(KT):
                        last = mm(bank[3][:, 0:NT], ones, sq[:, k, 0:NT], start=(k == 0), stop=(k == KT - 1))
                    last.then_inc(S("y_ss"), 1)
                pe.drain().then_inc(S("end_pe"), 1)

        @block.scalar
        def _(act):
            A = nc.scalar.activation

            def inverse_root(src, scale, e, ms, tmp, name):
                A(ms, src, ACT.Identity, scale=scale, bias=e)
                act.drain()
                A(tmp, ms, ACT.Ln)
                act.drain()
                A(tmp, tmp, ACT.Exp, scale=-0.5).then_inc(S(name), 1)

            for nph, (kind, b) in enumerate(SCHED):
                NT = ntok(b)
                t0 = TOK * b
                ntile = NT // 128 if b < NBLK else 1
                tw = min(NT, 128)
                phase_start(act, nph)
                stored_before(act, nph)
                if kind == "B":
                    act.wait_ge(S("consts_in"), 96)
                    act.sem_inc(S("u_bank_free"), 4)
                    act.sem_inc(S("d_bank_free"), 2)
                    act.sem_inc(S("u_pair_free"), 2)
                    act.sem_inc(S("d_buf_free"), 2)
                if kind == "P":
                    act.wait_ge(S("x_in"), 16 * x_loads(nph))
                    A(sq[:, :, 0:NT], X[:, :, 0:NT], ACT.Square).then_inc(S("p_sq"), 1)
                    act.wait_ge(S("p_ss"), b + 1)
                    inverse_root(bank[7][:, 0:NT], 1.0 / D, eps, nP[0][:, 0:NT], nP[1][:, 0:NT], "p_root")
                    for u, (what, j) in enumerate(P_UNITS):
                        n = len(P_UNITS) * b + u
                        act.wait_ge(S("p_mm"), n + 1)
                        o = bank[u % 4]
                        of = o[:, 0:NT]
                        scale = 1.0
                        if what == "iq":
                            dst, src = iq[:, j, 0:NT], of
                        elif what == "ik":
                            dst, src = ikx[:, 0:NT], of
                        elif what == "k":
                            dst, src = kT[:, j, t0:t0 + NT], of
                        elif what == "q":
                            dst, src, scale = q[:, j, 0:NT], of, HD ** -0.5
                        elif what == "gq":
                            dst, src, scale = gq[:, j, 0:NT], of, DK ** -0.5
                        elif what == "gk":
                            dst, src = gk[:, j, 0:NT], of
                        elif what == "gr":
                            dst, src = gr[:, j, 0:NT], of
                        elif what == "glr":
                            dst, src = glr[0:RANK, 0:NT], o[0:RANK, 0:NT]
                        elif what == "v" and b < NBLK:
                            dst, src = vtok[:, 4 * b:4 * b + 4, :], o[:, :].rearrange("p (t c) -> p t c", c=128)
                        elif what == "v":
                            dst, src = vnew[:, :], o[0:NS, 0:128]
                        elif what == "gv":
                            dst = gv[0:tw, 0:ntile, 128 * j:128 * j + 128]
                            src = o[0:tw, 0:128 * ntile].rearrange("p (t c) -> p t c", c=128)
                        else:
                            dst = iw[0:tw, 0:ntile, :]
                            src = o[0:tw, 0:8 * ntile].rearrange("p (t c) -> p t c", c=8)
                            scale = 8 ** -0.5 * 64 ** -0.5
                        A(dst, src, ACT.Copy, scale=scale).then_inc(S("p_copied"), 1)
                if kind == "G":
                    act.wait_ge(S("g_gate"), b + 1)
                    for j in range(2):
                        A(la[:, j, 0:NT], bank[2 + j][:, 0:NT], ACT.Identity, bias=gates[:, j:j + 1])
                    act.drain()
                    A(exa[:, :, 0:NT], la[:, :, 0:NT], ACT.Abs)
                    act.drain()
                    A(exb[:, :, 0:NT], exa[:, :, 0:NT], ACT.Exp, scale=-1.0)
                    act.drain()
                    A(exa[:, :, 0:NT], exb[:, :, 0:NT], ACT.Ln, bias=1.0).then_inc(S("g_lsig"), 1)
                    act.wait_ge(S("g_var"), b + 1)
                    inverse_root(bank[1][:, 0:NT], 1.0 / 128, lneps, nG[0][:, 0:NT], nG[1][:, 0:NT], "g_ikr")
                    act.wait_ge(S("g_cum"), b + 1)
                    A(la[:, :, 0:NT], cum[:, :, 0:NT], ACT.Exp, scale=1.0 / 16)
                    A(exe[:, :, 0:NT], exa[:, :, 0:NT], ACT.Exp, scale=1.0 / 16)
                    A(kg[:, :, 0:NT], exa[:, :, 0:NT], ACT.Exp, scale=-1.0 / 16)
                    A(kh[:, :, 0:NT], exb[:, :, 0:NT], ACT.Exp, scale=1.0 / 16).then_inc(S("g_ex"), 1)
                    act.wait_ge(S("g_zero"), b + 1)
                    if b < NBLK:
                        for t in range(4):
                            T = 4 * b + t
                            act.wait_ge(S("g_kt"), T + 1)
                            for c in range(2):
                                last = A(khz[64 * c:64 * c + 64, t, c, :], bank[t % 2][64 * c:64 * c + 64, 0:256], ACT.Copy)
                            last.then_inc(S("g_khz"), 1)
                            act.wait_ge(S("g_o"), 2 * T + 2)
                            A(oT[:, :, 128 * t:128 * t + 128],
                              bank[6 + t % 2][:, :].rearrange("p (h n) -> p h n", n=128), ACT.Copy).then_inc(S("g_oc"), 1)
                    else:
                        act.wait_ge(S("g_kt"), 4 * NBLK + 1)
                        A(khs[0:NS], bank[0][0:NS, 0:256], ACT.Copy).then_inc(S("g_khz"), 1)
                        act.wait_ge(S("g_o"), 8 * NBLK + 1)
                        A(oT[:, :, 0:NS], bank[6][:, 0:256].rearrange("p (h n) -> p h n", n=NS), ACT.Copy
                          ).then_inc(S("g_oc"), 1)
                    act.drain()
                    A(o2[:, :, 0:NT], oT[:, :, 0:NT], ACT.Square).then_inc(S("g_o2"), 1)
                    act.wait_ge(S("g_oss"), b + 1)
                    for h in range(GH):
                        A(o2[:, h, 0:NT], bank[h][:, 0:NT], ACT.Identity, scale=1.0 / DV, bias=eps)
                    act.drain()
                    A(qgz[:, :, 0:NT], o2[:, :, 0:NT], ACT.Ln)
                    act.drain()
                    A(qgz[:, :, 0:NT], qgz[:, :, 0:NT], ACT.Exp, scale=-0.5).then_inc(S("g_root"), 1)
                    A(gr[:, :, 0:NT], gr[:, :, 0:NT], ACT.Silu).then_inc(S("g_silu"), 1)
                if kind == "I" and b < NBLK:
                    for i in tiles_of(b):
                        if i < 2:
                            continue
                        for c, (k0, kn) in enumerate(score_chunks(i)):
                            for h in range(HEADS):
                                n = IN[i, c, h]
                                act.wait_ge(S("i_dots"), n + 1)
                                if n >= 4:
                                    act.wait_ge(S("i_added"), n - 3)
                                A(relu[:, n % 4, 0:kn], bank[n % 8][:, 0:kn], ACT.Relu).then_inc(S("i_relu"), 1)
                if kind == "I" and b == NBLK:
                    act.wait_ge(S("si_wt"), 1)
                    A(wsel[0:64], bank[0][0:64, :].rearrange("p (s t) -> p s t", t=64), ACT.Copy).then_inc(S("si_wsel"), 1)
                    for s in range(DB):
                        act.wait_ge(S("si_dots"), s + 1)
                        if s >= 2:
                            act.wait_ge(S("si_sum"), s - 1)
                        A(srelu[0:64, s % 2, 0:PAST], bank[2 + 2 * (s % 2)][0:64, :], ACT.Relu)
                        A(srelu[0:64, s % 2, PAST:LS], bank[3 + 2 * (s % 2)][0:64, 0:NS], ACT.Relu).then_inc(S("si_relu"), 1)
                    act.wait_ge(S("si_sum"), DB)
                    A(sscore[:, 0:PAST], bank[6][0:64, :], ACT.Copy).then_inc(S("si_copied"), 1)
                if kind == "A" and b < NBLK:
                    def probs(i, h):
                        u = 8 * i + h
                        act.wait_ge(S("a_max"), u + 1)
                        if u >= 2:
                            act.wait_ge(S("a_scaled"), u - 1)
                        A(lg[:, u % 2, 0:128 * (i + 1)], lg[:, u % 2, 0:128 * (i + 1)], ACT.Exp,
                          bias=nmax[:, u % 2:u % 2 + 1], accum_out=den[:, u % 2:u % 2 + 1]).then_inc(S("a_exp"), 1)

                    def copy_pT(i, h):
                        u = 8 * i + h
                        if u >= 2:
                            act.wait_ge(S("a_pv"), u - 1)
                        for g in range(-(-(i + 1) // 4)):
                            n = TN[i, h, g]
                            act.wait_ge(S("a_pT"), n + 1)
                            w = min(4, i + 1 - 4 * g)
                            A(pT[:, u % 2, 4 * g:4 * g + w, :],
                              bank[3 + n % 2][:, 0:128 * w].rearrange("p (t n) -> p t n", n=128),
                              ACT.Copy).then_inc(S("a_pTc"), 1)

                    units = [(i, h) for i in tiles_of(b) for h in range(HEADS)]
                    probs(*units[0])
                    for n, (i, h) in enumerate(units):
                        copy_pT(i, h)
                        if n and units[n - 1][1] == HEADS - 1:
                            ii = units[n - 1][0]
                            act.wait_ge(S("a_oT"), ii + 1)
                            A(mixA[:, :, 128 * (ii % 4):128 * (ii % 4) + 128],
                              bank[7][:, :].rearrange("p (j n) -> p j n", n=128), ACT.Copy).then_inc(S("a_mix"), 1)
                        if n + 1 < len(units):
                            probs(*units[n + 1])
                    ii = units[-1][0]
                    act.wait_ge(S("a_oT"), ii + 1)
                    A(mixA[:, :, 128 * (ii % 4):128 * (ii % 4) + 128],
                      bank[7][:, :].rearrange("p (j n) -> p j n", n=128), ACT.Copy).then_inc(S("a_mix"), 1)
                if kind == "A" and b == NBLK:
                    for s in range(DB):
                        act.wait_ge(S("sa_max"), s + 1)
                        if s >= 2:
                            act.wait_ge(S("sa_probs"), s - 1)
                        A(slg[0:64, s % 2, :], slg[0:64, s % 2, :], ACT.Exp, bias=nmax[0:64, s % 2:s % 2 + 1],
                          accum_out=den[0:64, s % 2:s % 2 + 1]).then_inc(S("sa_exp"), 1)
                        act.wait_ge(S("sa_pT"), s + 1)
                        if s >= 2:
                            act.wait_ge(S("sa_pv"), s - 1)
                        A(spT[:, s % 2, 0:NPG, :], bank[2 + s % 2][:, 0:256].rearrange("p (t n) -> p t n", n=64), ACT.Copy)
                        A(spT[0:64, s % 2, NPG, :], bank[4 + s % 2][0:64, 0:64], ACT.Copy).then_inc(S("sa_pTc"), 1)
                if kind == "F":
                    for dt in range(KT):
                        n = KT * b + dt
                        act.wait_ge(S("o_mm"), n + 1)
                        if dt >= 4:
                            act.wait_ge(S("o_added"), n - 3)
                        A(outev[:, dt % 4, 0:NT], bank[dt % 2][:, 0:NT], ACT.Copy).then_inc(S("o_copied"), 1)
                    act.wait_ge(S("o_added"), KT * (b + 1))
                    A(sq[:, :, 0:NT], X[:, :, 0:NT], ACT.Square).then_inc(S("f_sq"), 1)
                    act.wait_ge(S("f_ss"), b + 1)
                    inverse_root(bank[2][:, 0:NT], 1.0 / D, eps, nF[0][:, 0:NT], nF[1][:, 0:NT], "f_root")
                    for k in range(KT):
                        act.wait_ge(S("f_scaled"), KT * b + k + 1)
                        last = A(H[:, k, 0:NT], H[:, k, 0:NT], ACT.Copy, scale=gvec[:, KT + k:KT + k + 1])
                    last.then_inc(S("f_h"), 1)
                    u0 = 2 * NF * b
                    with act.Fori(0, NF // 2) as i:
                        for s in range(2):
                            act.wait_ge(S("u_pair_free"), i * 2 + (NF * b + s + 1))
                            act.wait_ge(S("u_mm"), i * 4 + (u0 + 2 * s + 1))
                            A(ffev[:, 2 * s, 0:NT], bank[4 + 2 * s][:, 0:NT], ACT.Silu).then_inc(S("u_bank_free"), 1)
                            act.wait_ge(S("u_mm"), i * 4 + (u0 + 2 * s + 2))
                            A(ffev[:, 2 * s + 1, 0:NT], bank[5 + 2 * s][:, 0:NT], ACT.Copy).then_inc(S("u_bank_free"), 1)
                    with act.Fori(0, KT // 2) as i:
                        for dt in range(2):
                            act.wait_ge(S("d_buf_free"), i * 2 + (KT * b + dt + 1))
                            act.wait_ge(S("d_half"), i * 4 + (2 * KT * b + 2 * dt + 2))
                            A(ffev[:, dt, 0:NT], bank[dt][:, 0:NT], ACT.Copy).then_inc(S("d_bank_free"), 1)
                    act.wait_ge(S("d_buf_free"), 2 + KT * (b + 1))
                    A(sq[:, :, 0:NT], X[:, :, 0:NT], ACT.Square).then_inc(S("y_sq"), 1)
                    act.wait_ge(S("y_ss"), b + 1)
                    inverse_root(bank[3][:, 0:NT], 1.0 / D, eps, nF[0][:, 0:NT], nF[1][:, 0:NT], "y_root")
                    for k in range(KT):
                        act.wait_ge(S("y_scaled"), KT * b + k + 1)
                        last = A(H[:, k, 0:NT], X[:, k, 0:NT], ACT.Copy, scale=gvec[:, 2 * KT + k:2 * KT + k + 1])
                    last.then_inc(S("f_y"), 1)
                act.drain().then_inc(S("end_act"), 1)

        @block.vector
        def _(dve):
            v = nc.vector

            def newton(ms, r, tmp, out):
                v.tensor_tensor(tmp, r, r, ALU.mult)
                dve.drain()
                v.tensor_tensor(tmp, tmp, ms, ALU.mult)
                dve.drain()
                v.tensor_scalar(tmp, tmp, -0.5, 1.5, ALU.mult, ALU.add)
                dve.drain()
                v.tensor_tensor(out, tmp, r, ALU.mult)
                dve.drain()

            def pick(rows, view, k):
                with dve.Fori(0, k // 8):
                    v.max(top8[rows, :], view)
                    dve.drain()
                    v.match_replace(view, top8[rows, :], view, TAKEN)
                    dve.drain()
                v.tensor_scalar(view, view, TAKEN_CUT, OUTSIDE, ALU.is_ge, ALU.mult)

            def pick_block(b):
                if b < NBLK:
                    for i in tiles_of(b):
                        if i >= 2:
                            at = SEQ * (i % 4)
                            pick(slice(0, 128), Sf[:, at:at + 128 * (i + 1)], TOPK)
                else:
                    pick(slice(0, 64), sscore, TOPK_S + 6)

            for nph, (kind, b) in enumerate(SCHED):
                NT = ntok(b)
                t0 = TOK * b
                phase_start(dve, nph)
                stored_before(dve, nph)
                if kind == "B":
                    dve.wait_ge(S("consts_in"), 96)
                    v.memset(state[:, :, :], 0.0)
                    v.tensor_copy(relw[0:RB], relb[0:RB].unsqueeze(2).broadcast_to([RB, HEADS, 128])).then_inc(S("bias_wide"), 1)
                    for h in range(HEADS):
                        dve.wait_ge(S("bias_mm"), h + 1)
                        k = 3 * (h % 2)
                        v.tensor_copy(row1[:, h, :], bank[k][:, 0:W1])
                        v.tensor_copy(row2[:, h, 0:512], bank[k + 1][:, :])
                        v.tensor_copy(row2[:, h, 512:W2], bank[k + 2][:, 0:W2 - 512]).then_inc(S("bias_copied"), 1)
                    dve.drain().then_inc(S("bias_rows"), 1)
                    dve.wait_ge(S("skew_dma"), 16 * (3 + HEADS))
                if kind == "P":
                    dve.wait_ge(S("p_root"), b + 1)
                    newton(nP[0][:, 0:NT], nP[1][:, 0:NT], nP[2][:, 0:NT], nP[3][:, 0:NT])
                    for k in range(KT):
                        last = v.scalar_tensor_tensor(H[:, k, 0:NT], X[:, k, 0:NT], gvec[:, k:k + 1],
                                                      nP[3][:, 0:NT], ALU.mult, ALU.mult)
                    last.then_inc(S("p_h"), 1)
                if kind == "G":
                    C = CH if b < NBLK else TS
                    nc_ = NT // C
                    dve.wait_ge(S("g_mean"), b + 1)
                    v.scalar_tensor_tensor(ikc[:, 0:NT], bank[0][:, 0:NT], -1.0 / 128, ikx[:, 0:NT], ALU.mult, ALU.add)
                    dve.drain()
                    v.tensor_tensor(ikx[:, 0:NT], ikc[:, 0:NT], ikc[:, 0:NT], ALU.mult).then_inc(S("g_ikc"), 1)
                    dve.wait_ge(S("g_lsig"), b + 1)
                    v.scalar_tensor_tensor(la[:, :, 0:NT], la[:, :, 0:NT], 0.0, exa[:, :, 0:NT], ALU.min, ALU.subtract)
                    rst = cst[:, C_RST:C_RST + NT] if b < NBLK else cst[:, C_RST8:C_RST8 + NT]
                    dve.drain()
                    for j in range(2):
                        v.tensor_tensor_scan(cum[:, j, 0:NT], rst, la[:, j, 0:NT], 0.0, ALU.mult, ALU.add)
                    dve.drain()
                    for j in range(2):
                        def chunks(t):
                            return t[:, j, 0:NT].rearrange("p (n c) -> p n c", c=C)
                        mid = chunks(cum)[:, :, C // 2 - 1:C // 2].broadcast_to([128, nc_, C])
                        end = chunks(cum)[:, :, C - 1:C].broadcast_to([128, nc_, C])
                        v.tensor_tensor(chunks(exa), chunks(cum), mid, ALU.subtract)
                        v.tensor_tensor(chunks(exb), end, chunks(cum), ALU.subtract)
                    dve.wait_ge(S("g_ikr"), b + 1)
                    newton(nG[0][:, 0:NT], nG[1][:, 0:NT], nG[2][:, 0:NT], nG[3][:, 0:NT])
                    v.tensor_tensor(ikc[:, 0:NT], ikc[:, 0:NT], nG[3][:, 0:NT], ALU.mult)
                    dve.drain()
                    v.tensor_scalar(ikT[:, t0:t0 + NT], ikc[:, 0:NT], gates[:, 3:4], gates[:, 4:5], ALU.mult, ALU.add)
                    dve.drain().then_inc(S("g_cum"), 1)
                    dve.wait_ge(S("g_ex"), b + 1)
                    dve.wait_ge(S("g_zero"), b + 1)
                    for e in range(2):
                        p = slice(64 * e, 64 * e + 64)
                        v.tensor_tensor(qgz[p, e::2, 0:NT], gq[p, :, 0:NT], exe[p, :, 0:NT], ALU.mult)
                        last = v.tensor_tensor(qiz[p, e::2, 0:NT], gq[p, :, 0:NT], la[p, :, 0:NT], ALU.mult)
                    last.then_inc(S("g_q"), 1)
                    if b < NBLK:
                        for t in range(4):
                            T = 4 * b + t
                            dve.wait_ge(S("g_at"), T + 1)
                            if t >= 2:
                                dve.wait_ge(S("g_o"), 2 * T - 3)
                            for c in range(2):
                                p = slice(64 * c, 64 * c + 64)
                                last = v.tensor_tensor(
                                    att[p, t % 2, :, 64 * c:64 * c + 64],
                                    bank[2 + t % 2][p, 0:256].rearrange("p (h n) -> p h n", n=64),
                                    cst[p, C_TRI:C_TRI + 64].unsqueeze(1).broadcast_to([64, GH, 64]), ALU.mult)
                            last.then_inc(S("g_atm"), 1)
                            for c in range(2):
                                dve.wait_ge(S("g_o"), 2 * T + c + 1)
                                at = 128 * t + CH * c + CH - 1
                                for e in range(2):
                                    for j in range(2):
                                        p = slice(64 * e, 64 * e + 64)
                                        last = v.scalar_tensor_tensor(
                                            state[p, j, :], state[p, j, :], la[p, j, at:at + 1],
                                            bank[4 + c][p, j * 256 + e * 128:j * 256 + e * 128 + 128],
                                            ALU.mult, ALU.add)
                                last.then_inc(S("g_state"), 1)
                                dve.drain()
                    else:
                        dve.wait_ge(S("g_at"), 4 * NBLK + 1)
                        v.tensor_tensor(atts[0:NS], bank[2][0:NS, 0:256].rearrange("p (h n) -> p h n", n=64),
                                        cst[0:NS, C_TRI8:C_TRI8 + 64].unsqueeze(1).broadcast_to([NS, GH, 64]),
                                        ALU.mult).then_inc(S("g_atm"), 1)
                        dve.wait_ge(S("g_o"), 8 * NBLK + 1)
                        for s in range(DB):
                            dve.wait_ge(S("gs_u"), s + 1)
                            at = TS * s + TS - 1
                            for e in range(2):
                                for j in range(2):
                                    p = slice(64 * e, 64 * e + 64)
                                    last = v.scalar_tensor_tensor(
                                        sin[p, s, j, :], sin[p, s, j, :], la[p, j, at:at + 1],
                                        bank[4 + s % 2][p, j * 256 + e * 128:j * 256 + e * 128 + 128],
                                        ALU.mult, ALU.add)
                            last.then_inc(S("gs_new"), 1)
                    dve.wait_ge(S("g_root"), b + 1)
                    newton(o2[:, :, 0:NT], qgz[:, :, 0:NT], qiz[:, :, 0:NT], qgz[:, :, 0:NT])
                    v.tensor_tensor(oT[:, :, 0:NT], oT[:, :, 0:NT], qgz[:, :, 0:NT], ALU.mult)
                    dve.drain()
                    dve.wait_ge(S("g_silu"), b + 1)
                    v.scalar_tensor_tensor(mixG[:, b % 2, :, 0:NT], oT[:, :, 0:NT], gates[:, 2:3],
                                           gr[:, :, 0:NT], ALU.mult, ALU.mult)
                if kind == "I" and b < NBLK:
                    for i in tiles_of(b):
                        if i < 2:
                            continue
                        base = SEQ * (i % 4)
                        for c, (k0, kn) in enumerate(score_chunks(i)):
                            out = Sf[:, base + k0:base + k0 + kn]
                            for h in range(HEADS):
                                n = IN[i, c, h]
                                w = iw[:, i % 4, h:h + 1]
                                dve.wait_ge(S("i_relu"), n + 1)
                                if h == 0:
                                    v.tensor_scalar(out, relu[:, n % 4, 0:kn], w, None, ALU.mult).then_inc(S("i_added"), 1)
                                else:
                                    v.scalar_tensor_tensor(out, relu[:, n % 4, 0:kn], w, out, ALU.mult, ALU.add
                                                           ).then_inc(S("i_added"), 1)
                                dve.drain()
                if kind == "I" and b == NBLK:
                    dve.wait_ge(S("si_zero"), 1)
                    for h in range(HEADS):
                        e, j = h % 2, h // 2
                        p = slice(64 * e, 64 * e + 64)
                        last = v.tensor_copy(iqz[p, :, 8 * h:8 * h + 8], iq[p, j, 0:NS].rearrange("p (s t) -> p s t", t=TS))
                    last.then_inc(S("si_iqz"), 1)
                    dve.wait_ge(S("rep_in"), 16)
                    for h in range(HEADS):
                        last = v.tensor_scalar(wrow[0:64, :, 8 * h:8 * h + 8], rep[0:64, :, 8 * h:8 * h + 8],
                                               iw[0:64, 0, h:h + 1], None, ALU.mult)
                    last.then_inc(S("si_wrow"), 1)
                    dve.wait_ge(S("si_sum"), DB)
                    v.tensor_tensor(sscore[:, PAST:LS], bank[7][0:64, 0:NS], cst[0:64, C_SEQ:C_SEQ + 64], ALU.add)
                if kind == "T":
                    pick_block(0)
                if kind == "F" and b < NBLK:
                    pick_block(b + 1)
                if kind == "A" and b < NBLK:
                    def mask(i, h):
                        u = 8 * i + h
                        if u >= 2:
                            pi, ph = (u - 2) // 8, (u - 2) % 8
                            dve.wait_ge(S("a_pT"), TN[pi, ph, -(-(pi + 1) // 4) - 1] + 1)
                            dve.wait_ge(S("a_exp"), u - 1)
                        cs = near_chunks(i)
                        for c, (k0, kn, near) in enumerate(cs):
                            n = QN[i, h, c]
                            dve.wait_ge(S("a_logits"), n + 1)
                            if near:
                                dve.wait_ge(S("a_near"), u + 1)
                                m = nearm[:, u % 2, 0:kn]
                            else:
                                at = SEQ * (i % 4) + k0
                                m = Sf[:, at:at + kn]
                            v.tensor_tensor_reduce(lg[:, u % 2, k0:k0 + kn], bank[n % 3][:, 0:kn], m, 1.0, OUTSIDE,
                                                   ALU.add, ALU.max, mx[:, u % 2, c:c + 1]).then_inc(S("a_masked"), 1)
                        dve.drain()
                        v.tensor_reduce(nmax[:, u % 2:u % 2 + 1], mx[:, u % 2, 0:len(cs)], AX.X, ALU.max,
                                        negate=True).then_inc(S("a_max"), 1)

                    def scale(i, h):
                        u = 8 * i + h
                        dve.wait_ge(S("a_pv"), u + 1)
                        v.reciprocal(rden[:, u % 2:u % 2 + 1], den[:, u % 2:u % 2 + 1])
                        if h == 0 and i >= 2:
                            dve.wait_ge(S("a_oT"), i - 1)
                        dve.drain()
                        v.tensor_scalar(osb[:, i % 2, 64 * h:64 * h + 64], bank[5 + u % 2][:, 0:64],
                                        rden[:, u % 2:u % 2 + 1], None, ALU.mult).then_inc(S("a_scaled"), 1)

                    units = [(i, h) for i in tiles_of(b) for h in range(HEADS)]
                    mask(*units[0])
                    for n in range(len(units)):
                        if n + 1 < len(units):
                            mask(*units[n + 1])
                        if n:
                            scale(*units[n - 1])
                    scale(*units[-1])
                if kind == "A" and b == NBLK:
                    dve.wait_ge(S("sa_zero"), 1)
                    for h in range(HEADS):
                        e, j = h % 2, h // 2
                        p = slice(64 * e, 64 * e + 64)
                        last = v.tensor_copy(qz[p, :, 8 * h:8 * h + 8], q[p, j, 0:NS].rearrange("p (s t) -> p s t", t=TS))
                    last.then_inc(S("sa_qz"), 1)
                    for s in range(DB):
                        dve.wait_ge(S("sa_logits"), s + 1)
                        if s >= 2:
                            dve.wait_ge(S("sa_pT"), s - 1)
                        out = slg[0:64, s % 2, :]
                        v.tensor_tensor(out[:, 0:PAST], bank[0][0:64, :], sbias[:, 0:PAST], ALU.add)
                        v.tensor_tensor(out[:, PAST:LS].rearrange("p (s t) -> p s t", t=TS),
                                        bank[1][0:64, 0:NS].rearrange("p (s t) -> p s t", t=TS),
                                        sbias[:, PAST:PAST + TS].unsqueeze(1).broadcast_to([64, DB, TS]),
                                        ALU.add).then_inc(S("sa_added"), 1)
                        dve.drain()
                        v.tensor_reduce(nmax[0:64, s % 2:s % 2 + 1], out, AX.X, ALU.max, negate=True).then_inc(S("sa_max"), 1)
                        dve.wait_ge(S("sa_exp"), s + 1)
                        v.reciprocal(rden[0:64, s % 2:s % 2 + 1], den[0:64, s % 2:s % 2 + 1])
                        dve.drain()
                        v.tensor_scalar(out, out, rden[0:64, s % 2:s % 2 + 1], None, ALU.mult).then_inc(S("sa_probs"), 1)
                    dve.wait_ge(S("sa_pv"), DB)
                    for h in range(HEADS):
                        e, j = h % 2, h // 2
                        v.tensor_copy(mixA[64 * e:64 * e + 64, j, 0:NS].rearrange("p (s t) -> p s t", t=TS),
                                      bank[6][0:64, :].rearrange("p (s m) -> p s m", m=64)[:, :, 8 * h:8 * h + 8])
                dve.drain().then_inc(S("end_dve"), 1)

        @block.gpsimd
        def _(pool):
            g = nc.gpsimd

            def newton(ms, r, tmp, out):
                g.tensor_tensor(tmp, r, r, ALU.mult)
                pool.drain()
                g.tensor_tensor(tmp, tmp, ms, ALU.mult)
                pool.drain()
                g.tensor_scalar(tmp, tmp, -0.5, 1.5, ALU.mult, ALU.add)
                pool.drain()
                g.tensor_tensor(out, tmp, r, ALU.mult)
                pool.drain()

            for nph, (kind, b) in enumerate(SCHED):
                NT = ntok(b)
                phase_start(pool, nph)
                stored_before(pool, nph)
                if kind == "B":
                    pool.wait_ge(S("consts_in"), 96)
                if kind == "G":
                    g.memset(qgz[:, :, 0:NT], 0.0)
                    g.memset(qiz[:, :, 0:NT], 0.0)
                    if b < NBLK:
                        g.memset(khz, 0.0)
                        g.memset(att, 0.0)
                    pool.drain().then_inc(S("g_zero"), 1)
                    pool.wait_ge(S("g_ex"), b + 1)
                    g.tensor_tensor(kg[:, :, 0:NT], gk[:, :, 0:NT], kg[:, :, 0:NT], ALU.mult)
                    g.tensor_tensor(kh[:, :, 0:NT], gk[:, :, 0:NT], kh[:, :, 0:NT], ALU.mult)
                    pool.drain().then_inc(S("g_k"), 1)
                    if b == NBLK:
                        for s in range(DB):
                            if s >= 2:
                                pool.wait_ge(S("gs_u"), s - 1)
                            g.tensor_scalar(gvz[0:NS, s % 2, :], gv[0:NS, 0, :], cst[0:NS, C_ROW + s:C_ROW + s + 1],
                                            None, ALU.mult).then_inc(S("gs_gvz"), 1)
                if kind == "I" and b == 0:
                    for i in range(2):
                        g.memset(Sf[:, SEQ * i:SEQ * i + 128 * (i + 1)], 0.0)
                    pool.drain()
                if kind == "I" and b == NBLK:
                    g.memset(iqz, 0.0).then_inc(S("si_zero"), 1)
                    g.memset(sscore[:, LS:LS + 6], 3e38)
                if kind == "I" and b < NBLK:
                    for i in tiles_of(b):
                        if i >= 2:
                            pool.wait_ge(S("i_added"), IN[i, len(score_chunks(i)) - 1, HEADS - 1] + 1)
                        at = SEQ * (i % 4) + 128 * i
                        diag = Sf[:, at:at + 128]
                        g.affine_select(out=diag, in_=diag, compare_op=ALU.is_ge, fill=OUTSIDE, base=0,
                                        pattern=[[-1, 128]], channel_multiplier=1)
                if kind == "A" and b < NBLK:
                    for i in tiles_of(b):
                        k0, kn, _near = near_chunks(i)[-1]
                        at = SEQ * (i % 4) + k0
                        for h in range(HEADS):
                            u = 8 * i + h
                            if u >= 2:
                                pool.wait_ge(S("a_max"), u - 1)
                            g.tensor_tensor(nearm[:, u % 2, 0:kn], Sf[:, at:at + kn],
                                            near_bias[:, h, 256 - kn:256], ALU.add).then_inc(S("a_near"), 1)
                if kind == "A" and b == NBLK:
                    g.memset(qz, 0.0).then_inc(S("sa_zero"), 1)
                if kind == "F":
                    pool.wait_ge(S("x_in"), 16 * x_loads(nph))
                    for dt in range(KT):
                        pool.wait_ge(S("o_copied"), KT * b + dt + 1)
                        g.tensor_tensor(X[:, dt, 0:NT], X[:, dt, 0:NT], outev[:, dt % 4, 0:NT], ALU.add
                                        ).then_inc(S("o_added"), 1)
                    pool.wait_ge(S("f_root"), b + 1)
                    newton(nF[0][:, 0:NT], nF[1][:, 0:NT], nF[2][:, 0:NT], nF[3][:, 0:NT])
                    for k in range(KT):
                        g.tensor_tensor(H[:, k, 0:NT], X[:, k, 0:NT], nF[3][:, 0:NT], ALU.mult).then_inc(S("f_scaled"), 1)
                    with pool.Fori(0, NF // 2) as i:
                        for s in range(2):
                            pool.wait_ge(S("u_bank_free"), i * 4 + (4 + 2 * NF * b + 2 * s + 2))
                            pool.sem_inc(S("pool_ticks"), 1)
                            g.tensor_tensor(U[:, bass.ds(i * 2 + s, 1), 0:NT].rearrange("p a n -> p (a n)"),
                                            ffev[:, 2 * s, 0:NT], ffev[:, 2 * s + 1, 0:NT], ALU.mult
                                            ).then_inc(S("u_pair_free"), 1)
                    with pool.Fori(0, KT // 2) as i:
                        for dt in range(2):
                            pool.wait_ge(S("d_bank_free"), i * 2 + (2 + KT * b + dt + 1))
                            pool.sem_inc(S("pool_ticks"), 1)
                            x = X[:, bass.ds(i * 2 + dt, 1), 0:NT].rearrange("p a n -> p (a n)")
                            g.tensor_tensor(x, x, ffev[:, dt, 0:NT], ALU.add).then_inc(S("d_buf_free"), 1)
                    pool.wait_ge(S("y_root"), b + 1)
                    newton(nF[0][:, 0:NT], nF[1][:, 0:NT], nF[2][:, 0:NT], nF[3][:, 0:NT])
                    for k in range(KT):
                        g.tensor_tensor(X[:, k, 0:NT], X[:, k, 0:NT], nF[3][:, 0:NT], ALU.mult).then_inc(S("y_scaled"), 1)
                pool.drain().then_inc(S("end_pool"), 1)


def outputs_of():
    return {
        "o_y": (128, KT, ALLT), "o_k": (64, KVH, ALLT), "o_v": (ALLT, KVH * HD), "o_ik": (64, ALLT),
        "o_gp": (128, 2, DV), "o_gs": (128, DB, 2, DV),
    }


def laid_out(i):
    def tiles(w, cols):
        return w.reshape(KT, 128, cols).transpose(1, 0, 2).reshape(128, KT * cols)

    w = np.asarray(i["w_in"])[0]
    at = dict(q=0, k=512, v=640, iq=768, ik=1280, iw=1344, gq=1352, gk=1608, gv=1864, gr=2376, glr=2888)
    parts = []
    for what, j in TILES:
        if what == "k":
            c = w[:, at["k"] + 64 * j:at["k"] + 64 * j + 64]
            c = np.concatenate([c, c], 1)
        elif what == "ik":
            c = w[:, at["ik"]:at["ik"] + 64]
            c = np.concatenate([c, c], 1)
        elif what == "glr":
            c = np.concatenate([w[:, at["glr"]:at["glr"] + RANK], w[:, at["iw"]:at["iw"] + 8],
                                np.zeros((D, 128 - RANK - 8), w.dtype)], 1)
        else:
            c = w[:, at[what] + 128 * j:at[what] + 128 * j + 128]
        parts.append(tiles(c, 128))
    wo, wg, wu, wd = (np.asarray(i[n])[0] for n in ("w_out", "w_gate", "w_up", "w_down"))
    x = np.concatenate([np.asarray(i["x_prompt"])[0], np.asarray(i["x_sample"]).reshape(NS, D)], 0)
    ck, cv, ci = (np.asarray(i[n])[0] for n in ("cache_k", "cache_v", "cache_idx_k"))
    kt = ck.transpose(0, 3, 2, 1)
    kt = np.concatenate([kt, kt], 1).reshape(NPOOL, 128, 256)
    it = ci.transpose(0, 2, 1)
    cache = np.concatenate([kt, np.concatenate([it, it], 1), cv.reshape(NPOOL, 128, 128)], 2)
    cst, rep, hots = constants()

    def col(v):
        return np.asarray(v).reshape(-1, 128).T

    kn = [np.concatenate([np.asarray(i[n])[0]] * 2) for n in ("idx_knorm_g", "idx_knorm_b")]
    out = {
        "xT": x.T.reshape(KT, 128, ALLT).transpose(1, 0, 2),
        "w_in": np.stack(parts),
        "w_out": np.stack([tiles(wo[:, 128 * t:128 * t + 128], 128) for t in range(KT)]),
        "w_gu": np.stack([np.concatenate([tiles(m[:, 128 * f:128 * f + 128], 128) for m in (wg, wu)], 1)
                          for f in range(NF)]),
        "w_d": wd.reshape(2, NF // 2, 128, KT, 128).transpose(3, 0, 2, 1, 4).reshape(2 * KT, 128, NF // 2 * 128),
        "cache": cache,
        "state": np.asarray(i["state_gla"])[0],
        "pages": np.asarray(i["page_table"]).reshape(1, DB * NPG),
        "gains": np.concatenate([col(i["attn_norm_g"]), col(i["ffn_norm_g"]), col(i["final_norm_g"])], 1),
        "gates": np.concatenate([col(i["gla_gate_b"]), col(i["gla_onorm_g"]), col(kn[0]), col(kn[1])], 1),
        "gate_up": np.asarray(i["gla_gate_up"])[0],
        "rel_bias": np.asarray(i["rel_bias"]),
        "consts": cst, "rep": rep, "hots": hots,
    }
    return {k: np.ascontiguousarray(v) for k, v in out.items()}


def returned(r):
    y = r["o_y"].transpose(1, 0, 2).reshape(D, ALLT).T
    k = r["o_k"].transpose(2, 1, 0)
    vv = r["o_v"].reshape(ALLT, KVH, HD)
    ik = r["o_ik"].T
    gp = r["o_gp"].reshape(2, 64, 2, DV).transpose(2, 0, 1, 3).reshape(1, 1, GH, DK, DV)
    gs = r["o_gs"].reshape(2, 64, DB, 2, DV).transpose(2, 3, 0, 1, 4).reshape(1, DB, GH, DK, DV)
    c = np.ascontiguousarray
    return (c(y[:SEQ].reshape(1, SEQ, D)), c(y[SEQ:].reshape(DB, TS, D)),
            c(k[:SEQ].reshape(1, 1, SEQ, KVH, HD)), c(vv[:SEQ].reshape(1, 1, SEQ, KVH, HD)),
            c(ik[:SEQ].reshape(1, 1, SEQ, HD)), c(gp),
            c(k[SEQ:].reshape(1, DB, TS, KVH, HD)), c(vv[SEQ:].reshape(1, DB, TS, KVH, HD)),
            c(ik[SEQ:].reshape(1, DB, TS, HD)), c(gs))


def kernel(**inputs):
    import concourse.bacc as bacc
    from concourse.bass_utils import run_bass_kernel_spmd

    arrays = {"in_" + n: v for n, v in laid_out(inputs).items()}
    nc = bacc.Bacc("TRN2", target_bir_lowering=False, num_devices=1)
    a = {n[3:]: nc.dram_tensor(n, v.shape, mybir.dt.from_np(v.dtype), kind="ExternalInput").ap()
         for n, v in arrays.items()}
    for n, shape in outputs_of().items():
        a[n] = nc.dram_tensor(n, shape, F32, kind="ExternalOutput").ap()
    layer(nc, a)
    r = run_bass_kernel_spmd(nc, [arrays], core_ids=[0])
    return returned(r.results[0])
```

```python
from contextlib import ExitStack

import numpy as np

import concourse.bass as bass
from concourse import mybir

F32 = mybir.dt.float32
F16 = mybir.dt.float16
I32 = mybir.dt.int32
ALU = mybir.AluOpType
ACT = mybir.ActivationFunctionType
AX = mybir.AxisListType

D = 1024
KT = D // 128
SEQ = 2048
TOK = 512
NBLK = SEQ // TOK
DB, TS = 8, 8
NS = DB * TS
ALLT = SEQ + NS
PAST = 512
PAGE = 128
NPG = PAST // PAGE
NPOOL = 40
LS = PAST + NS
HEADS, KVH, HD = 8, 2, 64
GH, DK, DV = 4, 64, 128
CH = 64
RANK = 16
FF = 2816
NF = FF // 128
TOPK = 256
TOPK_S = (PAST + TS) // 4
RB, RD = 32, 128
EPS, LN_EPS = 1e-6, 1e-5
OUTSIDE = -1e30
TAKEN = -3e38
TAKEN_CUT = -2e38
W1, W2 = 384, 528

TILES = ([("glr", 0), ("ik", 0)] + [("gk", j) for j in range(2)] + [("gq", j) for j in range(2)]
         + [("iq", j) for j in range(4)] + [("k", g) for g in range(2)] + [("q", j) for j in range(4)]
         + [("gr", j) for j in range(4)] + [("v", 0)] + [("gv", j) for j in range(4)])
P_UNITS = TILES + [("iw", 0)]
SPLIT = ("iq", "q", "k")
NSPLIT = sum(what in SPLIT for what, _ in P_UNITS)
Q_UP, K_UP = 8.0, 16.0
Q_SCALE = Q_UP * K_UP * HD ** 0.5
I_UP = 16.0
W_UP, H_UP, M_UP, U_UP = 256.0, 64.0, 16.0, 4.0
WT = KT * 128
ND = 4
D_BLOCKS = (range(0, 6), range(6, 11), range(11, 17), range(17, 22))

C_ID, C_ONE, C_TRI, C_TRI8, C_ROW, C_SEQ, C_EPS, C_LNEPS = (
    0, 128, 256, 320, 384, 392, 456, 457)
NC_COLS = 458


def bucket_table():
    n = np.arange(1024)
    f = np.log(np.maximum(n, 1).astype(np.float32) / np.float32(RB // 2)) / np.float32(np.log(RD / (RB // 2)))
    large = np.minimum(RB // 2 + (f * np.float32(RB - RB // 2)).astype(np.int32), RB - 1)
    return np.where(n < RB // 2, n, large)


def constants():
    c = np.zeros((128, NC_COLS), np.float32)
    p = np.arange(128)[:, None]
    t64 = np.arange(64)[None, :]
    c[:, C_ID:C_ID + 128] = np.eye(128)
    c[:, C_ONE:C_ONE + 128] = 1.0
    c[:, C_TRI:C_TRI + 64] = (p % 64) <= t64
    same = (p // TS == t64 // TS) & (p <= t64)
    c[:, C_TRI8:C_TRI8 + 64] = same
    c[:, C_ROW:C_ROW + 8] = (p // TS) == np.arange(8)[None, :]
    c[:, C_SEQ:C_SEQ + 64] = np.where((p // TS == t64 // TS) & (p >= t64), 0.0, OUTSIDE)
    c[:, C_EPS] = EPS
    c[:, C_LNEPS] = LN_EPS
    rep = np.zeros((64, DB, HEADS * TS), np.float32)
    for b in range(DB):
        for m in range(HEADS * TS):
            rep[b * TS + m % TS, b, m] = 1.0
    bucket = bucket_table()
    far = bucket == RB - 1
    assert far[RD:].all()
    hot1 = np.zeros((RB, W1), np.float32)
    hot2 = np.zeros((RB, W2), np.float32)
    for u in range(W1):
        hot1[bucket[max(255 - u, 0)], u] += 1.0
    for u in range(W2):
        hot2[bucket[max(PAST + TS - 1 - u, 0)], u] += 1.0
    hot1[RB - 1] -= 1.0
    hot2[RB - 1] -= 1.0
    return c, rep.reshape(64, -1), np.concatenate([hot1, hot2], 1)


def near_chunks(i):
    keys = 128 * (i + 1)
    near = min(256, keys)
    far = keys - near
    out = [(a, min(512, far - a), False) for a in range(0, far, 512)]
    return out + [(far, near, True)]


def score_chunks(i):
    keys = 128 * (i + 1)
    return [(a, min(512, keys - a)) for a in range(0, keys, 512)]


def layer(nc, a):
    with ExitStack() as ctx:
        def sb(name, shape, dt=F32):
            return ctx.enter_context(nc.sbuf_tensor(name, shape, dt))

        bank = [ctx.enter_context(nc.psum_tensor(f"bank{i}", [128, 512], F32)) for i in range(8)]
        skew1 = nc.dram_tensor("skew1", (HEADS, 128, W1), F32, kind="Internal").ap()
        skew2 = nc.dram_tensor("skew2", (HEADS, TS, W2), F32, kind="Internal").ap()

        cst = sb("cst", [128, NC_COLS])
        kT = sb("kT", [128, KVH, 2, SEQ], F16)
        ikT = sb("ikT", [128, 2, SEQ], F16)
        kTs = sb("kTs", [128, KVH, NS])
        ikTs = sb("ikTs", [128, NS])
        vtok = sb("vtok", [128, SEQ // 128, 128])
        vnew = sb("vnew", [NS, 128])
        near_bias = sb("near_bias", [128, HEADS, 256])
        gvec = sb("gvec", [128, 3 * KT])
        gates = sb("gates", [128, 5])
        gate_up = sb("gate_up", [RANK, 2 * 128])
        state = sb("state", [128, 2, DV])
        X = sb("X", [128, KT, TOK])
        H = sb("H", [128, 2, KT, TOK], F16)
        q = sb("q", [128, HEADS, TOK], F16)
        iw = sb("iw", [128, TOK // 128, 8])
        scores = sb("scores", [128, 4 * SEQ - 6 * 128])
        R = sb("R", [128, NF * TOK])
        mixA = sb("mixA", [128, 2, 4, TOK], F16)
        mixG = sb("mixG", [128, 2, 2, GH, TOK], F16)
        raw = sb("raw", [128, 2, WT])
        ring = sb("ring", [128, 4, 2, WT], F16)
        top8 = sb("top8", [128, 8])
        mx = sb("mx", [128, 2, 8])
        nmax = sb("nmax", [128, 2])
        den = sb("den", [128, 4])
        rden = sb("rden", [128, 4])
        pages = sb("pages", [1, DB * NPG], I32)

        ident = cst[:, C_ID:C_ID + 128]
        ones = cst[:, C_ONE:C_ONE + 128]
        eps = cst[:, C_EPS:C_EPS + 1]
        lneps = cst[:, C_LNEPS:C_LNEPS + 1]

        def cut(t, at, *dims):
            n = int(np.prod(dims))
            v = t[:, at:at + n]
            if len(dims) == 1:
                return v
            if len(dims) == 2:
                return v.rearrange("p (a b) -> p a b", b=dims[1])
            return v.rearrange("p (a b c) -> p a b c", b=dims[1], c=dims[2])

        Xf = X[:, :, :].rearrange("p k n -> p (k n)")
        Hf = H[:, :, :, :].rearrange("p s k n -> p (s k n)").bitcast(F32)
        Sf = scores[:, :]
        Rf = R[:, :]
        hots = cut(Rf, 0, W1 + W2)
        relb = cut(Rf, 1024, HEADS)
        relw = cut(Rf, 1032, HEADS, 128)
        row1 = cut(Rf, 2056, HEADS, W1)
        row2 = cut(Rf, 2056 + HEADS * W1, HEADS, W2)
        sq = cut(Rf, 0, KT, TOK)
        iq = cut(Rf, 0, 2048).bitcast(F16).rearrange("p (h n) -> p h n", n=TOK)
        iqs = cut(Rf, 0, 4, TOK)
        qs = q[:, :, :].rearrange("p h n -> p (h n)").bitcast(F32).rearrange("p (j n) -> p j n", n=TOK)
        k32 = cut(Xf, 2048, KVH, TOK)
        ik32 = cut(Rf, 9216, TOK)
        gq = cut(Rf, 2048, 2, TOK)
        gk = cut(Rf, 3072, 2, TOK)
        gr = cut(Rf, 4096, 4, TOK)
        la = cut(Rf, 6144, 2, TOK)
        gv = cut(Rf, 7168, 4, TOK)
        glr = cut(Rf, 9216, TOK)
        att = cut(Rf, 9728, 2, 4, 128)
        khs = cut(Rf, 9728, 256)
        atts = cut(Rf, 9984, 4, 64)
        cum = cut(Sf, 0, 2, TOK)
        exa = cut(Sf, 1024, 2, TOK)
        exb = cut(Sf, 2048, 2, TOK)
        qgz = cut(Sf, 3072, 4, TOK)
        qiz = cut(Sf, 5120, 4, TOK)
        ikx = cut(Rf, 10752, TOK)
        rst = cut(Rf, 9728, TOK)
        ikc = cut(Rf, 10240, TOK)
        gvz = cut(Sf, 2048, 2, 512)
        nG = [cut(Xf, 512 * j, TOK) for j in range(4)]
        kg = cut(Xf, 0, 2, TOK)
        kh = cut(Xf, 1024, 2, TOK)
        khz = cut(Xf, 2048, 4, 2, 256)
        sin = cut(Xf, 2048, DB, 2, DV)
        oT = cut(Hf, 0, GH, TOK)
        o2 = cut(Hf, 2048, GH, TOK)
        nP = [cut(Sf, 512 * j, TOK) for j in range(4)]
        nF = [cut(Rf, 4096 + 512 * j, TOK) for j in range(4)]
        hn = cut(Rf, 0, KT, TOK)
        relu = cut(Rf, 2048, 4, 512)
        lg = cut(Rf, 0, 2, 2048)
        pT = cut(Rf, 4096, 2, 16, 128)
        nearm = cut(Rf, 8192, 2, 256)
        osb = cut(Rf, 8704, 2, 512)
        mix32 = cut(Rf, 9728, 4, 128)
        iqz = cut(Rf, 2048, DB, 64)
        rep = cut(Rf, 2560, DB, 64)
        cache = cut(Rf, 4096, 2, NPG, 512)
        srelu = cut(Rf, 8192, 2, LS)
        wrow = cut(Rf, 9344, DB, 64)
        wsel = cut(Rf, 9856, DB, 64)
        qz = cut(Rf, 2048, DB, 64)
        slg = cut(Rf, 8192, 2, LS)
        spT = cut(Rf, 9344, 2, 5, 64)
        sbias = cut(Rf, 9984, PAST + TS)[0:HEADS * TS]
        sscore = Sf[0:64, 0:LS + 6]
        outev = cut(Rf, 6144, 4, 512)
        H32 = cut(Hf, 0, KT, TOK)
        U = Rf.bitcast(F16).rearrange("p (f s n) -> p f s n", s=2, n=TOK)
        ffev = mixA[:, :, :, :].rearrange("p s j n -> p (s j n)").bitcast(F32).rearrange("p (j n) -> p j n", n=TOK)

        sems = {}

        def S(name):
            if name not in sems:
                sems[name] = ctx.enter_context(nc.semaphore(name))
            return sems[name]

        SCHED = [("B", 0), ("P", 0), ("G", 0), ("I", 0), ("T", 0), ("A", 0)]
        for b in range(1, NBLK + 1):
            SCHED += [("P", b), ("G", b), ("I", b), ("F", b - 1), ("A", b)]
        SCHED += [("F", NBLK)]

        def ntok(b):
            return TOK if b < NBLK else NS

        ENG = ("pe", "act", "dve", "pool")

        def phase_start(eng, n):
            if n:
                for who in ENG:
                    eng.wait_ge(S("end_" + who), n)

        base, at = {}, 0
        for kind, b in SCHED:
            for part, count in {"P": [("P", len(TILES))],
                                "F": [("O", KT), ("U", 2 * NF), ("D", ND * KT)]}.get(kind, []):
                base[part, b] = at
                at += count

        def value(c, i, step):
            return c if i is None else i * step + c

        def first_tiles(nph):
            if nph + 1 == len(SCHED) or SCHED[nph + 1][0] not in "PF":
                return [], None
            kind, b = SCHED[nph + 1]
            n = base[{"P": "P", "F": "O"}[kind], b]
            return range(n, n + 4), lows_by(kind, b)

        def lows_by(kind, b):
            return "pool" if kind == "F" and b < NBLK else "dve"

        def score_at(i):
            return sum(128 * (j + 1) for j in range(12, 12 + i % 4))

        IU = [(i, c, h) for i in range(2, 16) for c in range(len(score_chunks(i))) for h in range(HEADS)]
        IN = {u: n for n, u in enumerate(IU)}
        AU = [(i, h) for i in range(16) for h in range(HEADS)]
        QU = [(i, h, c) for i, h in AU for c in range(len(near_chunks(i)))]
        QN = {u: n for n, u in enumerate(QU)}
        TU = [(i, h, g) for i, h in AU for g in range(-(-(i + 1) // 4))]
        TN = {u: n for n, u in enumerate(TU)}

        def x_loads(nph):
            return 1 + sum(k in "PF" for k, _ in SCHED[:nph])

        def tiles_of(b):
            return range(4 * b, 4 * b + 4)

        block = ctx.enter_context(nc.Block())

        @block.sync
        def _(sp):
            sp.dma_start(cst[:, :], a["consts"]).then_inc(S("consts_in"), 16)
            sp.dma_start(hots[0:RB], a["hots"]).then_inc(S("consts_in"), 16)
            sp.dma_start(relb[0:RB], a["rel_bias"]).then_inc(S("consts_in"), 16)
            sp.dma_start(gvec[:, :], a["gains"]).then_inc(S("consts_in"), 16)
            sp.dma_start(gates[:, :], a["gates"]).then_inc(S("consts_in"), 16)
            sp.dma_start(gate_up[:, :], a["gate_up"]).then_inc(S("consts_in"), 16)
            sp.dma_start(pages[:, :], a["pages"]).then_inc(S("pages_in"), 16)
            stores = 0

            def weights(n, src, i=None, step=0):
                cols = src.shape[-1]
                if n >= 2:
                    sp.wait_ge(S("w_split"), value(n - 1, i, step))
                sp.dma_start(raw[:, n % 2, 0:cols], src).then_inc(S(f"weights_in{n % 2}"), 16)

            def load_cache(n, s):
                for p in range(NPG):
                    at = sp.value_load(pages[0:1, s * NPG + p:s * NPG + p + 1], min_val=0, max_val=NPOOL - 1)
                    sp.dma_start(cache[:, n % 2, p, :],
                                 a["cache"][bass.ds(at, 1)].rearrange("o p n -> p (o n)")
                                 ).then_inc(S(f"cache_in{n % 2}"), 16)

            for nph, (kind, b) in enumerate(SCHED):
                NT = ntok(b)
                t0 = TOK * b
                if kind == "B":
                    sp.wait_ge(S("pages_in"), 16)
                    sp.wait_ge(S("bias_rows"), 1)
                    sp.dma_start(skew1.rearrange("h p w -> p h w"), row1).then_inc(S("skew_dma"), 16)
                    sp.dma_start(skew2.rearrange("h p w -> p h w"), row2[0:TS]).then_inc(S("skew_dma"), 16)
                    sp.wait_ge(S("skew_dma"), 32)
                    sp.dma_start(near_bias[:, :, :],
                                 bass.AP(skew1.tensor, 127, [[W1 - 1, 128], [128 * W1, HEADS], [1, 256]])
                                 ).then_inc(S("skew_dma"), 16)
                if kind == "P":
                    n0 = base["P", b]
                    for t in range(4):
                        weights(n0 + t, a["w_in"][t])
                    phase_start(sp, nph)
                    sp.dma_start(X[:, :, 0:NT], a["xT"][:, :, t0:t0 + NT]).then_inc(S("x_in"), 16)
                    for t in range(4, len(TILES)):
                        weights(n0 + t, a["w_in"][t])
                        if t == 18 and b < NBLK:
                            sp.wait_ge(S("p_split"), NSPLIT * b + 6)
                            sp.dma_start(a["o_k"][:, :, t0:t0 + NT], k32[0:64]).then_inc(S("outputs"), 16)
                            stores += 16
                    if stores:
                        sp.wait_ge(S("outputs"), stores)
                    sp.sem_inc(S("stored"), 1)
                if kind == "G" and b == NBLK:
                    phase_start(sp, nph)
                    for e in range(2):
                        for j in range(2):
                            sp.dma_start(sin[64 * e:64 * e + 64, :, j, :],
                                         a["state"][:, 2 * j + e].rearrange("b k v -> k b v")
                                         ).then_inc(S("state_in"), 16)
                if kind == "I":
                    phase_start(sp, nph)
                    pairs = [(a["o_ik"][:, t0:t0 + NT], (ik32 if b < NBLK else ikTs)[0:64])]
                    if b < NBLK:
                        pairs.append((a["o_v"][t0:t0 + NT].rearrange("(t p) n -> p t n", p=128),
                                      vtok[:, 4 * b:4 * b + 4, :]))
                    else:
                        pairs += [(a["o_k"][:, :, t0:t0 + NT], kTs[0:64]),
                                  (a["o_v"][t0:t0 + NT], vnew[:, :]), (a["o_gs"], sin)]
                    if b == NBLK - 1:
                        pairs.append((a["o_gp"], state[:, :, :]))
                    for dst, src in pairs:
                        sp.dma_start(dst, src).then_inc(S("outputs"), 16)
                        stores += 16
                    sp.wait_ge(S("outputs"), stores)
                    sp.sem_inc(S("stored"), 1)
                    if b == NBLK:
                        sp.dma_start(rep[0:64], a["rep"].rearrange("p (a b) -> p a b", b=64)
                                     ).then_inc(S("rep_in"), 16)
                        for s in range(DB):
                            if s >= 2:
                                sp.wait_ge(S("si_dots"), s - 1)
                            load_cache(s, s)
                if kind == "A" and b == NBLK:
                    phase_start(sp, nph)
                    sp.dma_start(rep[0:64], a["rep"].rearrange("p (a b) -> p a b", b=64)
                                 ).then_inc(S("rep_in"), 16)
                    for h in range(HEADS):
                        sp.dma_start(sbias[h * TS:(h + 1) * TS, :],
                                     bass.AP(skew2.tensor, h * TS * W2 + TS - 1, [[W2 - 1, TS], [1, PAST + TS]])
                                     ).then_inc(S("sbias_in"), 16)
                    for s in range(DB):
                        if s >= 2:
                            sp.wait_ge(S("sa_pv"), s - 1)
                        load_cache(s, s)
                if kind == "F":
                    n0 = base["O", b]
                    for t in range(4):
                        weights(n0 + t, a["w_out"][t])
                    phase_start(sp, nph)
                    sp.dma_start(X[:, :, 0:NT], a["xT"][:, :, t0:t0 + NT]).then_inc(S("x_in"), 16)
                    for t in range(4, KT):
                        weights(n0 + t, a["w_out"][t])
                    with sp.Fori(0, NF // 2) as i:
                        for r in range(4):
                            row = a["w_gu"][bass.ds(i * 2 + r // 2, 1)].rearrange("t p m -> p (t m)")
                            weights(base["U", b] + r, row[:, WT * (r % 2):WT * (r % 2) + WT], i, 4)
                    with sp.Fori(0, KT // 2) as i:
                        for r in range(2 * ND):
                            row = a["w_d"][bass.ds(i * 2 + r // ND, 1)].rearrange("t p m -> p (t m)")
                            ks = D_BLOCKS[r % ND]
                            weights(base["D", b] + r, row[:, 128 * ks[0]:128 * ks[-1] + 128], i, 2 * ND)
                    sp.wait_ge(S("f_y"), b + 1)
                    sp.dma_start(a["o_y"][:, :, t0:t0 + NT], H32[:, :, 0:NT]).then_inc(S("outputs"), 16)
                    stores += 16
                    sp.wait_ge(S("outputs"), stores)
                    sp.sem_inc(S("stored"), 1)

        def halves(h):
            e = 64 * (h % 2)
            return slice(e, e + 64), slice(64 - e, 128 - e)

        def out_counts(b, u):
            split = [b < NBLK and what in SPLIT for what, _ in P_UNITS]
            n = min(b, NBLK)
            before = NSPLIT * n
            return (len(P_UNITS) * b - before + split[:u + 1].count(False),
                    before + split[:u + 1].count(True))

        def stored_before(eng, nph):
            n = sum(1 for k, _ in SCHED[:nph] if k in "PIF")
            if n:
                eng.wait_ge(S("stored"), n)

        @block.tensor
        def _(pe):
            mm = nc.tensor.matmul

            def weights_at(n, i=None, step=0):
                pe.wait_ge(S("w_split"), value(n + 1, i, step))
                return ring[:, n % 4, 0, :], ring[:, n % 4, 1, :]

            def three(o, lhs, rhs, first, last):
                mm(o, lhs[0], rhs[0], start=first, stop=False)
                mm(o, lhs[0], rhs[1], start=False, stop=False)
                return mm(o, lhs[1], rhs[0], start=False, stop=last)

            for nph, (kind, b) in enumerate(SCHED):
                NT = ntok(b)
                t0 = TOK * b
                ntile = NT // 128 if b < NBLK else 1
                tw = min(NT, 128)
                phase_start(pe, nph)
                if kind == "B":
                    pe.wait_ge(S("bias_wide"), 1)
                    for h in range(HEADS):
                        if h >= 2:
                            pe.wait_ge(S("bias_copied"), h - 1)
                        k = 3 * (h % 2)
                        mm(bank[k][:, 0:W1], relw[0:RB, h, :], hots[0:RB, 0:W1], start=True, stop=True)
                        mm(bank[k + 1][:, 0:512], relw[0:RB, h, :], hots[0:RB, W1:W1 + 512], start=True, stop=True)
                        mm(bank[k + 2][:, 0:W2 - 512], relw[0:RB, h, :], hots[0:RB, W1 + 512:W1 + W2],
                           start=True, stop=True).then_inc(S("bias_mm"), 1)
                if kind == "P":
                    pe.wait_ge(S("p_sq"), b + 1)
                    for k in range(KT):
                        last = mm(bank[7][:, 0:NT], ones, sq[:, k, 0:NT], start=(k == 0), stop=(k == KT - 1))
                    last.then_inc(S("p_ss"), 1)
                    for u, (what, j) in enumerate(TILES):
                        w = weights_at(base["P", b] + u)
                        if u >= 4:
                            copied, taken = out_counts(b, u - 4)
                            if b < NBLK and TILES[u - 4][0] in SPLIT:
                                pe.wait_ge(S("p_split"), taken)
                            else:
                                pe.wait_ge(S("p_copied"), copied)

                        def token_rows(o, lo, hi):
                            for t in range(ntile):
                                for k in range(KT):
                                    last = three(o[0:tw, t * (hi - lo):(t + 1) * (hi - lo)],
                                                 [H[:, s, k, t * 128:t * 128 + tw] for s in range(2)],
                                                 [w[s][:, 128 * k + lo:128 * k + hi] for s in range(2)],
                                                 k == 0, k == KT - 1)
                            return last

                        if what in ("v", "gv"):
                            last = token_rows(bank[u % 4], 0, 128)
                        else:
                            hi = RANK if what == "glr" else 128
                            for k in range(KT):
                                if u == 0:
                                    pe.wait_ge(S("p_h"), KT * b + k + 1)
                                last = three(bank[u % 4][0:hi, 0:NT],
                                             [w[s][:, 128 * k:128 * k + hi] for s in range(2)],
                                             [H[:, s, k, 0:NT] for s in range(2)], k == 0, k == KT - 1)
                            if what == "glr":
                                last = token_rows(bank[4], RANK, RANK + 8)
                        last.then_inc(S("products"), 1)
                        if u == 3:
                            pe.wait_ge(S("p_copied"), out_counts(b, 1)[0])
                            mm(bank[7][:, 0:NT], ones, ikx[:, 0:NT], start=True, stop=True).then_inc(S("g_mean"), 1)
                            for j in range(2):
                                last = mm(bank[5 + j][:, 0:NT], gate_up[:, j * 128:(j + 1) * 128],
                                          glr[0:RANK, 0:NT], start=True, stop=True)
                            last.then_inc(S("g_gate"), 1)
                        if u == 6:
                            pe.wait_ge(S("g_ikc"), b + 1)
                            mm(bank[7][:, 0:NT], ones, ikx[:, 0:NT], start=True, stop=True).then_inc(S("g_var"), 1)
                if kind == "G":
                    pe.wait_ge(S("g_k"), b + 1)
                    pe.wait_ge(S("g_q"), b + 1)
                    if b < NBLK:
                        for t in range(4):
                            T = 4 * b + t
                            c0 = 128 * t
                            if t >= 2:
                                pe.wait_ge(S("g_khz"), T - 1)
                            for j in range(2):
                                last = nc.tensor.transpose(bank[t % 2][:, j * 128:(j + 1) * 128],
                                                           kh[:, j, c0:c0 + 128], ident)
                            last.then_inc(S("g_kt"), 1)
                            if t >= 2:
                                pe.wait_ge(S("g_atm"), T - 1)
                            for c in range(2):
                                for h in range(GH):
                                    cc = c0 + CH * c
                                    last = mm(bank[2 + t % 2][64 * c:64 * c + 64, h * 64:(h + 1) * 64],
                                              kg[:, h // 2, cc:cc + CH], qgz[:, h, cc:cc + CH],
                                              start=True, stop=True)
                            last.then_inc(S("g_at"), 1)
                            pe.wait_ge(S("g_atm"), T + 1)
                            pe.wait_ge(S("g_khz"), T + 1)
                            if t >= 2:
                                pe.wait_ge(S("g_oc"), T - 1)
                            for h in range(GH):
                                mm(bank[6 + t % 2][:, h * 128:(h + 1) * 128], gv[:, t, h * 128:(h + 1) * 128],
                                   att[:, t % 2, h, :], start=(h == 0), stop=False, skip_group_check=True)
                            for c in range(2):
                                cc = c0 + CH * c
                                n = 2 * T + c
                                if n:
                                    pe.wait_ge(S("g_state"), n)
                                for h in range(GH):
                                    mm(bank[6 + t % 2][:, h * 128 + CH * c:h * 128 + CH * c + CH],
                                       state[:, h // 2, :], qiz[:, h, cc:cc + CH],
                                       start=False, stop=(c == 1), skip_group_check=True)
                                for j in range(2):
                                    last = mm(bank[4 + c][:, j * 256:(j + 1) * 256],
                                              khz[:, t, c, j * 128:(j + 1) * 128],
                                              gv[:, t, j * 256:(j + 1) * 256], start=True, stop=True)
                                last.then_inc(S("g_o"), 1)
                    else:
                        for j in range(2):
                            last = nc.tensor.transpose(bank[0][0:NS, j * 128:(j + 1) * 128], kh[:, j, 0:NS], ident)
                        last.then_inc(S("g_kt"), 1)
                        for h in range(GH):
                            last = mm(bank[2][0:NS, h * 64:(h + 1) * 64], kg[:, h // 2, 0:NS], qgz[:, h, 0:NS],
                                      start=True, stop=True)
                        last.then_inc(S("g_at"), 1)
                        pe.wait_ge(S("g_atm"), 4 * NBLK + 1)
                        pe.wait_ge(S("state_in"), 64)
                        for h in range(GH):
                            mm(bank[6][:, h * 64:(h + 1) * 64], gv[0:NS, 0, h * 128:(h + 1) * 128],
                               atts[0:NS, h, :], start=(h == 0), stop=False, skip_group_check=True)
                        for s in range(DB):
                            for h in range(GH):
                                last = mm(bank[6][:, h * 64 + TS * s:h * 64 + TS * s + TS], sin[:, s, h // 2, :],
                                          qiz[:, h, TS * s:TS * s + TS], start=False, stop=True,
                                          skip_group_check=True)
                        last.then_inc(S("g_o"), 1)
                        pe.wait_ge(S("g_khz"), 4 * NBLK + 1)
                        for s in range(DB):
                            pe.wait_ge(S("gs_gvz"), s + 1)
                            if s >= 2:
                                pe.wait_ge(S("gs_new"), s - 1)
                            for j in range(2):
                                last = mm(bank[4 + s % 2][:, j * 256:(j + 1) * 256], khs[0:NS, j * 128:(j + 1) * 128],
                                          gvz[0:NS, s % 2, j * 256:(j + 1) * 256], start=True, stop=True)
                            last.then_inc(S("gs_u"), 1)
                    pe.wait_ge(S("g_o2"), b + 1)
                    for h in range(GH):
                        last = mm(bank[h][:, 0:NT], ones, o2[:, h, 0:NT], start=True, stop=True)
                    last.then_inc(S("g_oss"), 1)
                if kind == "I" and b < NBLK:
                    for i in tiles_of(b):
                        if i < 2:
                            continue
                        cq = 128 * (i % 4)
                        for c, (k0, kn) in enumerate(score_chunks(i)):
                            for h in range(HEADS):
                                n = IN[i, c, h]
                                if n >= 8:
                                    pe.wait_ge(S("i_relu"), n - 7)
                                mm(bank[n % 8][:, 0:kn], iq[:, h, cq:cq + 128], ikT[:, 0, k0:k0 + kn],
                                   start=True, stop=False)
                                mm(bank[n % 8][:, 0:kn], iq[:, h, cq:cq + 128], ikT[:, 1, k0:k0 + kn],
                                   start=False, stop=True).then_inc(S("i_dots"), 1)
                if kind == "I" and b == NBLK:
                    pe.wait_ge(S("si_wrow"), 1)
                    for s in range(DB):
                        last = mm(bank[0][0:64, s * 64:(s + 1) * 64], wrow[0:64, s, :], ident[0:64, 0:64],
                                  start=True, stop=True)
                    last.then_inc(S("si_wt"), 1)
                    pe.wait_ge(S("si_iqz"), 1)
                    for s in range(DB):
                        pe.wait_ge(S(f"cache_in{s % 2}"), 16 * NPG * (s // 2 + 1))
                        if s >= 2:
                            pe.wait_ge(S("si_relu"), s - 1)
                        mm(bank[2 + 2 * (s % 2)][0:64, :], iqz[:, s, :], cache[:, s % 2, :, 256:384],
                           start=True, stop=True)
                        mm(bank[3 + 2 * (s % 2)][0:64, 0:NS], iqz[:, s, :], ikTs[:, :],
                           start=True, stop=True).then_inc(S("si_dots"), 1)
                        pe.wait_ge(S("si_wsel"), 1)
                        pe.wait_ge(S("si_relu"), s + 1)
                        mm(bank[6][0:64, :], wsel[0:64, s, :], srelu[0:64, s % 2, 0:PAST],
                           start=(s == 0), stop=(s == DB - 1))
                        mm(bank[7][0:64, 0:NS], wsel[0:64, s, :], srelu[0:64, s % 2, PAST:LS],
                           start=(s == 0), stop=(s == DB - 1)).then_inc(S("si_sum"), 1)
                if kind == "A" and b < NBLK:
                    def logits(i, h):
                        cq = 128 * (i % 4)
                        for c, (k0, kn, near) in enumerate(near_chunks(i)):
                            n = QN[i, h, c]
                            if n >= 3:
                                pe.wait_ge(S("a_masked"), n - 2)
                            mm(bank[n % 3][:, 0:kn], q[:, h, cq:cq + 128], kT[:, h // 4, 0, k0:k0 + kn],
                               start=True, stop=False)
                            mm(bank[n % 3][:, 0:kn], q[:, h, cq:cq + 128], kT[:, h // 4, 1, k0:k0 + kn],
                               start=False, stop=True).then_inc(S("a_logits"), 1)

                    def turn(i, h, groups):
                        u = 8 * i + h
                        pe.wait_ge(S("a_exp"), u + 1)
                        for g in range(-(-(i + 1) // 4))[groups]:
                            n = TN[i, h, g]
                            if n >= 2:
                                pe.wait_ge(S("a_pTc"), n - 1)
                            for t in range(4 * g, min(4 * g + 4, i + 1)):
                                last = nc.tensor.transpose(bank[3 + n % 2][:, 128 * (t % 4):128 * (t % 4) + 128],
                                                           lg[:, u % 2, 128 * t:128 * t + 128], ident)
                            last.then_inc(S("a_pT"), 1)

                    def values(i, h):
                        u = 8 * i + h
                        pe.wait_ge(S("a_pTc"), TN[i, h, -(-(i + 1) // 4) - 1] + 1)
                        if u >= 2:
                            pe.wait_ge(S("a_scaled"), u - 1)
                        for t in range(i + 1):
                            last = mm(bank[5 + u % 2][:, 0:128], pT[:, u % 2, t, :], vtok[:, t, :],
                                      start=(t == 0), stop=(t == i))
                        last.then_inc(S("a_pv"), 1)

                    def turn_out(i):
                        pe.wait_ge(S("a_scaled"), 8 * i + 8)
                        if i:
                            pe.wait_ge(S("a_mix"), i)
                        for j in range(4):
                            last = nc.tensor.transpose(bank[7][:, 128 * j:128 * j + 128],
                                                       osb[:, i % 2, 128 * j:128 * j + 128], ident)
                        last.then_inc(S("a_oT"), 1)

                    units = [(i, h) for i in tiles_of(b) for h in range(HEADS)]
                    logits(*units[0])
                    for n, (i, h) in enumerate(units):
                        if n + 1 < len(units):
                            logits(*units[n + 1])
                        turn(i, h, slice(0, 2))
                        if n:
                            values(*units[n - 1])
                        turn(i, h, slice(2, None))
                        if n >= 2 and units[n - 2][1] == HEADS - 1:
                            turn_out(units[n - 2][0])
                    values(*units[-1])
                    turn_out(units[-1][0])
                if kind == "A" and b == NBLK:
                    pe.wait_ge(S("sa_qz"), 1)
                    pe.wait_ge(S("rep_in"), 32)
                    for s in range(DB):
                        pe.wait_ge(S(f"cache_in{s % 2}"), 16 * NPG * ((DB + s) // 2 + 1))
                        if s:
                            pe.wait_ge(S("sa_added"), s)
                        mm(bank[0][0:64, :], rep[0:64, s, :], sscore[:, 0:PAST], start=True, stop=False,
                           skip_group_check=True)
                        mm(bank[1][0:64, 0:NS], rep[0:64, s, :], sscore[:, PAST:LS], start=True, stop=False,
                           skip_group_check=True)
                        for g in range(KVH):
                            mm(bank[0][32 * g:32 * g + 32, :], qz[:, s, 32 * g:32 * g + 32],
                               cache[:, s % 2, :, 128 * g:128 * g + 128], start=False, stop=True,
                               skip_group_check=True)
                            last = mm(bank[1][32 * g:32 * g + 32, 0:NS], qz[:, s, 32 * g:32 * g + 32],
                                      kTs[:, g, :], start=False, stop=True, skip_group_check=True)
                        last.then_inc(S("sa_logits"), 1)
                        pe.wait_ge(S("sa_probs"), s + 1)
                        if s >= 2:
                            pe.wait_ge(S("sa_pTc"), s - 1)
                        for p in range(NPG):
                            nc.tensor.transpose(bank[2 + s % 2][:, 64 * p:64 * p + 64],
                                                slg[0:64, s % 2, 128 * p:128 * p + 128], ident[0:64, 0:64])
                        nc.tensor.transpose(bank[4 + s % 2][0:64, 0:64], slg[0:64, s % 2, PAST:LS],
                                            ident[0:64, 0:64]).then_inc(S("sa_pT"), 1)
                        pe.wait_ge(S("sa_pTc"), s + 1)
                        for g in range(KVH):
                            o = bank[6][0:64, s * 64 + 32 * g:s * 64 + 32 * g + 32]
                            for p in range(NPG):
                                mm(o, cache[:, s % 2, p, 384 + 64 * g:384 + 64 * g + 64],
                                   spT[:, s % 2, p, 32 * g:32 * g + 32], start=(p == 0), stop=False)
                            last = mm(o, vnew[:, 64 * g:64 * g + 64], spT[0:64, s % 2, 4, 32 * g:32 * g + 32],
                                      start=False, stop=True)
                        last.then_inc(S("sa_pv"), 1)
                if kind == "F":
                    par = b % 2
                    for dt in range(KT):
                        w = weights_at(base["O", b] + dt)
                        if dt >= 2:
                            pe.wait_ge(S("o_copied"), KT * b + dt - 1)
                        for k in range(KT):
                            x = [mixA[:, s, k, 0:NT] if k < 4 else mixG[:, par, s, k - 4, 0:NT] for s in range(2)]
                            last = three(bank[dt % 2][:, 0:NT], [w[s][:, 128 * k:128 * k + 128] for s in range(2)],
                                         x, k == 0, k == KT - 1)
                        last.then_inc(S("products"), 1)
                    pe.wait_ge(S("f_sq"), b + 1)
                    for k in range(KT):
                        last = mm(bank[2][:, 0:NT], ones, sq[:, k, 0:NT], start=(k == 0), stop=(k == KT - 1))
                    last.then_inc(S("f_ss"), 1)
                    pe.wait_ge(S("f_h"), b + 1)
                    u0 = 2 * NF * b
                    with pe.Fori(0, NF // 2) as i:
                        for r in range(4):
                            w = weights_at(base["U", b] + r, i, 4)
                            pe.wait_ge(S("u_bank_free"), i * 4 + (u0 + r + 1))
                            for k in range(KT):
                                last = three(bank[4 + r][:, 0:NT], [w[s][:, 128 * k:128 * k + 128] for s in range(2)],
                                             [H[:, s, k, 0:NT] for s in range(2)], k == 0, k == KT - 1)
                            last.then_inc(S("products"), 1)
                    pe.wait_ge(S("u_pair_free"), 2 + NF * (b + 1))
                    with pe.Fori(0, KT // 2) as i:
                        for r in range(2 * ND):
                            if r % ND == 0:
                                pe.wait_ge(S("d_bank_free"), i * 2 + (KT * b + r // ND + 1))
                            w = weights_at(base["D", b] + r, i, 2 * ND)
                            for c, k in enumerate(D_BLOCKS[r % ND]):
                                last = three(bank[r // ND][:, 0:NT], [w[s][:, 128 * c:128 * c + 128] for s in range(2)],
                                             [U[:, k, s, 0:NT] for s in range(2)], k == 0, k == NF - 1)
                            last.then_inc(S("products"), 1)
                    pe.wait_ge(S("y_sq"), b + 1)
                    for k in range(KT):
                        last = mm(bank[3][:, 0:NT], ones, sq[:, k, 0:NT], start=(k == 0), stop=(k == KT - 1))
                    last.then_inc(S("y_ss"), 1)
                pe.drain().then_inc(S("end_pe"), 1)

        @block.scalar
        def _(act):
            A = nc.scalar.activation

            def inverse_root(src, scale, e, ms, tmp, name):
                A(ms, src, ACT.Identity, scale=scale, bias=e)
                act.drain()
                A(tmp, ms, ACT.Ln)
                act.drain()
                A(tmp, tmp, ACT.Exp, scale=-0.5).then_inc(S(name), 1)

            def highs(n, low_by, i=None, step=0, cols=WT):
                act.wait_ge(S(f"weights_in{n % 2}"), value(16 * (n // 2 + 1), i, 8 * step))
                if n >= 4:
                    act.wait_ge(S("products"), value(n - 3, i, step))
                last = A(ring[:, n % 4, 0, 0:cols], raw[:, n % 2, 0:cols], ACT.Copy, scale=W_UP)
                if low_by == "pool":
                    last = A(raw[:, n % 2, 0:cols], raw[:, n % 2, 0:cols], ACT.Copy, scale=W_UP)
                last.then_inc(S("w_high"), 1)

            def highs_ahead(nph):
                tiles, low_by = first_tiles(nph)
                for n in tiles:
                    highs(n, low_by)

            for nph, (kind, b) in enumerate(SCHED):
                NT = ntok(b)
                t0 = TOK * b
                ntile = NT // 128 if b < NBLK else 1
                tw = min(NT, 128)
                phase_start(act, nph)
                stored_before(act, nph)
                if kind == "B":
                    act.wait_ge(S("consts_in"), 96)
                    act.sem_inc(S("u_bank_free"), 4)
                    act.sem_inc(S("d_bank_free"), 2)
                    act.sem_inc(S("u_pair_free"), 2)
                    act.sem_inc(S("d_buf_free"), 2)
                    highs_ahead(nph)
                if kind == "P":
                    act.wait_ge(S("x_in"), 16 * x_loads(nph))
                    A(sq[:, :, 0:NT], X[:, :, 0:NT], ACT.Square).then_inc(S("p_sq"), 1)
                    act.wait_ge(S("p_ss"), b + 1)
                    def gates_step(u):
                        if u == 3:
                            act.wait_ge(S("g_gate"), b + 1)
                            for j in range(2):
                                A(la[:, j, 0:NT], bank[5 + j][:, 0:NT], ACT.Identity, bias=gates[:, j:j + 1])
                            act.drain()
                            A(exa[:, :, 0:NT], la[:, :, 0:NT], ACT.Abs)
                            act.drain()
                            A(exb[:, :, 0:NT], exa[:, :, 0:NT], ACT.Exp, scale=-1.0)
                            act.drain()
                            A(exa[:, :, 0:NT], exb[:, :, 0:NT], ACT.Ln, bias=1.0).then_inc(S("g_lsig"), 1)
                        if u == 8:
                            act.wait_ge(S("g_var"), b + 1)
                            inverse_root(bank[7][:, 0:NT], 1.0 / 128, lneps, nG[0][:, 0:NT], nG[1][:, 0:NT], "g_ikr")
                        if u == 12:
                            act.wait_ge(S("g_cum"), b + 1)
                            A(la[:, :, 0:NT], cum[:, :, 0:NT], ACT.Exp, scale=1.0 / 16)
                            A(kg[:, :, 0:NT], exa[:, :, 0:NT], ACT.Exp, scale=-1.0 / 16)
                            A(kh[:, :, 0:NT], exb[:, :, 0:NT], ACT.Exp, scale=1.0 / 16)
                            act.drain()
                            A(exa[:, :, 0:NT], exa[:, :, 0:NT], ACT.Exp, scale=1.0 / 16).then_inc(S("g_ex"), 1)

                    inverse_root(bank[7][:, 0:NT], 1.0 / D, eps, nP[0][:, 0:NT], nP[1][:, 0:NT], "p_root")
                    for u, (what, j) in enumerate(P_UNITS):
                        t = min(u, len(TILES) - 1)
                        if b < NBLK and what in SPLIT:
                            highs(base["P", b] + t + 4, "dve")
                            gates_step(u)
                            continue
                        act.wait_ge(S("products"), base["P", b] + t + 1)
                        o = bank[4 if what == "iw" else u % 4]
                        of = o[:, 0:NT]
                        scale = 1.0 / (W_UP * H_UP)
                        if what == "iq":
                            dst, src = iqs[:, j, 0:NT], of
                        elif what == "ik":
                            dst, src = ikx[:, 0:NT], of
                        elif what == "k":
                            dst, src = kTs[:, j, :], of
                        elif what == "q":
                            dst, src, scale = qs[:, j, 0:NT], of, scale * HD ** -0.5
                        elif what == "gq":
                            dst, src, scale = gq[:, j, 0:NT], of, scale * DK ** -0.5
                        elif what == "gk":
                            dst, src = gk[:, j, 0:NT], of
                        elif what == "gr":
                            dst, src = gr[:, j, 0:NT], of
                        elif what == "glr":
                            dst, src = glr[0:RANK, 0:NT], o[0:RANK, 0:NT]
                        elif what == "v" and b < NBLK:
                            dst, src = vtok[:, 4 * b:4 * b + 4, :], o[:, :].rearrange("p (t c) -> p t c", c=128)
                        elif what == "v":
                            dst, src = vnew[:, :], o[0:NS, 0:128]
                        elif what == "gv":
                            dst = gv[0:tw, 0:ntile, 128 * j:128 * j + 128]
                            src = o[0:tw, 0:128 * ntile].rearrange("p (t c) -> p t c", c=128)
                        else:
                            dst = iw[0:tw, 0:ntile, :]
                            src = o[0:tw, 0:8 * ntile].rearrange("p (t c) -> p t c", c=8)
                            scale *= 8 ** -0.5 * 64 ** -0.5
                        A(dst, src, ACT.Copy, scale=scale).then_inc(S("p_copied"), 1)
                        if u + 4 < len(TILES):
                            highs(base["P", b] + u + 4, "dve")
                        gates_step(u)
                if kind == "G":
                    act.wait_ge(S("g_zeros"), b + 1)
                    if b < NBLK:
                        for t in range(4):
                            T = 4 * b + t
                            act.wait_ge(S("g_kt"), T + 1)
                            for c in range(2):
                                last = A(khz[64 * c:64 * c + 64, t, c, :], bank[t % 2][64 * c:64 * c + 64, 0:256], ACT.Copy)
                            last.then_inc(S("g_khz"), 1)
                            act.wait_ge(S("g_o"), 2 * T + 2)
                            A(oT[:, :, 128 * t:128 * t + 128],
                              bank[6 + t % 2][:, :].rearrange("p (h n) -> p h n", n=128), ACT.Copy).then_inc(S("g_oc"), 1)
                    else:
                        act.wait_ge(S("g_kt"), 4 * NBLK + 1)
                        A(khs[0:NS], bank[0][0:NS, 0:256], ACT.Copy).then_inc(S("g_khz"), 1)
                        act.wait_ge(S("g_o"), 8 * NBLK + 1)
                        A(oT[:, :, 0:NS], bank[6][:, 0:256].rearrange("p (h n) -> p h n", n=NS), ACT.Copy
                          ).then_inc(S("g_oc"), 1)
                    act.drain()
                    A(o2[:, :, 0:NT], oT[:, :, 0:NT], ACT.Square).then_inc(S("g_o2"), 1)
                    act.wait_ge(S("g_oss"), b + 1)
                    for h in range(GH):
                        A(o2[:, h, 0:NT], bank[h][:, 0:NT], ACT.Identity, scale=1.0 / DV, bias=eps)
                    act.drain()
                    A(qgz[:, :, 0:NT], o2[:, :, 0:NT], ACT.Ln)
                    act.drain()
                    A(qgz[:, :, 0:NT], qgz[:, :, 0:NT], ACT.Exp, scale=-0.5).then_inc(S("g_root"), 1)
                    A(gr[:, :, 0:NT], gr[:, :, 0:NT], ACT.Silu).then_inc(S("g_silu"), 1)
                if kind == "I" and b < NBLK:
                    for i in tiles_of(b):
                        if i < 2:
                            continue
                        for c, (k0, kn) in enumerate(score_chunks(i)):
                            for h in range(HEADS):
                                n = IN[i, c, h]
                                act.wait_ge(S("i_dots"), n + 1)
                                if n >= 4:
                                    act.wait_ge(S("i_added"), n - 3)
                                A(relu[:, n % 4, 0:kn], bank[n % 8][:, 0:kn], ACT.Relu,
                                  scale=1.0 / (I_UP * I_UP)).then_inc(S("i_relu"), 1)
                            if (i, c) == (4 * b, 0):
                                highs_ahead(nph)
                if kind == "I" and b == NBLK:
                    act.wait_ge(S("si_wt"), 1)
                    A(wsel[0:64], bank[0][0:64, :].rearrange("p (s t) -> p s t", t=64), ACT.Copy).then_inc(S("si_wsel"), 1)
                    for s in range(DB):
                        act.wait_ge(S("si_dots"), s + 1)
                        if s >= 2:
                            act.wait_ge(S("si_sum"), s - 1)
                        A(srelu[0:64, s % 2, 0:PAST], bank[2 + 2 * (s % 2)][0:64, :], ACT.Relu)
                        A(srelu[0:64, s % 2, PAST:LS], bank[3 + 2 * (s % 2)][0:64, 0:NS], ACT.Relu).then_inc(S("si_relu"), 1)
                    act.wait_ge(S("si_sum"), DB)
                    A(sscore[:, 0:PAST], bank[6][0:64, :], ACT.Copy).then_inc(S("si_copied"), 1)
                    highs_ahead(nph)
                if kind == "A" and b < NBLK:
                    def probs(i, h):
                        u = 8 * i + h
                        act.wait_ge(S("a_max"), u + 1)
                        if u >= 4:
                            act.wait_ge(S("a_scaled"), u - 3)
                        A(lg[:, u % 2, 0:128 * (i + 1)], lg[:, u % 2, 0:128 * (i + 1)], ACT.Exp,
                          bias=nmax[:, u % 2:u % 2 + 1], accum_out=den[:, u % 4:u % 4 + 1]).then_inc(S("a_exp"), 1)

                    def copy_pT(i, h, groups):
                        u = 8 * i + h
                        if u >= 2:
                            act.wait_ge(S("a_pv"), u - 1)
                        for g in range(-(-(i + 1) // 4))[groups]:
                            n = TN[i, h, g]
                            act.wait_ge(S("a_pT"), n + 1)
                            w = min(4, i + 1 - 4 * g)
                            A(pT[:, u % 2, 4 * g:4 * g + w, :],
                              bank[3 + n % 2][:, 0:128 * w].rearrange("p (t n) -> p t n", n=128),
                              ACT.Copy).then_inc(S("a_pTc"), 1)

                    def copy_mix(i):
                        act.wait_ge(S("a_oT"), i + 1)
                        if i:
                            act.wait_ge(S("a_mix_low"), i)
                        src = bank[7][:, :].rearrange("p (j n) -> p j n", n=128)
                        A(mix32, src, ACT.Copy, scale=M_UP)
                        A(mixA[:, 0, :, 128 * (i % 4):128 * (i % 4) + 128], src, ACT.Copy, scale=M_UP
                          ).then_inc(S("a_mix"), 1)

                    units = [(i, h) for i in tiles_of(b) for h in range(HEADS)]
                    probs(*units[0])
                    for n, (i, h) in enumerate(units):
                        copy_pT(i, h, slice(0, 2))
                        if n + 1 < len(units):
                            probs(*units[n + 1])
                        copy_pT(i, h, slice(2, None))
                        if n == 0:
                            highs_ahead(nph)
                        if n >= 2 and units[n - 2][1] == HEADS - 1:
                            copy_mix(units[n - 2][0])
                    copy_mix(units[-1][0])
                if kind == "A" and b == NBLK:
                    for s in range(DB):
                        act.wait_ge(S("sa_max"), s + 1)
                        if s >= 2:
                            act.wait_ge(S("sa_probs"), s - 1)
                        A(slg[0:64, s % 2, :], slg[0:64, s % 2, :], ACT.Exp, bias=nmax[0:64, s % 2:s % 2 + 1],
                          accum_out=den[0:64, s % 2:s % 2 + 1]).then_inc(S("sa_exp"), 1)
                        act.wait_ge(S("sa_pT"), s + 1)
                        if s >= 2:
                            act.wait_ge(S("sa_pv"), s - 1)
                        A(spT[:, s % 2, 0:NPG, :], bank[2 + s % 2][:, 0:256].rearrange("p (t n) -> p t n", n=64), ACT.Copy)
                        A(spT[0:64, s % 2, NPG, :], bank[4 + s % 2][0:64, 0:64], ACT.Copy).then_inc(S("sa_pTc"), 1)
                    highs_ahead(nph)
                if kind == "F":
                    for dt in range(KT):
                        n = KT * b + dt
                        act.wait_ge(S("products"), base["O", b] + dt + 1)
                        if dt >= 4:
                            act.wait_ge(S("o_added"), n - 3)
                        A(outev[:, dt % 4, 0:NT], bank[dt % 2][:, 0:NT], ACT.Copy, scale=1.0 / (W_UP * M_UP)
                          ).then_inc(S("o_copied"), 1)
                        highs(base["O", b] + dt + 4, lows_by(kind, b))
                    act.wait_ge(S("o_added"), KT * (b + 1))
                    A(sq[:, :, 0:NT], X[:, :, 0:NT], ACT.Square).then_inc(S("f_sq"), 1)
                    act.wait_ge(S("f_ss"), b + 1)
                    inverse_root(bank[2][:, 0:NT], 1.0 / D, eps, nF[0][:, 0:NT], nF[1][:, 0:NT], "f_root")
                    for k in range(KT):
                        A(hn[:, k, 0:NT], X[:, k, 0:NT], ACT.Copy, scale=gvec[:, KT + k:KT + k + 1]
                          ).then_inc(S("f_gained"), 1)
                    for k in range(KT):
                        act.wait_ge(S("f_scaled"), KT * b + k + 1)
                        A(H[:, 0, k, 0:NT], hn[:, k, 0:NT], ACT.Copy).then_inc(S("f_high"), 1)

                    def gate_and_up(c, i, ahead):
                        pairs = NF * b + (c - base["U", b]) // 2
                        for r in range(4):
                            if r % 2 == 0:
                                act.wait_ge(S("u_pair_free"), value(pairs + r // 2 + 1, i, 2))
                            act.wait_ge(S("products"), value(c + r + 1, i, 4))
                            func, up = (ACT.Silu, 1.0) if r % 2 == 0 else (ACT.Copy, U_UP)
                            A(ffev[:, r, 0:NT], bank[4 + r][:, 0:NT], func, scale=up / (W_UP * H_UP)
                              ).then_inc(S("u_bank_free"), 1)
                            highs(c + r + 4, lows_by(kind, b), i, 4, 128 * len(D_BLOCKS[r]) if ahead == "D" else WT)

                    with act.Fori(0, NF // 2 - 1) as i:
                        gate_and_up(base["U", b], i, "U")
                    gate_and_up(base["D", b] - 4, None, "D")

                    def down(c, i, ahead):
                        outs = KT * b + (c - base["D", b]) // ND
                        for r in range(2 * ND):
                            if r < ahead:
                                highs(c + r + 4, lows_by(kind, b), i, 2 * ND, 128 * len(D_BLOCKS[r % ND]))
                            if r % ND == ND - 1:
                                dt = r // ND
                                act.wait_ge(S("d_buf_free"), value(outs + dt + 1, i, 2))
                                act.wait_ge(S("products"), value(c + r + 1, i, 2 * ND))
                                A(ffev[:, dt, 0:NT], bank[dt][:, 0:NT], ACT.Copy, scale=1.0 / (W_UP * U_UP)
                                  ).then_inc(S("d_bank_free"), 1)

                    with act.Fori(0, KT // 2 - 1) as i:
                        down(base["D", b], i, 2 * ND)
                    down(base["D", b] + ND * (KT - 2), None, ND)
                    act.wait_ge(S("d_buf_free"), 2 + KT * (b + 1))
                    A(sq[:, :, 0:NT], X[:, :, 0:NT], ACT.Square).then_inc(S("y_sq"), 1)
                    act.wait_ge(S("y_ss"), b + 1)
                    inverse_root(bank[3][:, 0:NT], 1.0 / D, eps, nF[0][:, 0:NT], nF[1][:, 0:NT], "y_root")
                    for k in range(KT):
                        act.wait_ge(S("y_scaled"), KT * b + k + 1)
                        last = A(H32[:, k, 0:NT], X[:, k, 0:NT], ACT.Copy, scale=gvec[:, 2 * KT + k:2 * KT + k + 1])
                    last.then_inc(S("f_y"), 1)
                act.drain().then_inc(S("end_act"), 1)

        @block.vector
        def _(dve):
            v = nc.vector

            def newton(ms, r, tmp, out, up=1.0):
                v.tensor_tensor(tmp, r, r, ALU.mult)
                dve.drain()
                v.tensor_tensor(tmp, tmp, ms, ALU.mult)
                dve.drain()
                v.tensor_scalar(tmp, tmp, -0.5 * up, 1.5 * up, ALU.mult, ALU.add)
                dve.drain()
                v.tensor_tensor(out, tmp, r, ALU.mult)
                dve.drain()

            def lows(n, i=None, step=0, cols=WT):
                dve.wait_ge(S("w_high"), value(n + 1, i, step))
                v.scalar_tensor_tensor(ring[:, n % 4, 1, 0:cols], raw[:, n % 2, 0:cols], W_UP,
                                       ring[:, n % 4, 0, 0:cols], ALU.mult, ALU.subtract).then_inc(S("w_split"), 1)

            def lows_ahead(nph):
                tiles, low_by = first_tiles(nph)
                for n in tiles:
                    if low_by == "dve":
                        lows(n)

            def pick_round(rows, view):
                v.max(top8[rows, :], view)
                dve.drain()
                v.match_replace(view, top8[rows, :], view, TAKEN)
                dve.drain()

            def picked(view):
                v.tensor_scalar(view, view, TAKEN_CUT, OUTSIDE, ALU.is_ge, ALU.mult)

            def pick(rows, view, k):
                with dve.Fori(0, k // 8):
                    pick_round(rows, view)
                picked(view)

            LATE = {0: (2, 3), NBLK - 1: (4 * NBLK - 1,)}

            def row_of(i):
                return Sf[:, score_at(i):score_at(i) + 128 * (i + 1)]

            def pick_block(b):
                if b < NBLK:
                    for i in tiles_of(b):
                        if i >= 2 and i not in LATE.get(b, ()):
                            pick(slice(0, 128), row_of(i), TOPK)
                else:
                    pick(slice(0, 64), sscore, TOPK_S + 6)

            def late_picks(b):
                plan, rounds = {}, TOPK // 8
                start = 0
                for i in LATE.get(b, ()):
                    units = range(start, HEADS * (i - 4 * b) - 1)
                    for n, u in enumerate(units):
                        plan.setdefault(u, []).append(
                            (i, rounds * (n + 1) // len(units) - rounds * n // len(units)))
                    start = units[-1] + 1
                return plan

            for nph, (kind, b) in enumerate(SCHED):
                NT = ntok(b)
                t0 = TOK * b
                phase_start(dve, nph)
                stored_before(dve, nph)
                if kind == "B":
                    dve.wait_ge(S("consts_in"), 96)
                    v.memset(state[:, :, :], 0.0)
                    v.tensor_copy(relw[0:RB], relb[0:RB].unsqueeze(2).broadcast_to([RB, HEADS, 128])).then_inc(S("bias_wide"), 1)
                    for h in range(HEADS):
                        dve.wait_ge(S("bias_mm"), h + 1)
                        k = 3 * (h % 2)
                        v.tensor_scalar(row1[:, h, :], bank[k][:, 0:W1], Q_SCALE, None, ALU.mult)
                        v.tensor_copy(row2[:, h, 0:512], bank[k + 1][:, :])
                        v.tensor_copy(row2[:, h, 512:W2], bank[k + 2][:, 0:W2 - 512]).then_inc(S("bias_copied"), 1)
                    dve.drain().then_inc(S("bias_rows"), 1)
                    dve.wait_ge(S("skew_dma"), 48)
                    lows_ahead(nph)
                if kind == "P":
                    dve.wait_ge(S("p_root"), b + 1)
                    newton(nP[0][:, 0:NT], nP[1][:, 0:NT], nP[2][:, 0:NT], nP[3][:, 0:NT], H_UP)
                    for k in range(KT):
                        v.scalar_tensor_tensor(hn[:, k, 0:NT], X[:, k, 0:NT], gvec[:, k:k + 1],
                                               nP[3][:, 0:NT], ALU.mult, ALU.mult)
                        dve.drain()
                        v.tensor_copy(H[:, 0, k, 0:NT], hn[:, k, 0:NT])
                        dve.drain()
                        v.tensor_tensor(H[:, 1, k, 0:NT], hn[:, k, 0:NT], H[:, 0, k, 0:NT], ALU.subtract
                                        ).then_inc(S("p_h"), 1)
                    C = CH if b < NBLK else TS
                    nc_ = NT // C

                    def gates_step(u):
                        if u == 5:
                            dve.wait_ge(S("g_mean"), b + 1)
                            v.scalar_tensor_tensor(ikc[:, 0:NT], bank[7][:, 0:NT], -1.0 / 128, ikx[:, 0:NT], ALU.mult, ALU.add)
                            dve.drain()
                            v.tensor_tensor(ikx[:, 0:NT], ikc[:, 0:NT], ikc[:, 0:NT], ALU.mult).then_inc(S("g_ikc"), 1)
                            dve.wait_ge(S("g_lsig"), b + 1)
                            v.scalar_tensor_tensor(la[:, :, 0:NT], la[:, :, 0:NT], 0.0, exa[:, :, 0:NT], ALU.min, ALU.subtract)
                            dve.wait_ge(S("g_rst"), b + 1)
                            dve.drain()
                            for j in range(2):
                                v.tensor_tensor_scan(cum[:, j, 0:NT], rst[:, 0:NT], la[:, j, 0:NT], 0.0, ALU.mult, ALU.add)
                            dve.drain()
                            for j in range(2):
                                def chunks(t):
                                    return t[:, j, 0:NT].rearrange("p (n c) -> p n c", c=C)
                                mid = chunks(cum)[:, :, C // 2 - 1:C // 2].broadcast_to([128, nc_, C])
                                end = chunks(cum)[:, :, C - 1:C].broadcast_to([128, nc_, C])
                                v.tensor_tensor(chunks(exa), chunks(cum), mid, ALU.subtract)
                                v.tensor_tensor(chunks(exb), end, chunks(cum), ALU.subtract)
                        if u == 9:
                            dve.wait_ge(S("g_ikr"), b + 1)
                            newton(nG[0][:, 0:NT], nG[1][:, 0:NT], nG[2][:, 0:NT], nG[3][:, 0:NT])
                            v.tensor_tensor(ikc[:, 0:NT], ikc[:, 0:NT], nG[3][:, 0:NT], ALU.mult)
                            dve.drain()
                            ik = ik32 if b < NBLK else ikTs[:, :]
                            v.tensor_scalar(ik, ikc[:, 0:NT], gates[:, 3:4], gates[:, 4:5], ALU.mult, ALU.add)
                            if b < NBLK:
                                dve.drain()
                                v.tensor_scalar(ikT[:, 0, t0:t0 + TOK], ik, I_UP, None, ALU.mult)
                                dve.drain()
                                v.scalar_tensor_tensor(ikT[:, 1, t0:t0 + TOK], ik, I_UP, ikT[:, 0, t0:t0 + TOK],
                                                       ALU.mult, ALU.subtract)
                            dve.drain().then_inc(S("g_cum"), 1)
                        if u == 14:
                            dve.wait_ge(S("g_ex"), b + 1)
                            dve.wait_ge(S("g_zero"), b + 1)
                            for e in range(2):
                                p = slice(64 * e, 64 * e + 64)
                                v.tensor_tensor(qgz[p, e::2, 0:NT], gq[p, :, 0:NT], exa[p, :, 0:NT], ALU.mult)
                                last = v.tensor_tensor(qiz[p, e::2, 0:NT], gq[p, :, 0:NT], la[p, :, 0:NT], ALU.mult)
                            last.then_inc(S("g_q"), 1)

                    back = 1.0 / (W_UP * H_UP)
                    for u, (what, j) in enumerate(TILES):
                        if b < NBLK and what in SPLIT:
                            dve.wait_ge(S("products"), base["P", b] + u + 1)
                            o = bank[u % 4]
                            if what == "k":
                                v.tensor_scalar(k32[:, j, :], o[:, :], back, None, ALU.mult)
                                v.tensor_scalar(kT[:, j, 0, t0:t0 + TOK], o[:, :], K_UP * back, None, ALU.mult)
                                dve.drain()
                                v.scalar_tensor_tensor(kT[:, j, 1, t0:t0 + TOK], o[:, :], K_UP * back,
                                                       kT[:, j, 0, t0:t0 + TOK], ALU.mult, ALU.subtract
                                                       ).then_inc(S("p_split"), 1)
                            else:
                                to, up = (iq, I_UP * back) if what == "iq" else (q, Q_UP * back)
                                for e in range(2):
                                    hi, lo = halves(e)
                                    v.tensor_scalar(to[hi, 2 * j + e, :], o[hi, :], up, None, ALU.mult)
                                dve.drain()
                                for e in range(2):
                                    hi, lo = halves(e)
                                    last = v.scalar_tensor_tensor(to[lo, 2 * j + e, :], o[hi, :], up,
                                                                  to[hi, 2 * j + e, :], ALU.mult, ALU.subtract)
                                last.then_inc(S("p_split"), 1)
                        if u + 4 < len(TILES):
                            lows(base["P", b] + u + 4)
                        gates_step(u)
                if kind == "G":
                    dve.wait_ge(S("g_zeros"), b + 1)
                    if b < NBLK:
                        for t in range(4):
                            T = 4 * b + t
                            dve.wait_ge(S("g_at"), T + 1)
                            if t >= 2:
                                dve.wait_ge(S("g_o"), 2 * T - 3)
                            for c in range(2):
                                p = slice(64 * c, 64 * c + 64)
                                last = v.tensor_tensor(
                                    att[p, t % 2, :, 64 * c:64 * c + 64],
                                    bank[2 + t % 2][p, 0:256].rearrange("p (h n) -> p h n", n=64),
                                    cst[p, C_TRI:C_TRI + 64].unsqueeze(1).broadcast_to([64, GH, 64]), ALU.mult)
                            last.then_inc(S("g_atm"), 1)
                            for c in range(2):
                                dve.wait_ge(S("g_o"), 2 * T + c + 1)
                                at = 128 * t + CH * c + CH - 1
                                for e in range(2):
                                    for j in range(2):
                                        p = slice(64 * e, 64 * e + 64)
                                        last = v.scalar_tensor_tensor(
                                            state[p, j, :], state[p, j, :], la[p, j, at:at + 1],
                                            bank[4 + c][p, j * 256 + e * 128:j * 256 + e * 128 + 128],
                                            ALU.mult, ALU.add)
                                last.then_inc(S("g_state"), 1)
                                dve.drain()
                    else:
                        dve.wait_ge(S("g_at"), 4 * NBLK + 1)
                        v.tensor_tensor(atts[0:NS], bank[2][0:NS, 0:256].rearrange("p (h n) -> p h n", n=64),
                                        cst[0:NS, C_TRI8:C_TRI8 + 64].unsqueeze(1).broadcast_to([NS, GH, 64]),
                                        ALU.mult).then_inc(S("g_atm"), 1)
                        dve.wait_ge(S("g_o"), 8 * NBLK + 1)
                        for s in range(DB):
                            dve.wait_ge(S("gs_u"), s + 1)
                            at = TS * s + TS - 1
                            for e in range(2):
                                for j in range(2):
                                    p = slice(64 * e, 64 * e + 64)
                                    last = v.scalar_tensor_tensor(
                                        sin[p, s, j, :], sin[p, s, j, :], la[p, j, at:at + 1],
                                        bank[4 + s % 2][p, j * 256 + e * 128:j * 256 + e * 128 + 128],
                                        ALU.mult, ALU.add)
                            last.then_inc(S("gs_new"), 1)
                    dve.wait_ge(S("g_root"), b + 1)
                    newton(o2[:, :, 0:NT], qgz[:, :, 0:NT], qiz[:, :, 0:NT], qgz[:, :, 0:NT])
                    v.tensor_tensor(oT[:, :, 0:NT], oT[:, :, 0:NT], qgz[:, :, 0:NT], ALU.mult)
                    dve.drain()
                    dve.wait_ge(S("g_silu"), b + 1)
                    v.scalar_tensor_tensor(oT[:, :, 0:NT], oT[:, :, 0:NT], gates[:, 2:3],
                                           gr[:, :, 0:NT], ALU.mult, ALU.mult)
                    dve.drain()
                    v.tensor_scalar(mixG[:, b % 2, 0, :, 0:NT], oT[:, :, 0:NT], M_UP, None, ALU.mult)
                    dve.drain()
                    v.scalar_tensor_tensor(mixG[:, b % 2, 1, :, 0:NT], oT[:, :, 0:NT], M_UP,
                                           mixG[:, b % 2, 0, :, 0:NT], ALU.mult, ALU.subtract)
                if kind == "I" and b < NBLK:
                    for i in tiles_of(b):
                        if i < 2:
                            continue
                        row_at = score_at(i)
                        for c, (k0, kn) in enumerate(score_chunks(i)):
                            out = Sf[:, row_at + k0:row_at + k0 + kn]
                            for h in range(HEADS):
                                n = IN[i, c, h]
                                w = iw[:, i % 4, h:h + 1]
                                dve.wait_ge(S("i_relu"), n + 1)
                                if h == 0:
                                    v.tensor_scalar(out, relu[:, n % 4, 0:kn], w, None, ALU.mult).then_inc(S("i_added"), 1)
                                else:
                                    v.scalar_tensor_tensor(out, relu[:, n % 4, 0:kn], w, out, ALU.mult, ALU.add
                                                           ).then_inc(S("i_added"), 1)
                                dve.drain()
                if kind == "I" and b == NBLK:
                    dve.wait_ge(S("si_zero"), 1)
                    for h in range(HEADS):
                        e, j = h % 2, h // 2
                        p = slice(64 * e, 64 * e + 64)
                        last = v.tensor_copy(iqz[p, :, 8 * h:8 * h + 8], iqs[p, j, 0:NS].rearrange("p (s t) -> p s t", t=TS))
                    last.then_inc(S("si_iqz"), 1)
                    dve.wait_ge(S("rep_in"), 16)
                    for h in range(HEADS):
                        last = v.tensor_scalar(wrow[0:64, :, 8 * h:8 * h + 8], rep[0:64, :, 8 * h:8 * h + 8],
                                               iw[0:64, 0, h:h + 1], None, ALU.mult)
                    last.then_inc(S("si_wrow"), 1)
                    dve.wait_ge(S("si_sum"), DB)
                    v.tensor_tensor(sscore[:, PAST:LS], bank[7][0:64, 0:NS], cst[0:64, C_SEQ:C_SEQ + 64], ALU.add)
                if kind == "T":
                    pick_block(0)
                if kind == "F" and b < NBLK:
                    pick_block(b + 1)
                if kind == "A" and b < NBLK:
                    def mask(i, h):
                        u = 8 * i + h
                        if u >= 2:
                            pi, ph = (u - 2) // 8, (u - 2) % 8
                            dve.wait_ge(S("a_pT"), TN[pi, ph, -(-(pi + 1) // 4) - 1] + 1)
                            dve.wait_ge(S("a_exp"), u - 1)
                        cs = near_chunks(i)
                        for c, (k0, kn, near) in enumerate(cs):
                            n = QN[i, h, c]
                            dve.wait_ge(S("a_logits"), n + 1)
                            if near:
                                dve.wait_ge(S("a_near"), u + 1)
                                m = nearm[:, u % 2, 0:kn]
                            else:
                                at = score_at(i) + k0
                                m = Sf[:, at:at + kn]
                            v.tensor_tensor_reduce(lg[:, u % 2, k0:k0 + kn], bank[n % 3][:, 0:kn], m, 1.0 / Q_SCALE, OUTSIDE,
                                                   ALU.add, ALU.max, mx[:, u % 2, c:c + 1]).then_inc(S("a_masked"), 1)
                        dve.drain()
                        v.tensor_reduce(nmax[:, u % 2:u % 2 + 1], mx[:, u % 2, 0:len(cs)], AX.X, ALU.max,
                                        negate=True).then_inc(S("a_max"), 1)

                    def scale(i, h):
                        u = 8 * i + h
                        dve.wait_ge(S("a_pv"), u + 1)
                        v.reciprocal(rden[:, u % 4:u % 4 + 1], den[:, u % 4:u % 4 + 1])
                        if h == 0 and i >= 2:
                            dve.wait_ge(S("a_oT"), i - 1)
                        dve.drain()
                        v.tensor_scalar(osb[:, i % 2, 64 * h:64 * h + 64], bank[5 + u % 2][:, 64 * (h // 4):64 * (h // 4) + 64],
                                        rden[:, u % 4:u % 4 + 1], None, ALU.mult).then_inc(S("a_scaled"), 1)

                    plan = late_picks(b)
                    units = [(i, h) for i in tiles_of(b) for h in range(HEADS)]
                    mask(*units[0])
                    for n in range(len(units)):
                        if n + 1 < len(units):
                            mask(*units[n + 1])
                        if n == 0:
                            lows_ahead(nph)
                        for i, rounds in plan.get(n, ()):
                            for _ in range(rounds):
                                pick_round(slice(0, 128), row_of(i))
                            if n == HEADS * (i - 4 * b) - 2:
                                picked(row_of(i))
                                dve.drain().then_inc(S("late_picked"), 1)
                        if n >= 2:
                            scale(*units[n - 2])
                    scale(*units[-2])
                    scale(*units[-1])
                if kind == "A" and b == NBLK:
                    dve.wait_ge(S("sa_zero"), 1)
                    for h in range(HEADS):
                        e, j = h % 2, h // 2
                        p = slice(64 * e, 64 * e + 64)
                        last = v.tensor_copy(qz[p, :, 8 * h:8 * h + 8], qs[p, j, 0:NS].rearrange("p (s t) -> p s t", t=TS))
                    last.then_inc(S("sa_qz"), 1)
                    for s in range(DB):
                        dve.wait_ge(S("sa_logits"), s + 1)
                        if s >= 2:
                            dve.wait_ge(S("sa_pT"), s - 1)
                        if s == 0:
                            dve.wait_ge(S("sbias_in"), 16 * HEADS)
                        out = slg[0:64, s % 2, :]
                        v.tensor_tensor(out[:, 0:PAST], bank[0][0:64, :], sbias[:, 0:PAST], ALU.add)
                        v.tensor_tensor(out[:, PAST:LS].rearrange("p (s t) -> p s t", t=TS),
                                        bank[1][0:64, 0:NS].rearrange("p (s t) -> p s t", t=TS),
                                        sbias[:, PAST:PAST + TS].unsqueeze(1).broadcast_to([64, DB, TS]),
                                        ALU.add).then_inc(S("sa_added"), 1)
                        dve.drain()
                        v.tensor_reduce(nmax[0:64, s % 2:s % 2 + 1], out, AX.X, ALU.max, negate=True).then_inc(S("sa_max"), 1)
                        dve.wait_ge(S("sa_exp"), s + 1)
                        v.reciprocal(rden[0:64, s % 2:s % 2 + 1], den[0:64, s % 2:s % 2 + 1])
                        dve.drain()
                        v.tensor_scalar(out, out, rden[0:64, s % 2:s % 2 + 1], None, ALU.mult).then_inc(S("sa_probs"), 1)
                    lows_ahead(nph)
                    dve.wait_ge(S("sa_pv"), DB)
                    for h in range(HEADS):
                        e, j = h % 2, h // 2
                        src = bank[6][0:64, :].rearrange("p (s m) -> p s m", m=64)[:, :, 8 * h:8 * h + 8]
                        to = [mixA[64 * e:64 * e + 64, half, j, 0:NS].rearrange("p (s t) -> p s t", t=TS)
                              for half in range(2)]
                        v.tensor_scalar(to[0], src, M_UP, None, ALU.mult)
                        dve.drain()
                        v.scalar_tensor_tensor(to[1], src, M_UP, to[0], ALU.mult, ALU.subtract)
                if kind == "F" and b == NBLK:
                    for t in range(4, KT + 4):
                        lows(base["O", b] + t)
                    with dve.Fori(0, NF // 2 - 1) as i:
                        for r in range(4):
                            lows(base["U", b] + 4 + r, i, 4)
                    for r in range(ND):
                        lows(base["D", b] + r, cols=128 * len(D_BLOCKS[r]))
                    with dve.Fori(0, KT - 1) as i:
                        for r in range(ND):
                            lows(base["D", b] + ND + r, i, ND, 128 * len(D_BLOCKS[r]))
                dve.drain().then_inc(S("end_dve"), 1)

        @block.gpsimd
        def _(pool):
            g = nc.gpsimd

            def newton(ms, r, tmp, out, up=1.0):
                g.tensor_tensor(tmp, r, r, ALU.mult)
                pool.drain()
                g.tensor_tensor(tmp, tmp, ms, ALU.mult)
                pool.drain()
                g.tensor_scalar(tmp, tmp, -0.5 * up, 1.5 * up, ALU.mult, ALU.add)
                pool.drain()
                g.tensor_tensor(out, tmp, r, ALU.mult)
                pool.drain()

            def lows(n, i=None, step=0, cols=WT):
                pool.wait_ge(S("w_high"), value(n + 1, i, step))
                g.tensor_tensor(ring[:, n % 4, 1, 0:cols], raw[:, n % 2, 0:cols], ring[:, n % 4, 0, 0:cols],
                                ALU.subtract).then_inc(S("w_split"), 1)

            for nph, (kind, b) in enumerate(SCHED):
                NT = ntok(b)
                phase_start(pool, nph)
                stored_before(pool, nph)
                if kind == "B":
                    pool.wait_ge(S("consts_in"), 96)
                if kind == "P":
                    g.memset(rst[:, 0:NT], 1.0)
                    pool.drain()
                    g.memset(rst[:, 0:NT].rearrange("p (n c) -> p n c", c=CH if b < NBLK else TS)[:, :, 0:1], 0.0)
                    pool.drain().then_inc(S("g_rst"), 1)
                    g.memset(qgz[:, :, 0:NT], 0.0)
                    g.memset(qiz[:, :, 0:NT], 0.0)
                    pool.drain().then_inc(S("g_zero"), 1)
                    pool.wait_ge(S("g_ex"), b + 1)
                    g.tensor_tensor(kg[:, :, 0:NT], gk[:, :, 0:NT], kg[:, :, 0:NT], ALU.mult)
                    g.tensor_tensor(kh[:, :, 0:NT], gk[:, :, 0:NT], kh[:, :, 0:NT], ALU.mult)
                    pool.drain().then_inc(S("g_k"), 1)
                if kind == "G":
                    if b < NBLK:
                        g.memset(khz, 0.0)
                        g.memset(att, 0.0)
                    pool.drain().then_inc(S("g_zeros"), 1)
                    if b == NBLK:
                        for s in range(DB):
                            if s >= 2:
                                pool.wait_ge(S("gs_u"), s - 1)
                            g.tensor_scalar(gvz[0:NS, s % 2, :], gv[0:NS, 0, :], cst[0:NS, C_ROW + s:C_ROW + s + 1],
                                            None, ALU.mult).then_inc(S("gs_gvz"), 1)
                if kind == "I" and b == 0:
                    for i in range(2):
                        g.memset(Sf[:, score_at(i):score_at(i) + 128 * (i + 1)], 0.0)
                    pool.drain()
                if kind == "I" and b == NBLK:
                    g.memset(iqz, 0.0).then_inc(S("si_zero"), 1)
                    g.memset(sscore[:, LS:LS + 6], 3e38)
                tiles, low_by = first_tiles(nph)
                if low_by == "pool":
                    for n in tiles:
                        lows(n)
                if kind == "I" and b < NBLK:
                    for i in tiles_of(b):
                        if i >= 2:
                            pool.wait_ge(S("i_added"), IN[i, len(score_chunks(i)) - 1, HEADS - 1] + 1)
                        at = score_at(i) + 128 * i
                        diag = Sf[:, at:at + 128]
                        g.affine_select(out=diag, in_=diag, compare_op=ALU.is_ge, fill=OUTSIDE, base=0,
                                        pattern=[[-1, 128]], channel_multiplier=1)
                if kind == "A" and b < NBLK:
                    def mix_low(i):
                        cols = slice(128 * (i % 4), 128 * (i % 4) + 128)
                        pool.wait_ge(S("a_mix"), i + 1)
                        g.tensor_tensor(mixA[:, 1, :, cols], mix32, mixA[:, 0, :, cols], ALU.subtract
                                        ).then_inc(S("a_mix_low"), 1)

                    for i in tiles_of(b):
                        if b == 0 and i >= 2 or i == 4 * NBLK - 1:
                            pool.wait_ge(S("late_picked"), i - 1 if b == 0 else 3)
                        k0, kn, _near = near_chunks(i)[-1]
                        at = score_at(i) + k0
                        for h in range(HEADS):
                            u = 8 * i + h
                            if u >= 2:
                                pool.wait_ge(S("a_max"), u - 1)
                            g.tensor_tensor(nearm[:, u % 2, 0:kn], Sf[:, at:at + kn],
                                            near_bias[:, h, 256 - kn:256], ALU.add).then_inc(S("a_near"), 1)
                            if h == HEADS // 2 and i > 4 * b:
                                mix_low(i - 1)
                    mix_low(4 * b + 3)
                if kind == "A" and b == NBLK:
                    g.memset(qz, 0.0).then_inc(S("sa_zero"), 1)
                if kind == "F":
                    pool.wait_ge(S("x_in"), 16 * x_loads(nph))
                    by_pool = lows_by(kind, b) == "pool"
                    for dt in range(KT):
                        pool.wait_ge(S("o_copied"), KT * b + dt + 1)
                        g.tensor_tensor(X[:, dt, 0:NT], X[:, dt, 0:NT], outev[:, dt % 4, 0:NT], ALU.add
                                        ).then_inc(S("o_added"), 1)
                        if by_pool:
                            lows(base["O", b] + dt + 4)
                    pool.wait_ge(S("f_root"), b + 1)
                    newton(nF[0][:, 0:NT], nF[1][:, 0:NT], nF[2][:, 0:NT], nF[3][:, 0:NT], H_UP)
                    for k in range(KT):
                        pool.wait_ge(S("f_gained"), KT * b + k + 1)
                        g.tensor_tensor(hn[:, k, 0:NT], hn[:, k, 0:NT], nF[3][:, 0:NT], ALU.mult
                                        ).then_inc(S("f_scaled"), 1)
                    for k in range(KT):
                        pool.wait_ge(S("f_high"), KT * b + k + 1)
                        last = g.tensor_tensor(H[:, 1, k, 0:NT], hn[:, k, 0:NT], H[:, 0, k, 0:NT], ALU.subtract)
                    last.then_inc(S("f_h"), 1)

                    def gated(c, i, ahead):
                        rows = (c - base["U", b]) // 2
                        for s in range(2):
                            if by_pool:
                                lows(c + 2 * s + 4, i, 4, 128 * len(D_BLOCKS[2 * s]) if ahead == "D" else WT)
                            pool.wait_ge(S("u_bank_free"), value(4 + 2 * NF * b + 2 * (rows + s) + 2, i, 4))
                            pool.sem_inc(S("pool_ticks"), 1)
                            gate, up = ffev[:, 2 * s, 0:NT], ffev[:, 2 * s + 1, 0:NT]
                            if i is None:
                                hi, lo = (U[:, rows + s, half, 0:NT] for half in range(2))
                            else:
                                hi, lo = (U[:, bass.ds(i * 2 + s, 1), half, 0:NT].rearrange("p a n -> p (a n)")
                                          for half in range(2))
                            g.tensor_tensor(hi, gate, up, ALU.mult)
                            pool.drain()
                            g.tensor_tensor(gate, gate, up, ALU.mult)
                            pool.drain()
                            g.tensor_tensor(lo, gate, hi, ALU.subtract).then_inc(S("u_pair_free"), 1)
                            if by_pool:
                                lows(c + 2 * s + 5, i, 4, 128 * len(D_BLOCKS[2 * s + 1]) if ahead == "D" else WT)

                    with pool.Fori(0, NF // 2 - 1) as i:
                        gated(base["U", b], i, "U")
                    gated(base["D", b] - 4, None, "D")

                    def added(c, i, ahead):
                        outs = (c - base["D", b]) // ND
                        for r in range(2 * ND):
                            if by_pool and r < ahead:
                                lows(c + r + 4, i, 2 * ND, 128 * len(D_BLOCKS[r % ND]))
                            if r % ND == ND - 1:
                                dt = r // ND
                                pool.wait_ge(S("d_bank_free"), value(2 + KT * b + outs + dt + 1, i, 2))
                                pool.sem_inc(S("pool_ticks"), 1)
                                x = (X[:, outs + dt, 0:NT] if i is None else
                                     X[:, bass.ds(i * 2 + dt, 1), 0:NT].rearrange("p a n -> p (a n)"))
                                g.tensor_tensor(x, x, ffev[:, dt, 0:NT], ALU.add).then_inc(S("d_buf_free"), 1)

                    with pool.Fori(0, KT // 2 - 1) as i:
                        added(base["D", b], i, 2 * ND)
                    added(base["D", b] + ND * (KT - 2), None, ND)
                    pool.wait_ge(S("y_root"), b + 1)
                    newton(nF[0][:, 0:NT], nF[1][:, 0:NT], nF[2][:, 0:NT], nF[3][:, 0:NT])
                    for k in range(KT):
                        g.tensor_tensor(X[:, k, 0:NT], X[:, k, 0:NT], nF[3][:, 0:NT], ALU.mult).then_inc(S("y_scaled"), 1)
                pool.drain().then_inc(S("end_pool"), 1)


def outputs_of():
    return {
        "o_y": (128, KT, ALLT), "o_k": (64, KVH, ALLT), "o_v": (ALLT, KVH * HD), "o_ik": (64, ALLT),
        "o_gp": (128, 2, DV), "o_gs": (128, DB, 2, DV),
    }


def laid_out(i):
    def tiles(w, cols):
        return w.reshape(KT, 128, cols).transpose(1, 0, 2).reshape(128, KT * cols)

    w = np.asarray(i["w_in"])[0]
    at = dict(q=0, k=512, v=640, iq=768, ik=1280, iw=1344, gq=1352, gk=1608, gv=1864, gr=2376, glr=2888)
    parts = []
    for what, j in TILES:
        if what == "k":
            c = w[:, at["k"] + 64 * j:at["k"] + 64 * j + 64]
            c = np.concatenate([c, c], 1)
        elif what == "ik":
            c = w[:, at["ik"]:at["ik"] + 64]
            c = np.concatenate([c, c], 1)
        elif what == "glr":
            c = np.concatenate([w[:, at["glr"]:at["glr"] + RANK], w[:, at["iw"]:at["iw"] + 8],
                                np.zeros((D, 128 - RANK - 8), w.dtype)], 1)
        else:
            c = w[:, at[what] + 128 * j:at[what] + 128 * j + 128]
        parts.append(tiles(c, 128))
    wo, wg, wu, wd = (np.asarray(i[n])[0] for n in ("w_out", "w_gate", "w_up", "w_down"))
    x = np.concatenate([np.asarray(i["x_prompt"])[0], np.asarray(i["x_sample"]).reshape(NS, D)], 0)
    ck, cv, ci = (np.asarray(i[n])[0] for n in ("cache_k", "cache_v", "cache_idx_k"))
    kt = ck.transpose(0, 3, 2, 1)
    kt = np.concatenate([kt, kt], 1).reshape(NPOOL, 128, 256)
    it = ci.transpose(0, 2, 1)
    cache = np.concatenate([kt, np.concatenate([it, it], 1), cv.reshape(NPOOL, 128, 128)], 2)
    cst, rep, hots = constants()

    def col(v):
        return np.asarray(v).reshape(-1, 128).T

    kn = [np.concatenate([np.asarray(i[n])[0]] * 2) for n in ("idx_knorm_g", "idx_knorm_b")]
    out = {
        "xT": x.T.reshape(KT, 128, ALLT).transpose(1, 0, 2),
        "w_in": np.stack(parts),
        "w_out": np.stack([tiles(wo[:, 128 * t:128 * t + 128], 128) for t in range(KT)]),
        "w_gu": np.stack([np.concatenate([tiles(m[:, 128 * f:128 * f + 128], 128) for m in (wg, wu)], 1)
                          for f in range(NF)]),
        "w_d": wd.reshape(NF, 128, KT, 128).transpose(2, 1, 0, 3).reshape(KT, 128, NF * 128),
        "cache": cache,
        "state": np.asarray(i["state_gla"])[0],
        "pages": np.asarray(i["page_table"]).reshape(1, DB * NPG),
        "gains": np.concatenate([col(i["attn_norm_g"]), col(i["ffn_norm_g"]), col(i["final_norm_g"])], 1),
        "gates": np.concatenate([col(i["gla_gate_b"]), col(i["gla_onorm_g"]), col(kn[0]), col(kn[1])], 1),
        "gate_up": np.asarray(i["gla_gate_up"])[0],
        "rel_bias": np.asarray(i["rel_bias"]),
        "consts": cst, "rep": rep, "hots": hots,
    }
    return {k: np.ascontiguousarray(v) for k, v in out.items()}


def returned(r):
    y = r["o_y"].transpose(1, 0, 2).reshape(D, ALLT).T
    k = r["o_k"].transpose(2, 1, 0)
    vv = r["o_v"].reshape(ALLT, KVH, HD)
    ik = r["o_ik"].T
    gp = r["o_gp"].reshape(2, 64, 2, DV).transpose(2, 0, 1, 3).reshape(1, 1, GH, DK, DV)
    gs = r["o_gs"].reshape(2, 64, DB, 2, DV).transpose(2, 3, 0, 1, 4).reshape(1, DB, GH, DK, DV)
    c = np.ascontiguousarray
    return (c(y[:SEQ].reshape(1, SEQ, D)), c(y[SEQ:].reshape(DB, TS, D)),
            c(k[:SEQ].reshape(1, 1, SEQ, KVH, HD)), c(vv[:SEQ].reshape(1, 1, SEQ, KVH, HD)),
            c(ik[:SEQ].reshape(1, 1, SEQ, HD)), c(gp),
            c(k[SEQ:].reshape(1, DB, TS, KVH, HD)), c(vv[SEQ:].reshape(1, DB, TS, KVH, HD)),
            c(ik[SEQ:].reshape(1, DB, TS, HD)), c(gs))


def kernel(**inputs):
    import concourse.bacc as bacc
    from concourse.bass_utils import run_bass_kernel_spmd

    arrays = {"in_" + n: v for n, v in laid_out(inputs).items()}
    nc = bacc.Bacc("TRN2", target_bir_lowering=False, num_devices=1)
    a = {n[3:]: nc.dram_tensor(n, v.shape, mybir.dt.from_np(v.dtype), kind="ExternalInput").ap()
         for n, v in arrays.items()}
    for n, shape in outputs_of().items():
        a[n] = nc.dram_tensor(n, shape, F32, kind="ExternalOutput").ap()
    layer(nc, a)
    r = run_bass_kernel_spmd(nc, [arrays], core_ids=[0])
    return returned(r.results[0])
```

```python
from contextlib import ExitStack

import numpy as np

import concourse.bass as bass
from concourse import mybir

F32 = mybir.dt.float32
F16 = mybir.dt.float16
I32 = mybir.dt.int32
ALU = mybir.AluOpType
ACT = mybir.ActivationFunctionType
AX = mybir.AxisListType

D = 1024
KT = D // 128
SEQ = 2048
TOK = 512
NBLK = SEQ // TOK
DB, TS = 8, 8
NS = DB * TS
ALLT = SEQ + NS
PAST = 512
PAGE = 128
NPG = PAST // PAGE
NPOOL = 40
LS = PAST + NS
HEADS, KVH, HD = 8, 2, 64
GH, DK, DV = 4, 64, 128
CH = 64
RANK = 16
FF = 2816
NF = FF // 128
TOPK = 256
TOPK_S = (PAST + TS) // 4
RB, RD = 32, 128
EPS, LN_EPS = 1e-6, 1e-5
OUTSIDE = -1e30
TAKEN = -3e38
TAKEN_CUT = -2e38
W1, W2 = 384, 528

TILES = ([("glr", 0), ("ik", 0)] + [("gk", j) for j in range(2)] + [("gq", j) for j in range(2)]
         + [("iq", j) for j in range(4)] + [("k", g) for g in range(2)] + [("q", j) for j in range(4)]
         + [("gr", j) for j in range(4)] + [("v", 0)] + [("gv", j) for j in range(4)])
P_UNITS = TILES + [("iw", 0)]
SPLIT = ("iq", "q", "k")
NSPLIT = sum(what in SPLIT for what, _ in P_UNITS)
Q_UP, K_UP = 8.0, 16.0
Q_SCALE = Q_UP * K_UP * HD ** 0.5
I_UP = 16.0
W_UP, H_UP, M_UP, U_UP = 256.0, 64.0, 16.0, 4.0
WT = KT * 128
ND = 4
D_BLOCKS = (range(0, 6), range(6, 11), range(11, 17), range(17, 22))

C_ID, C_ONE, C_TRI, C_TRI8, C_ROW, C_SEQ, C_EPS, C_LNEPS = (
    0, 128, 256, 320, 384, 392, 456, 457)
NC_COLS = 458


ROUNDS = TOPK // 8
LATE = {0: {2: ROUNDS, 3: ROUNDS}, 2: {11: 8}, 3: {15: 20}}
LATE_TILES = [i for tiles in LATE.values() for i in tiles]


def bucket_table():
    n = np.arange(1024)
    f = np.log(np.maximum(n, 1).astype(np.float32) / np.float32(RB // 2)) / np.float32(np.log(RD / (RB // 2)))
    large = np.minimum(RB // 2 + (f * np.float32(RB - RB // 2)).astype(np.int32), RB - 1)
    return np.where(n < RB // 2, n, large)


def constants():
    c = np.zeros((128, NC_COLS), np.float32)
    p = np.arange(128)[:, None]
    t64 = np.arange(64)[None, :]
    c[:, C_ID:C_ID + 128] = np.eye(128)
    c[:, C_ONE:C_ONE + 128] = 1.0
    c[:, C_TRI:C_TRI + 64] = (p % 64) <= t64
    same = (p // TS == t64 // TS) & (p <= t64)
    c[:, C_TRI8:C_TRI8 + 64] = same
    c[:, C_ROW:C_ROW + 8] = (p // TS) == np.arange(8)[None, :]
    c[:, C_SEQ:C_SEQ + 64] = np.where((p // TS == t64 // TS) & (p >= t64), 0.0, OUTSIDE)
    c[:, C_EPS] = EPS
    c[:, C_LNEPS] = LN_EPS
    rep = np.zeros((64, DB, HEADS * TS), np.float32)
    for b in range(DB):
        for m in range(HEADS * TS):
            rep[b * TS + m % TS, b, m] = 1.0
    bucket = bucket_table()
    far = bucket == RB - 1
    assert far[RD:].all()
    hot1 = np.zeros((RB, W1), np.float32)
    hot2 = np.zeros((RB, W2), np.float32)
    for u in range(W1):
        hot1[bucket[max(255 - u, 0)], u] += 1.0
    for u in range(W2):
        hot2[bucket[max(PAST + TS - 1 - u, 0)], u] += 1.0
    hot1[RB - 1] -= 1.0
    hot2[RB - 1] -= 1.0
    return c, rep.reshape(64, -1), np.concatenate([hot1, hot2], 1)


def near_chunks(i):
    keys = 128 * (i + 1)
    near = min(256, keys)
    far = keys - near
    out = [(a, min(512, far - a), False) for a in range(0, far, 512)]
    return out + [(far, near, True)]


def score_chunks(i):
    keys = 128 * (i + 1)
    return [(a, min(512, keys - a)) for a in range(0, keys, 512)]


def layer(nc, a):
    with ExitStack() as ctx:
        def sb(name, shape, dt=F32):
            return ctx.enter_context(nc.sbuf_tensor(name, shape, dt))

        bank = [ctx.enter_context(nc.psum_tensor(f"bank{i}", [128, 512], F32)) for i in range(8)]
        skew1 = nc.dram_tensor("skew1", (HEADS, 128, W1), F32, kind="Internal").ap()
        skew2 = nc.dram_tensor("skew2", (HEADS, TS, W2), F32, kind="Internal").ap()

        cst = sb("cst", [128, NC_COLS])
        kT = sb("kT", [128, KVH, 2, SEQ], F16)
        ikT = sb("ikT", [128, 2, SEQ], F16)
        kTs = sb("kTs", [128, KVH, NS])
        ikTs = sb("ikTs", [128, NS])
        vtok = sb("vtok", [128, SEQ // 128, 128])
        vnew = sb("vnew", [NS, 128])
        near_bias = sb("near_bias", [128, HEADS, 256])
        gvec = sb("gvec", [128, 3 * KT])
        gates = sb("gates", [128, 5])
        gate_up = sb("gate_up", [RANK, 2 * 128])
        state = sb("state", [128, 2, DV])
        X = sb("X", [128, KT, TOK])
        H = sb("H", [128, 2, KT, TOK], F16)
        q = sb("q", [128, HEADS, TOK], F16)
        iw = sb("iw", [128, TOK // 128, 8])
        scores = sb("scores", [128, 4 * SEQ - 6 * 128])
        R = sb("R", [128, NF * TOK])
        mixA = sb("mixA", [128, 2, 4, TOK], F16)
        mixG = sb("mixG", [128, 2, 2, GH, TOK], F16)
        raw = sb("raw", [128, 2, WT])
        ring = sb("ring", [128, 4, 2, WT], F16)
        top8 = sb("top8", [128, 8])
        mx = sb("mx", [128, 2, 8])
        nmax = sb("nmax", [128, 2])
        den = sb("den", [128, 4])
        rden = sb("rden", [128, 4])
        pages = sb("pages", [1, DB * NPG], I32)

        ident = cst[:, C_ID:C_ID + 128]
        ones = cst[:, C_ONE:C_ONE + 128]
        eps = cst[:, C_EPS:C_EPS + 1]
        lneps = cst[:, C_LNEPS:C_LNEPS + 1]

        def cut(t, at, *dims):
            n = int(np.prod(dims))
            v = t[:, at:at + n]
            if len(dims) == 1:
                return v
            if len(dims) == 2:
                return v.rearrange("p (a b) -> p a b", b=dims[1])
            return v.rearrange("p (a b c) -> p a b c", b=dims[1], c=dims[2])

        Xf = X[:, :, :].rearrange("p k n -> p (k n)")
        Hf = H[:, :, :, :].rearrange("p s k n -> p (s k n)").bitcast(F32)
        Sf = scores[:, :]
        Rf = R[:, :]
        hots = cut(Rf, 0, W1 + W2)
        relb = cut(Rf, 1024, HEADS)
        relw = cut(Rf, 1032, HEADS, 128)
        row1 = cut(Rf, 2056, HEADS, W1)
        row2 = cut(Rf, 2056 + HEADS * W1, HEADS, W2)
        sq = cut(Rf, 0, KT, TOK)
        iq = cut(Rf, 0, 2048).bitcast(F16).rearrange("p (h n) -> p h n", n=TOK)
        iqs = cut(Rf, 0, 4, TOK)
        qs = q[:, :, :].rearrange("p h n -> p (h n)").bitcast(F32).rearrange("p (j n) -> p j n", n=TOK)
        k32 = cut(Xf, 2048, KVH, TOK)
        ik32 = cut(Rf, 9216, TOK)
        gq = cut(Rf, 2048, 2, TOK)
        gk = cut(Rf, 3072, 2, TOK)
        gr = cut(Rf, 4096, 4, TOK)
        la = cut(Rf, 6144, 2, TOK)
        gv = cut(Rf, 7168, 4, TOK)
        glr = cut(Rf, 9216, TOK)
        att = cut(Rf, 9728, 2, 4, 128)
        khs = cut(Rf, 9728, 256)
        atts = cut(Rf, 9984, 4, 64)
        cum = cut(Sf, 0, 2, TOK)
        exa = cut(Sf, 1024, 2, TOK)
        exb = cut(Sf, 2048, 2, TOK)
        qgz = cut(Sf, 3072, 4, TOK)
        qiz = cut(Sf, 5120, 4, TOK)
        ikx = cut(Rf, 10752, TOK)
        rst = cut(Rf, 9728, TOK)
        ikc = cut(Rf, 10240, TOK)
        gvz = cut(Sf, 2048, 2, 512)
        nG = [cut(Xf, 512 * j, TOK) for j in range(4)]
        kg = cut(Xf, 0, 2, TOK)
        kh = cut(Xf, 1024, 2, TOK)
        khz = cut(Xf, 2048, 4, 2, 256)
        sin = cut(Xf, 2048, DB, 2, DV)
        oT = cut(Hf, 0, GH, TOK)
        o2 = cut(Hf, 2048, GH, TOK)
        oroot = cut(Rf, 7168, GH, TOK)
        nY = [[mixG[:, par, :, :, :].rearrange("p s h n -> p (s h n)").bitcast(F32)[:, 512 * j:512 * j + TOK]
               for j in range(4)] for par in range(2)]
        nP = [nY[b % 2] for b in range(NBLK + 1)]
        nF = [cut(Rf, 4096 + 512 * j, TOK) for j in range(4)]
        hn = cut(Rf, 0, KT, TOK)
        relu = cut(Rf, 2048, 4, 512)
        lg = cut(Rf, 0, 2, 2048)
        pT = cut(Rf, 4096, 2, 16, 128)
        nearm = cut(Rf, 8192, 2, 256)
        osb = cut(Rf, 8704, 2, 512)
        mix32 = cut(Rf, 9728, 4, 128)
        iqz = cut(Rf, 2048, DB, 64)
        rep = cut(ikT[:, :, :].rearrange("p s n -> p (s n)").bitcast(F32), 0, DB, 64)
        cache = [vtok[:, :, :].rearrange("p (g t) n -> p g (t n)", g=NPG),
                 near_bias[:, :, :].rearrange("p (g h) n -> p g (h n)", g=NPG),
                 cut(Rf, 4096, NPG, 512), cut(Rf, 6144, NPG, 512)]
        srelu = cut(Rf, 8192, 2, LS)
        wrow = cut(Rf, 9344, DB, 64)
        wsel = cut(Rf, 9856, DB, 64)
        qz = cut(Rf, 2048, DB, 64)
        slg = cut(Rf, 8192, 2, LS)
        spT = cut(Rf, 9344, 2, 5, 64)
        sbias = cut(Rf, 9984, PAST + TS)[0:HEADS * TS]
        sscore = Sf[0:64, 0:LS + 6]
        outev = cut(Rf, 6144, 4, 512)
        H32 = cut(Hf, 0, KT, TOK)
        U = Rf.bitcast(F16).rearrange("p (f s n) -> p f s n", s=2, n=TOK)
        ffev = mixA[:, :, :, :].rearrange("p s j n -> p (s j n)").bitcast(F32).rearrange("p (j n) -> p j n", n=TOK)

        sems = {}

        def S(name):
            if name not in sems:
                sems[name] = ctx.enter_context(nc.semaphore(name))
            return sems[name]

        SCHED = [("B", 0), ("P", 0), ("G", 0), ("I", 0), ("A", 0)]
        for b in range(1, NBLK + 1):
            SCHED += [("P", b), ("G", b), ("I", b), ("F", b - 1), ("A", b)]
        SCHED += [("F", NBLK)]

        def ntok(b):
            return TOK if b < NBLK else NS

        ENG = ("pe", "act", "dve", "pool")

        def phase_start(eng, n):
            if n:
                for who in ENG:
                    eng.wait_ge(S("end_" + who), n)

        def i_start(eng, n, b):
            if b == NBLK:
                phase_start(eng, n)
            else:
                phase_start(eng, n - 1)

        def a_start(eng, n, b, waits_picks=False):
            if b:
                phase_start(eng, n - 1)
                if waits_picks:
                    eng.wait_ge(S("end_dve"), n)
            else:
                phase_start(eng, n)

        base, at = {}, 0
        for kind, b in SCHED:
            for part, count in {"P": [("P", len(TILES))],
                                "F": [("O", KT), ("U", 2 * NF), ("D", ND * KT)]}.get(kind, []):
                base[part, b] = at
                at += count

        def value(c, i, step):
            return c if i is None else i * step + c

        def raw_at(n):
            last = base["P", NBLK] + 4
            if n < last:
                return raw[:, n % 2, :], S(f"weights_in{n % 2}"), n // 2, 2
            m = (n - last) % 4
            keys = kT[:, :, :, :].rearrange("p g s n -> p (g s n)").bitcast(F32)
            return keys[:, WT * m:WT * m + WT], S(f"last_weights_in{m}"), (n - last) // 4, 4

        def first_tiles(nph):
            if nph + 1 == len(SCHED) or SCHED[nph + 1][0] not in "PF":
                return [], None
            kind, b = SCHED[nph + 1]
            n = base[{"P": "P", "F": "O"}[kind], b]
            return range(n, n + 4), lows_by(kind, b)

        def lows_by(kind, b):
            return "pool" if kind == "F" and b < NBLK else "dve"

        def score_at(i):
            return sum(128 * (j + 1) for j in range(12, 12 + i % 4))

        IU = [(i, c, h) for i in range(2, 16) for c in range(len(score_chunks(i))) for h in range(HEADS)]
        IN = {u: n for n, u in enumerate(IU)}
        AU = [(i, h) for i in range(16) for h in range(HEADS)]
        QU = [(i, h, c) for i, h in AU for c in range(len(near_chunks(i)))]
        QN = {u: n for n, u in enumerate(QU)}
        TU = [(i, h, g) for i, h in AU for g in range(-(-(i + 1) // 4))]
        TN = {u: n for n, u in enumerate(TU)}

        def x_loads(nph):
            return 1 + sum(k in "PF" for k, _ in SCHED[:nph])

        def tiles_of(b):
            return range(4 * b, 4 * b + 4)

        block = ctx.enter_context(nc.Block())

        @block.sync
        def _(sp):
            sp.dma_start(cst[:, :], a["consts"]).then_inc(S("consts_in"), 16)
            sp.dma_start(hots[0:RB], a["hots"]).then_inc(S("consts_in"), 16)
            sp.dma_start(relb[0:RB], a["rel_bias"]).then_inc(S("consts_in"), 16)
            sp.dma_start(gvec[:, :], a["gains"]).then_inc(S("consts_in"), 16)
            sp.dma_start(gates[:, :], a["gates"]).then_inc(S("consts_in"), 16)
            sp.dma_start(gate_up[:, :], a["gate_up"]).then_inc(S("consts_in"), 16)
            sp.dma_start(pages[:, :], a["pages"]).then_inc(S("pages_in"), 16)
            stores = 0

            def weights(n, src, i=None, step=0):
                cols = src.shape[-1]
                place, arrived, m, places = raw_at(n)
                if m:
                    sp.wait_ge(S("w_split"), value(n - places + 1, i, step))
                sp.dma_start(place[:, 0:cols], src).then_inc(arrived, 16)

            def load_x(b, NT):
                sp.dma_start(X[:, :, 0:NT], a["xT"][:, :, TOK * b:TOK * b + NT]).then_inc(S("x_in"), 16)

            def load_cache(n, s):
                for p in range(NPG):
                    at = sp.value_load(pages[0:1, s * NPG + p:s * NPG + p + 1], min_val=0, max_val=NPOOL - 1)
                    sp.dma_start(cache[n % 4][:, p, :],
                                 a["cache"][bass.ds(at, 1)].rearrange("o p n -> p (o n)")
                                 ).then_inc(S(f"cache_in{n % 4}"), 16)

            for nph, (kind, b) in enumerate(SCHED):
                NT = ntok(b)
                t0 = TOK * b
                if kind == "B":
                    load_x(0, NT=TOK)
                    for t in range(2):
                        weights(base["P", 0] + t, a["w_in"][t])
                    sp.wait_ge(S("pages_in"), 16)
                    sp.wait_ge(S("bias_rows"), 1)
                    sp.dma_start(skew1.rearrange("h p w -> p h w"), row1).then_inc(S("skew_dma"), 16)
                    sp.dma_start(skew2.rearrange("h p w -> p h w"), row2[0:TS]).then_inc(S("skew_dma"), 16)
                    sp.wait_ge(S("skew_dma"), 32)
                    sp.dma_start(near_bias[:, :, :],
                                 bass.AP(skew1.tensor, 127, [[W1 - 1, 128], [128 * W1, HEADS], [1, 256]])
                                 ).then_inc(S("skew_dma"), 16)
                if kind == "P":
                    n0 = base["P", b]
                    for t in range(2, len(TILES)):
                        if t == 4 and b == NBLK:
                            phase_start(sp, nph)
                        weights(n0 + t, a["w_in"][t])
                        if t == 18 and b < NBLK:
                            sp.wait_ge(S("p_split"), NSPLIT * b + 6)
                            sp.dma_start(a["o_k"][:, :, t0:t0 + NT], k32[0:64]).then_inc(S("outputs"), 16)
                            stores += 16
                    if stores:
                        sp.wait_ge(S("outputs"), stores)
                    sp.sem_inc(S("stored"), 1)
                if kind == "G" and b == NBLK:
                    phase_start(sp, nph)
                    for e in range(2):
                        for j in range(2):
                            sp.dma_start(sin[64 * e:64 * e + 64, :, j, :],
                                         a["state"][:, 2 * j + e].rearrange("b k v -> k b v")
                                         ).then_inc(S("state_in"), 16)
                    sp.dma_start(rep[0:64], a["rep"].rearrange("p (a b) -> p a b", b=64)
                                 ).then_inc(S("rep_in"), 16)
                    for s in range(2):
                        load_cache(s, s)
                if kind == "I":
                    if b:
                        for t in range(2):
                            weights(base["O", b - 1] + t, a["w_out"][t])
                    i_start(sp, nph, b)
                    for who in ("pe", "act", "dve"):
                        sp.wait_ge(S("end_" + who), nph)
                    pairs = [(a["o_ik"][:, t0:t0 + NT], (ik32 if b < NBLK else ikTs)[0:64])]
                    if b < NBLK:
                        pairs.append((a["o_v"][t0:t0 + NT].rearrange("(t p) n -> p t n", p=128),
                                      vtok[:, 4 * b:4 * b + 4, :]))
                    else:
                        pairs += [(a["o_k"][:, :, t0:t0 + NT], kTs[0:64]),
                                  (a["o_v"][t0:t0 + NT], vnew[:, :]), (a["o_gs"], sin)]
                    if b == NBLK - 1:
                        pairs.append((a["o_gp"], state[:, :, :]))
                    for dst, src in pairs:
                        sp.dma_start(dst, src).then_inc(S("outputs"), 16)
                        stores += 16
                    sp.wait_ge(S("outputs"), stores)
                    sp.sem_inc(S("stored"), 1)
                    if b:
                        load_x(b - 1, TOK)
                    if b == NBLK:
                        for s in range(2, DB + 2):
                            if s >= 4:
                                sp.wait_ge(S("si_dots"), s - 3)
                            load_cache(s, s % DB)
                if kind == "A" and b < NBLK:
                    for t in range(2):
                        weights(base["P", b + 1] + t, a["w_in"][t])
                    if b == 0:
                        phase_start(sp, nph)
                    load_x(b + 1, ntok(b + 1))
                if kind == "A" and b == NBLK:
                    for s in range(4, DB):
                        sp.wait_ge(S("sa_pv"), s - 3)
                        load_cache(s, s)
                    for t in range(2):
                        weights(base["O", b] + t, a["w_out"][t])
                    load_x(b, NT)
                if kind == "F":
                    n0 = base["O", b]
                    for t in range(2, KT):
                        weights(n0 + t, a["w_out"][t])
                    with sp.Fori(0, NF // 2) as i:
                        for r in range(4):
                            row = a["w_gu"][bass.ds(i * 2 + r // 2, 1)].rearrange("t p m -> p (t m)")
                            weights(base["U", b] + r, row[:, WT * (r % 2):WT * (r % 2) + WT], i, 4)
                    with sp.Fori(0, KT // 2) as i:
                        for r in range(2 * ND):
                            row = a["w_d"][bass.ds(i * 2 + r // ND, 1)].rearrange("t p m -> p (t m)")
                            ks = D_BLOCKS[r % ND]
                            weights(base["D", b] + r, row[:, 128 * ks[0]:128 * ks[-1] + 128], i, 2 * ND)
                    if b == NBLK - 1:
                        sp.wait_ge(S("end_pe"), nph + 1)
                        sp.dma_start(sbias, bass.AP(skew2.tensor, TS - 1, [[TS * W2, HEADS], [W2 - 1, TS],
                                                                           [1, PAST + TS]])
                                     ).then_inc(S("sbias_in"), 16)
                        for s in range(2, 4):
                            load_cache(s, s)
                    sp.wait_ge(S("f_y"), b + 1)
                    sp.dma_start(a["o_y"][:, :, t0:t0 + NT], H32[:, :, 0:NT]).then_inc(S("outputs"), 16)
                    stores += 16
                    sp.wait_ge(S("outputs"), stores)
                    sp.sem_inc(S("stored"), 1)

        def halves(h):
            e = 64 * (h % 2)
            return slice(e, e + 64), slice(64 - e, 128 - e)

        def out_counts(b, u):
            split = [b < NBLK and what in SPLIT for what, _ in P_UNITS]
            n = min(b, NBLK)
            before = NSPLIT * n
            return (len(P_UNITS) * b - before + split[:u + 1].count(False),
                    before + split[:u + 1].count(True))

        def stored_before(eng, nph):
            n = sum(1 for k, _ in SCHED[:nph] if k in "PIF")
            if n:
                eng.wait_ge(S("stored"), n)

        @block.tensor
        def _(pe):
            mm = nc.tensor.matmul

            def weights_at(n, i=None, step=0):
                pe.wait_ge(S("w_split"), value(n + 1, i, step))
                return ring[:, n % 4, 0, :], ring[:, n % 4, 1, :]

            def three(o, lhs, rhs, first, last):
                mm(o, lhs[0], rhs[0], start=first, stop=False)
                mm(o, lhs[0], rhs[1], start=False, stop=False)
                return mm(o, lhs[1], rhs[0], start=False, stop=last)

            def token_squares(b, ks=range(KT)):
                for k in ks:
                    pe.wait_ge(S("p_sq"), KT * b + k + 1)
                    last = mm(bank[7][:, 0:ntok(b)], ones, H32[:, k, 0:ntok(b)], start=(k == 0), stop=(k == KT - 1))
                if k == KT - 1:
                    last.then_inc(S("p_ss"), 1)

            for nph, (kind, b) in enumerate(SCHED):
                NT = ntok(b)
                t0 = TOK * b
                ntile = NT // 128 if b < NBLK else 1
                tw = min(NT, 128)
                if kind == "A":
                    a_start(pe, nph, b)
                elif kind == "I":
                    i_start(pe, nph, b)
                else:
                    phase_start(pe, nph)
                if kind == "B":
                    pe.wait_ge(S("bias_wide"), 1)
                    for h in range(HEADS):
                        if h >= 2:
                            pe.wait_ge(S("bias_copied"), h - 1)
                        k = 3 * (h % 2)
                        mm(bank[k][:, 0:W1], relw[0:RB, h, :], hots[0:RB, 0:W1], start=True, stop=True)
                        mm(bank[k + 1][:, 0:512], relw[0:RB, h, :], hots[0:RB, W1:W1 + 512], start=True, stop=True)
                        mm(bank[k + 2][:, 0:W2 - 512], relw[0:RB, h, :], hots[0:RB, W1 + 512:W1 + W2],
                           start=True, stop=True).then_inc(S("bias_mm"), 1)
                if kind == "P":
                    if b == 0:
                        token_squares(0)
                    for u, (what, j) in enumerate(TILES):
                        w = weights_at(base["P", b] + u)
                        if u >= 4:
                            copied, taken = out_counts(b, u - 4)
                            if b < NBLK and TILES[u - 4][0] in SPLIT:
                                pe.wait_ge(S("p_split"), taken)
                            else:
                                pe.wait_ge(S("p_copied"), copied)

                        def token_rows(o, lo, hi):
                            for t in range(ntile):
                                for k in range(KT):
                                    last = three(o[0:tw, t * (hi - lo):(t + 1) * (hi - lo)],
                                                 [H[:, s, k, t * 128:t * 128 + tw] for s in range(2)],
                                                 [w[s][:, 128 * k + lo:128 * k + hi] for s in range(2)],
                                                 k == 0, k == KT - 1)
                            return last

                        if what in ("v", "gv"):
                            last = token_rows(bank[u % 4], 0, 128)
                        else:
                            hi = RANK if what == "glr" else 128
                            for k in range(KT):
                                if u == 0:
                                    pe.wait_ge(S("p_h"), KT * b + k + 1)
                                last = three(bank[u % 4][0:hi, 0:NT],
                                             [w[s][:, 128 * k:128 * k + hi] for s in range(2)],
                                             [H[:, s, k, 0:NT] for s in range(2)], k == 0, k == KT - 1)
                            if what == "glr":
                                last = token_rows(bank[4], RANK, RANK + 8)
                        last.then_inc(S("products"), 1)
                        if u == 3:
                            pe.wait_ge(S("p_copied"), out_counts(b, 1)[0])
                            mm(bank[7][:, 0:NT], ones, ikx[:, 0:NT], start=True, stop=True).then_inc(S("g_mean"), 1)
                            for j in range(2):
                                last = mm(bank[5 + j][:, 0:NT], gate_up[:, j * 128:(j + 1) * 128],
                                          glr[0:RANK, 0:NT], start=True, stop=True)
                            last.then_inc(S("g_gate"), 1)
                        if u == 6:
                            pe.wait_ge(S("g_ikc"), b + 1)
                            mm(bank[7][:, 0:NT], ones, ikx[:, 0:NT], start=True, stop=True).then_inc(S("g_var"), 1)
                if kind == "G":
                    pe.wait_ge(S("g_k"), b + 1)
                    pe.wait_ge(S("g_q"), b + 1)
                    if b < NBLK:
                        for t in range(4):
                            T = 4 * b + t
                            c0 = 128 * t
                            if t >= 2:
                                pe.wait_ge(S("g_khz"), T - 1)
                            for j in range(2):
                                last = nc.tensor.transpose(bank[t % 2][:, j * 128:(j + 1) * 128],
                                                           kh[:, j, c0:c0 + 128], ident)
                            last.then_inc(S("g_kt"), 1)
                            if t >= 2:
                                pe.wait_ge(S("g_atm"), T - 1)
                            for c in range(2):
                                for h in range(GH):
                                    cc = c0 + CH * c
                                    last = mm(bank[2 + t % 2][64 * c:64 * c + 64, h * 64:(h + 1) * 64],
                                              kg[:, h // 2, cc:cc + CH], qgz[:, h, cc:cc + CH],
                                              start=True, stop=True)
                            last.then_inc(S("g_at"), 1)
                            pe.wait_ge(S("g_atm"), T + 1)
                            pe.wait_ge(S("g_khz"), T + 1)
                            if t >= 2:
                                pe.wait_ge(S("g_oc"), T - 1)
                            for h in range(GH):
                                mm(bank[6 + t % 2][:, h * 128:(h + 1) * 128], gv[:, t, h * 128:(h + 1) * 128],
                                   att[:, t % 2, h, :], start=(h == 0), stop=False, skip_group_check=True)
                            for c in range(2):
                                cc = c0 + CH * c
                                n = 2 * T + c
                                if n:
                                    pe.wait_ge(S("g_state"), n)
                                for h in range(GH):
                                    mm(bank[6 + t % 2][:, h * 128 + CH * c:h * 128 + CH * c + CH],
                                       state[:, h // 2, :], qiz[:, h, cc:cc + CH],
                                       start=False, stop=(c == 1), skip_group_check=True)
                                for j in range(2):
                                    last = mm(bank[4 + c][:, j * 256:(j + 1) * 256],
                                              khz[:, t, c, j * 128:(j + 1) * 128],
                                              gv[:, t, j * 256:(j + 1) * 256], start=True, stop=True)
                                last.then_inc(S("g_o"), 1)
                    else:
                        for j in range(2):
                            last = nc.tensor.transpose(bank[0][0:NS, j * 128:(j + 1) * 128], kh[:, j, 0:NS], ident)
                        last.then_inc(S("g_kt"), 1)
                        for h in range(GH):
                            last = mm(bank[2][0:NS, h * 64:(h + 1) * 64], kg[:, h // 2, 0:NS], qgz[:, h, 0:NS],
                                      start=True, stop=True)
                        last.then_inc(S("g_at"), 1)
                        pe.wait_ge(S("g_atm"), 4 * NBLK + 1)
                        pe.wait_ge(S("state_in"), 64)
                        for h in range(GH):
                            mm(bank[6][:, h * 64:(h + 1) * 64], gv[0:NS, 0, h * 128:(h + 1) * 128],
                               atts[0:NS, h, :], start=(h == 0), stop=False, skip_group_check=True)
                        for s in range(DB):
                            for h in range(GH):
                                last = mm(bank[6][:, h * 64 + TS * s:h * 64 + TS * s + TS], sin[:, s, h // 2, :],
                                          qiz[:, h, TS * s:TS * s + TS], start=False, stop=True,
                                          skip_group_check=True)
                        last.then_inc(S("g_o"), 1)
                        pe.wait_ge(S("g_khz"), 4 * NBLK + 1)
                        for s in range(DB):
                            pe.wait_ge(S("gs_gvz"), s + 1)
                            if s >= 2:
                                pe.wait_ge(S("gs_new"), s - 1)
                            for j in range(2):
                                last = mm(bank[4 + s % 2][:, j * 256:(j + 1) * 256], khs[0:NS, j * 128:(j + 1) * 128],
                                          gvz[0:NS, s % 2, j * 256:(j + 1) * 256], start=True, stop=True)
                            last.then_inc(S("gs_u"), 1)
                    pe.wait_ge(S("g_o2"), b + 1)
                    for h in range(GH):
                        last = mm(bank[h][:, 0:NT], ones, o2[:, h, 0:NT], start=True, stop=True)
                    last.then_inc(S("g_oss"), 1)
                if kind == "I" and b < NBLK:
                    pe.wait_ge(S("g_root"), b + 1)
                    pe.wait_ge(S("g_state"), 8 * (b + 1))
                    for i in tiles_of(b):
                        if i < 2:
                            continue
                        cq = 128 * (i % 4)
                        for c, (k0, kn) in enumerate(score_chunks(i)):
                            for h in range(HEADS):
                                n = IN[i, c, h]
                                if n >= 8:
                                    pe.wait_ge(S("i_relu"), n - 7)
                                mm(bank[n % 8][:, 0:kn], iq[:, h, cq:cq + 128], ikT[:, 0, k0:k0 + kn],
                                   start=True, stop=False)
                                mm(bank[n % 8][:, 0:kn], iq[:, h, cq:cq + 128], ikT[:, 1, k0:k0 + kn],
                                   start=False, stop=True).then_inc(S("i_dots"), 1)
                if kind == "I" and b == NBLK:
                    pe.wait_ge(S("si_wrow"), 1)
                    for s in range(DB):
                        last = mm(bank[0][0:64, s * 64:(s + 1) * 64], wrow[0:64, s, :], ident[0:64, 0:64],
                                  start=True, stop=True)
                    last.then_inc(S("si_wt"), 1)
                    pe.wait_ge(S("si_iqz"), 1)

                    def dots(s):
                        pe.wait_ge(S(f"cache_in{s % 4}"), 16 * NPG * (s // 4 + 1))
                        if s >= 2:
                            pe.wait_ge(S("si_relu"), s - 1)
                        mm(bank[2 + 2 * (s % 2)][0:64, :], iqz[:, s, :], cache[s % 4][:, :, 256:384],
                           start=True, stop=True)
                        mm(bank[3 + 2 * (s % 2)][0:64, 0:NS], iqz[:, s, :], ikTs[:, :],
                           start=True, stop=True).then_inc(S("si_dots"), 1)

                    dots(0)
                    pe.wait_ge(S("si_wsel"), 1)
                    for s in range(DB):
                        if s + 1 < DB:
                            dots(s + 1)
                        pe.wait_ge(S("si_relu"), s + 1)
                        mm(bank[6][0:64, :], wsel[0:64, s, :], srelu[0:64, s % 2, 0:PAST],
                           start=(s == 0), stop=(s == DB - 1))
                        mm(bank[7][0:64, 0:NS], wsel[0:64, s, :], srelu[0:64, s % 2, PAST:LS],
                           start=(s == 0), stop=(s == DB - 1)).then_inc(S("si_sum"), 1)
                if kind == "A" and b < NBLK:
                    def logits(i, h):
                        cq = 128 * (i % 4)
                        for c, (k0, kn, near) in enumerate(near_chunks(i)):
                            n = QN[i, h, c]
                            if n >= 3:
                                pe.wait_ge(S("a_masked"), n - 2)
                            mm(bank[n % 3][:, 0:kn], q[:, h, cq:cq + 128], kT[:, h // 4, 0, k0:k0 + kn],
                               start=True, stop=False)
                            mm(bank[n % 3][:, 0:kn], q[:, h, cq:cq + 128], kT[:, h // 4, 1, k0:k0 + kn],
                               start=False, stop=True).then_inc(S("a_logits"), 1)

                    def turn(i, h, groups):
                        u = 8 * i + h
                        pe.wait_ge(S("a_exp"), u + 1)
                        for g in range(-(-(i + 1) // 4))[groups]:
                            n = TN[i, h, g]
                            if n >= 2:
                                pe.wait_ge(S("a_pTc"), n - 1)
                            for t in range(4 * g, min(4 * g + 4, i + 1)):
                                last = nc.tensor.transpose(bank[3 + n % 2][:, 128 * (t % 4):128 * (t % 4) + 128],
                                                           lg[:, u % 2, 128 * t:128 * t + 128], ident)
                            last.then_inc(S("a_pT"), 1)

                    def values(i, h):
                        u = 8 * i + h
                        pe.wait_ge(S("a_pTc"), TN[i, h, -(-(i + 1) // 4) - 1] + 1)
                        if u >= 2:
                            pe.wait_ge(S("a_scaled"), u - 1)
                        for t in range(i + 1):
                            last = mm(bank[5 + u % 2][:, 0:128], pT[:, u % 2, t, :], vtok[:, t, :],
                                      start=(t == 0), stop=(t == i))
                        last.then_inc(S("a_pv"), 1)

                    def turn_out(i):
                        pe.wait_ge(S("a_scaled"), 8 * i + 8)
                        if i:
                            pe.wait_ge(S("a_mix"), i)
                        for j in range(4):
                            last = nc.tensor.transpose(bank[7][:, 128 * j:128 * j + 128],
                                                       osb[:, i % 2, 128 * j:128 * j + 128], ident)
                        last.then_inc(S("a_oT"), 1)

                    units = [(i, h) for i in tiles_of(b) for h in range(HEADS)]
                    logits(*units[0])
                    for n, (i, h) in enumerate(units):
                        if n + 1 < len(units):
                            logits(*units[n + 1])
                        turn(i, h, slice(0, 2))
                        if n:
                            values(*units[n - 1])
                        turn(i, h, slice(2, None))
                        if n >= 2 and units[n - 2][1] == HEADS - 1:
                            turn_out(units[n - 2][0])
                        if n >= len(units) - 5 and n < len(units) - 1:
                            pe.wait_ge(S("a_mix"), i)
                            k = 2 * (n - len(units) + 5)
                            token_squares(b + 1, range(k, k + 2))
                    values(*units[-1])
                    pe.wait_ge(S("p_root"), b + 2)
                    turn_out(units[-1][0])
                if kind == "A" and b == NBLK:
                    pe.wait_ge(S("sa_qz"), 1)
                    pe.wait_ge(S("rep_in"), 16)

                    def sample_logits(s):
                        pe.wait_ge(S(f"cache_in{s % 4}"), 16 * NPG * ((DB + s) // 4 + 1))
                        if s >= 2:
                            pe.wait_ge(S("sa_added"), s - 1)
                        past, new = bank[4 * (s % 2)], bank[4 * (s % 2) + 1]
                        mm(past[0:64, :], rep[0:64, s, :], sscore[:, 0:PAST], start=True, stop=False,
                           skip_group_check=True)
                        mm(new[0:64, 0:NS], rep[0:64, s, :], sscore[:, PAST:LS], start=True, stop=False,
                           skip_group_check=True)
                        for g in range(KVH):
                            mm(past[32 * g:32 * g + 32, :], qz[:, s, 32 * g:32 * g + 32],
                               cache[s % 4][:, :, 128 * g:128 * g + 128], start=False, stop=True,
                               skip_group_check=True)
                            last = mm(new[32 * g:32 * g + 32, 0:NS], qz[:, s, 32 * g:32 * g + 32],
                                      kTs[:, g, :], start=False, stop=True, skip_group_check=True)
                        last.then_inc(S("sa_logits"), 1)

                    sample_logits(0)
                    for s in range(DB):
                        if s + 1 < DB:
                            sample_logits(s + 1)
                        pe.wait_ge(S("sa_probs"), s + 1)
                        if s >= 2:
                            pe.wait_ge(S("sa_pTc"), s - 1)
                        for p in range(NPG):
                            nc.tensor.transpose(bank[2 + s % 2][:, 64 * p:64 * p + 64],
                                                slg[0:64, s % 2, 128 * p:128 * p + 128], ident[0:64, 0:64])
                        nc.tensor.transpose(bank[2 + s % 2][0:64, 256:320], slg[0:64, s % 2, PAST:LS],
                                            ident[0:64, 0:64]).then_inc(S("sa_pT"), 1)
                        pe.wait_ge(S("sa_pTc"), s + 1)
                        for g in range(KVH):
                            o = bank[6][0:64, s * 64 + 32 * g:s * 64 + 32 * g + 32]
                            for p in range(NPG):
                                mm(o, cache[s % 4][:, p, 384 + 64 * g:384 + 64 * g + 64],
                                   spT[:, s % 2, p, 32 * g:32 * g + 32], start=(p == 0), stop=False)
                            last = mm(o, vnew[:, 64 * g:64 * g + 64], spT[0:64, s % 2, 4, 32 * g:32 * g + 32],
                                      start=False, stop=True)
                        last.then_inc(S("sa_pv"), 1)
                if kind == "F":
                    par = b % 2
                    def squares(k):
                        pe.wait_ge(S("f_sq"), KT * b + k + 1)
                        last = mm(bank[2][:, 0:NT], ones, sq[:, k, 0:NT], start=(k == 0), stop=(k == KT - 1))
                        if k == KT - 1:
                            last.then_inc(S("f_ss"), 1)

                    for dt in range(KT):
                        if dt >= 3:
                            squares(dt - 3)
                        w = weights_at(base["O", b] + dt)
                        if dt >= 2:
                            pe.wait_ge(S("o_copied"), KT * b + dt - 1)
                        for k in range(KT):
                            x = [mixA[:, s, k, 0:NT] if k < 4 else mixG[:, par, s, k - 4, 0:NT] for s in range(2)]
                            last = three(bank[dt % 2][:, 0:NT], [w[s][:, 128 * k:128 * k + 128] for s in range(2)],
                                         x, k == 0, k == KT - 1)
                        last.then_inc(S("products"), 1)
                    for k in range(KT - 3, KT):
                        squares(k)
                    pe.wait_ge(S("f_h"), b + 1)
                    u0 = 2 * NF * b
                    with pe.Fori(0, NF // 2) as i:
                        for r in range(4):
                            w = weights_at(base["U", b] + r, i, 4)
                            pe.wait_ge(S("u_bank_free"), i * 4 + (u0 + r + 1))
                            for k in range(KT):
                                last = three(bank[4 + r][:, 0:NT], [w[s][:, 128 * k:128 * k + 128] for s in range(2)],
                                             [H[:, s, k, 0:NT] for s in range(2)], k == 0, k == KT - 1)
                            last.then_inc(S("products"), 1)
                    pe.wait_ge(S("u_pair_free"), 2 + NF * (b + 1))
                    with pe.Fori(0, KT // 2) as i:
                        for r in range(2 * ND):
                            if r % ND == 0:
                                pe.wait_ge(S("d_bank_free"), i * 2 + (KT * b + r // ND + 1))
                            w = weights_at(base["D", b] + r, i, 2 * ND)
                            for c, k in enumerate(D_BLOCKS[r % ND]):
                                last = three(bank[r // ND][:, 0:NT], [w[s][:, 128 * c:128 * c + 128] for s in range(2)],
                                             [U[:, k, s, 0:NT] for s in range(2)], k == 0, k == NF - 1)
                            last.then_inc(S("products"), 1)
                    for k in range(KT):
                        pe.wait_ge(S("y_sq"), KT * b + k + 1)
                        last = mm(bank[3][:, 0:NT], ones, H32[:, k, 0:NT], start=(k == 0), stop=(k == KT - 1))
                    last.then_inc(S("y_ss"), 1)
                pe.drain().then_inc(S("end_pe"), 1)

        @block.scalar
        def _(act):
            A = nc.scalar.activation

            def inverse_root(src, scale, e, ms, tmp, name):
                A(ms, src, ACT.Identity, scale=scale, bias=e)
                act.drain()
                A(tmp, ms, ACT.Ln)
                act.drain()
                A(tmp, tmp, ACT.Exp, scale=-0.5).then_inc(S(name), 1)

            def token_squares(b, loads, ks=range(KT)):
                act.wait_ge(S("x_in"), 16 * loads)
                for k in ks:
                    A(H32[:, k, 0:ntok(b)], X[:, k, 0:ntok(b)], ACT.Square).then_inc(S("p_sq"), 1)

            def token_root(b):
                act.wait_ge(S("p_ss"), b + 1)
                inverse_root(bank[7][:, 0:ntok(b)], 1.0 / D, eps, nP[b][0][:, 0:ntok(b)], nP[b][1][:, 0:ntok(b)],
                             "p_root")

            def highs(n, low_by, i=None, step=0, cols=WT):
                whole, arrived, m, places = raw_at(n)
                act.wait_ge(arrived, value(16 * (m + 1), i, 16 * step // places))
                if n >= 4:
                    act.wait_ge(S("products"), value(n - 3, i, step))
                last = A(ring[:, n % 4, 0, 0:cols], whole[:, 0:cols], ACT.Copy, scale=W_UP)
                if low_by == "pool":
                    last = A(whole[:, 0:cols], whole[:, 0:cols], ACT.Copy, scale=W_UP)
                last.then_inc(S("w_high"), 1)

            def highs_ahead(nph, which=slice(None)):
                tiles, low_by = first_tiles(nph)
                for n in tiles[which]:
                    highs(n, low_by)

            for nph, (kind, b) in enumerate(SCHED):
                NT = ntok(b)
                t0 = TOK * b
                ntile = NT // 128 if b < NBLK else 1
                tw = min(NT, 128)
                if kind == "A":
                    a_start(act, nph, b)
                elif kind == "I":
                    i_start(act, nph, b)
                else:
                    phase_start(act, nph)
                stored_before(act, nph - (kind == "A" and b > 0))
                if kind == "B":
                    act.wait_ge(S("consts_in"), 96)
                    act.sem_inc(S("u_bank_free"), 4)
                    act.sem_inc(S("d_bank_free"), 2)
                    act.sem_inc(S("u_pair_free"), 2)
                    act.sem_inc(S("d_buf_free"), 2)
                    highs_ahead(nph)
                if kind == "P":
                    if b == 0:
                        token_squares(0, x_loads(nph))
                        token_root(0)
                    def gates_step(u):
                        if u == 3:
                            act.wait_ge(S("g_gate"), b + 1)
                            for j in range(2):
                                A(la[:, j, 0:NT], bank[5 + j][:, 0:NT], ACT.Identity, bias=gates[:, j:j + 1])
                            act.drain()
                            A(exa[:, :, 0:NT], la[:, :, 0:NT], ACT.Abs)
                            act.drain()
                            A(exb[:, :, 0:NT], exa[:, :, 0:NT], ACT.Exp, scale=-1.0)
                            act.drain()
                            A(exa[:, :, 0:NT], exb[:, :, 0:NT], ACT.Ln, bias=1.0).then_inc(S("g_lsig"), 1)
                        if u == 8:
                            act.wait_ge(S("g_var"), b + 1)
                            inverse_root(bank[7][:, 0:NT], 1.0 / 128, lneps, nG[0][:, 0:NT], nG[1][:, 0:NT], "g_ikr")
                        if u == 12:
                            act.wait_ge(S("g_cum"), b + 1)
                            A(la[:, :, 0:NT], cum[:, :, 0:NT], ACT.Exp, scale=1.0 / 16)
                            A(kg[:, :, 0:NT], exa[:, :, 0:NT], ACT.Exp, scale=-1.0 / 16)
                            A(kh[:, :, 0:NT], exb[:, :, 0:NT], ACT.Exp, scale=1.0 / 16)
                            act.drain()
                            A(exa[:, :, 0:NT], exa[:, :, 0:NT], ACT.Exp, scale=1.0 / 16).then_inc(S("g_ex"), 1)

                    for u, (what, j) in enumerate(P_UNITS):
                        t = min(u, len(TILES) - 1)
                        if b < NBLK and what in SPLIT:
                            highs(base["P", b] + t + 4, "dve")
                            gates_step(u)
                            continue
                        act.wait_ge(S("products"), base["P", b] + t + 1)
                        o = bank[4 if what == "iw" else u % 4]
                        of = o[:, 0:NT]
                        scale = 1.0 / (W_UP * H_UP)
                        if what == "iq":
                            dst, src = iqs[:, j, 0:NT], of
                        elif what == "ik":
                            dst, src = ikx[:, 0:NT], of
                        elif what == "k":
                            dst, src = kTs[:, j, :], of
                        elif what == "q":
                            dst, src, scale = qs[:, j, 0:NT], of, scale * HD ** -0.5
                        elif what == "gq":
                            dst, src, scale = gq[:, j, 0:NT], of, scale * DK ** -0.5
                        elif what == "gk":
                            dst, src = gk[:, j, 0:NT], of
                        elif what == "gr":
                            dst, src = gr[:, j, 0:NT], of
                        elif what == "glr":
                            dst, src = glr[0:RANK, 0:NT], o[0:RANK, 0:NT]
                        elif what == "v" and b < NBLK:
                            dst, src = vtok[:, 4 * b:4 * b + 4, :], o[:, :].rearrange("p (t c) -> p t c", c=128)
                        elif what == "v":
                            dst, src = vnew[:, :], o[0:NS, 0:128]
                        elif what == "gv":
                            dst = gv[0:tw, 0:ntile, 128 * j:128 * j + 128]
                            src = o[0:tw, 0:128 * ntile].rearrange("p (t c) -> p t c", c=128)
                        else:
                            dst = iw[0:tw, 0:ntile, :]
                            src = o[0:tw, 0:8 * ntile].rearrange("p (t c) -> p t c", c=8)
                            scale *= 8 ** -0.5 * 64 ** -0.5
                        A(dst, src, ACT.Copy, scale=scale).then_inc(S("p_copied"), 1)
                        if u + 4 < len(TILES):
                            highs(base["P", b] + u + 4, "dve")
                        gates_step(u)
                if kind == "G":
                    act.wait_ge(S("g_zeros"), b + 1)
                    if b < NBLK:
                        for t in range(4):
                            T = 4 * b + t
                            act.wait_ge(S("g_kt"), T + 1)
                            for c in range(2):
                                last = A(khz[64 * c:64 * c + 64, t, c, :], bank[t % 2][64 * c:64 * c + 64, 0:256], ACT.Copy)
                            last.then_inc(S("g_khz"), 1)
                            act.wait_ge(S("g_o"), 2 * T + 2)
                            A(oT[:, :, 128 * t:128 * t + 128],
                              bank[6 + t % 2][:, :].rearrange("p (h n) -> p h n", n=128), ACT.Copy).then_inc(S("g_oc"), 1)
                    else:
                        act.wait_ge(S("g_kt"), 4 * NBLK + 1)
                        A(khs[0:NS], bank[0][0:NS, 0:256], ACT.Copy).then_inc(S("g_khz"), 1)
                        act.wait_ge(S("g_o"), 8 * NBLK + 1)
                        A(oT[:, :, 0:NS], bank[6][:, 0:256].rearrange("p (h n) -> p h n", n=NS), ACT.Copy
                          ).then_inc(S("g_oc"), 1)
                    act.drain()
                    A(o2[:, :, 0:NT], oT[:, :, 0:NT], ACT.Square).then_inc(S("g_o2"), 1)
                    act.wait_ge(S("g_oss"), b + 1)
                    for h in range(GH):
                        A(o2[:, h, 0:NT], bank[h][:, 0:NT], ACT.Identity, scale=1.0 / DV, bias=eps)
                    act.drain()
                    A(oroot[:, :, 0:NT], o2[:, :, 0:NT], ACT.Ln)
                    act.drain()
                    A(oroot[:, :, 0:NT], oroot[:, :, 0:NT], ACT.Exp, scale=-0.5).then_inc(S("g_root"), 1)
                    A(gr[:, :, 0:NT], gr[:, :, 0:NT], ACT.Silu)
                    act.drain()
                    A(gr[:, :, 0:NT], gr[:, :, 0:NT], ACT.Copy, scale=gates[:, 2:3]).then_inc(S("g_silu"), 1)
                if kind == "I" and b < NBLK:
                    chunk = 5 - sum(len(score_chunks(i)) for i in tiles_of(b))
                    for i in tiles_of(b):
                        if i < 2:
                            continue
                        for c, (k0, kn) in enumerate(score_chunks(i)):
                            for h in range(HEADS):
                                n = IN[i, c, h]
                                act.wait_ge(S("i_dots"), n + 1)
                                if n >= 4:
                                    act.wait_ge(S("i_added"), n - 3)
                                A(relu[:, n % 4, 0:kn], bank[n % 8][:, 0:kn], ACT.Relu,
                                  scale=1.0 / (I_UP * I_UP)).then_inc(S("i_relu"), 1)
                            if 0 <= chunk < 4:
                                highs_ahead(nph, slice(chunk, chunk + 1))
                            chunk += 1
                if kind == "I" and b == NBLK:
                    act.wait_ge(S("si_wt"), 1)
                    A(wsel[0:64], bank[0][0:64, :].rearrange("p (s t) -> p s t", t=64), ACT.Copy).then_inc(S("si_wsel"), 1)
                    for s in range(DB):
                        act.wait_ge(S("si_dots"), s + 1)
                        if s >= 2:
                            act.wait_ge(S("si_sum"), s - 1)
                        A(srelu[0:64, s % 2, 0:PAST], bank[2 + 2 * (s % 2)][0:64, :], ACT.Relu)
                        A(srelu[0:64, s % 2, PAST:LS], bank[3 + 2 * (s % 2)][0:64, 0:NS], ACT.Relu).then_inc(S("si_relu"), 1)
                    act.wait_ge(S("si_sum"), DB)
                    A(sscore[:, 0:PAST], bank[6][0:64, :], ACT.Copy).then_inc(S("si_copied"), 1)
                    highs_ahead(nph)
                if kind == "A" and b < NBLK:
                    def probs(i, h):
                        u = 8 * i + h
                        act.wait_ge(S("a_max"), u + 1)
                        if u >= 4:
                            act.wait_ge(S("a_scaled"), u - 3)
                        A(lg[:, u % 2, 0:128 * (i + 1)], lg[:, u % 2, 0:128 * (i + 1)], ACT.Exp,
                          bias=nmax[:, u % 2:u % 2 + 1], accum_out=den[:, u % 4:u % 4 + 1]).then_inc(S("a_exp"), 1)

                    def copy_pT(i, h, groups):
                        u = 8 * i + h
                        if u >= 2:
                            act.wait_ge(S("a_pv"), u - 1)
                        for g in range(-(-(i + 1) // 4))[groups]:
                            n = TN[i, h, g]
                            act.wait_ge(S("a_pT"), n + 1)
                            w = min(4, i + 1 - 4 * g)
                            A(pT[:, u % 2, 4 * g:4 * g + w, :],
                              bank[3 + n % 2][:, 0:128 * w].rearrange("p (t n) -> p t n", n=128),
                              ACT.Copy).then_inc(S("a_pTc"), 1)

                    def copy_mix(i):
                        act.wait_ge(S("a_oT"), i + 1)
                        if i:
                            act.wait_ge(S("a_mix_low"), i)
                        src = bank[7][:, :].rearrange("p (j n) -> p j n", n=128)
                        A(mix32, src, ACT.Copy, scale=M_UP)
                        A(mixA[:, 0, :, 128 * (i % 4):128 * (i % 4) + 128], src, ACT.Copy, scale=M_UP
                          ).then_inc(S("a_mix"), 1)

                    units = [(i, h) for i in tiles_of(b) for h in range(HEADS)]
                    probs(*units[0])
                    for n, (i, h) in enumerate(units):
                        copy_pT(i, h, slice(0, 2))
                        if n + 1 < len(units):
                            probs(*units[n + 1])
                        copy_pT(i, h, slice(2, None))
                        if n == 0:
                            highs_ahead(nph)
                        if n >= 2 and units[n - 2][1] == HEADS - 1:
                            copy_mix(units[n - 2][0])
                        if n >= len(units) - 6 and n < len(units) - 2:
                            stored_before(act, nph)
                            k = 2 * (n - len(units) + 6)
                            token_squares(b + 1, x_loads(nph + 1), range(k, k + 2))
                        if n == len(units) - 1:
                            token_root(b + 1)
                    copy_mix(units[-1][0])
                if kind == "A" and b == NBLK:
                    def sample_probs(s):
                        act.wait_ge(S("sa_max"), s + 1)
                        if s >= 2:
                            act.wait_ge(S("sa_probs"), s - 1)
                        A(slg[0:64, s % 2, :], slg[0:64, s % 2, :], ACT.Exp, bias=nmax[0:64, s % 2:s % 2 + 1],
                          accum_out=den[0:64, s % 2:s % 2 + 1]).then_inc(S("sa_exp"), 1)

                    sample_probs(0)
                    for s in range(DB):
                        act.wait_ge(S("sa_pT"), s + 1)
                        if s >= 2:
                            act.wait_ge(S("sa_pv"), s - 1)
                        A(spT[:, s % 2, 0:NPG, :], bank[2 + s % 2][:, 0:256].rearrange("p (t n) -> p t n", n=64), ACT.Copy)
                        A(spT[0:64, s % 2, NPG, :], bank[2 + s % 2][0:64, 256:320], ACT.Copy).then_inc(S("sa_pTc"), 1)
                        if s + 1 < DB:
                            sample_probs(s + 1)
                    highs_ahead(nph)
                if kind == "F":
                    def square(k):
                        act.wait_ge(S("o_added"), KT * b + k + 1)
                        A(sq[:, k, 0:NT], X[:, k, 0:NT], ACT.Square).then_inc(S("f_sq"), 1)

                    for dt in range(KT):
                        n = KT * b + dt
                        act.wait_ge(S("products"), base["O", b] + dt + 1)
                        if dt >= 4:
                            act.wait_ge(S("o_added"), n - 3)
                        A(outev[:, dt % 4, 0:NT], bank[dt % 2][:, 0:NT], ACT.Copy, scale=1.0 / (W_UP * M_UP)
                          ).then_inc(S("o_copied"), 1)
                        highs(base["O", b] + dt + 4, lows_by(kind, b))
                        if dt:
                            square(dt - 1)
                    square(KT - 1)
                    act.wait_ge(S("f_ss"), b + 1)
                    inverse_root(bank[2][:, 0:NT], 1.0 / D, eps, nF[0][:, 0:NT], nF[1][:, 0:NT], "f_root")
                    for k in range(KT):
                        A(hn[:, k, 0:NT], X[:, k, 0:NT], ACT.Copy, scale=gvec[:, KT + k:KT + k + 1]
                          ).then_inc(S("f_gained"), 1)
                    for k in range(KT):
                        act.wait_ge(S("f_scaled"), KT * b + k + 1)
                        A(H[:, 0, k, 0:NT], hn[:, k, 0:NT], ACT.Copy).then_inc(S("f_high"), 1)

                    def gate_and_up(c, i, ahead):
                        pairs = NF * b + (c - base["U", b]) // 2
                        for r in range(4):
                            if r % 2 == 0:
                                act.wait_ge(S("u_pair_free"), value(pairs + r // 2 + 1, i, 2))
                            act.wait_ge(S("products"), value(c + r + 1, i, 4))
                            func, up = (ACT.Silu, 1.0) if r % 2 == 0 else (ACT.Copy, U_UP)
                            A(ffev[:, r, 0:NT], bank[4 + r][:, 0:NT], func, scale=up / (W_UP * H_UP)
                              ).then_inc(S("u_bank_free"), 1)
                            highs(c + r + 4, lows_by(kind, b), i, 4, 128 * len(D_BLOCKS[r]) if ahead == "D" else WT)

                    with act.Fori(0, NF // 2 - 1) as i:
                        gate_and_up(base["U", b], i, "U")
                    gate_and_up(base["D", b] - 4, None, "D")

                    def down(c, i, ahead):
                        outs = KT * b + (c - base["D", b]) // ND
                        for r in range(2 * ND):
                            if r < ahead:
                                highs(c + r + 4, lows_by(kind, b), i, 2 * ND, 128 * len(D_BLOCKS[r % ND]))
                            if r % ND == ND - 1:
                                dt = r // ND
                                act.wait_ge(S("d_buf_free"), value(outs + dt + 1, i, 2))
                                act.wait_ge(S("products"), value(c + r + 1, i, 2 * ND))
                                A(ffev[:, dt, 0:NT], bank[dt][:, 0:NT], ACT.Copy, scale=1.0 / (W_UP * U_UP)
                                  ).then_inc(S("d_bank_free"), 1)

                    with act.Fori(0, KT // 2 - 1) as i:
                        down(base["D", b], i, 2 * ND)
                    down(base["D", b] + ND * (KT - 2), None, ND)
                    act.wait_ge(S("d_buf_free"), 2 + KT * (b + 1))
                    for k in range(KT):
                        A(H32[:, k, 0:NT], X[:, k, 0:NT], ACT.Square).then_inc(S("y_sq"), 1)
                    act.wait_ge(S("y_ss"), b + 1)
                    n = nY[b % 2]
                    inverse_root(bank[3][:, 0:NT], 1.0 / D, eps, n[0][:, 0:NT], n[1][:, 0:NT], "y_root")
                    for k in range(KT):
                        act.wait_ge(S("y_scaled"), KT * b + k + 1)
                        last = A(H32[:, k, 0:NT], X[:, k, 0:NT], ACT.Copy, scale=gvec[:, 2 * KT + k:2 * KT + k + 1])
                    last.then_inc(S("f_y"), 1)
                act.drain().then_inc(S("end_act"), 1)

        @block.vector
        def _(dve):
            v = nc.vector

            def newton(ms, r, tmp, out, up=1.0):
                v.tensor_tensor(tmp, r, r, ALU.mult)
                dve.drain()
                v.tensor_tensor(tmp, tmp, ms, ALU.mult)
                dve.drain()
                v.tensor_scalar(tmp, tmp, -0.5 * up, 1.5 * up, ALU.mult, ALU.add)
                dve.drain()
                v.tensor_tensor(out, tmp, r, ALU.mult)
                dve.drain()

            def lows(n, i=None, step=0, cols=WT):
                dve.wait_ge(S("w_high"), value(n + 1, i, step))
                v.scalar_tensor_tensor(ring[:, n % 4, 1, 0:cols], raw_at(n)[0][:, 0:cols], W_UP,
                                       ring[:, n % 4, 0, 0:cols], ALU.mult, ALU.subtract).then_inc(S("w_split"), 1)

            def lows_ahead(nph):
                tiles, low_by = first_tiles(nph)
                for n in tiles:
                    if low_by == "dve":
                        lows(n)

            def pick_round(rows, view):
                v.max(top8[rows, :], view)
                dve.drain()
                v.match_replace(view, top8[rows, :], view, TAKEN)
                dve.drain()

            def picked(view):
                v.tensor_scalar(view, view, TAKEN_CUT, OUTSIDE, ALU.is_ge, ALU.mult)

            EARLY_COLS = 20000

            def row_of(i):
                return Sf[:, score_at(i):score_at(i) + 128 * (i + 1)]

            def early_rounds(b):
                return min(ROUNDS, EARLY_COLS // (128 * (4 * b + 1))) if b < NBLK else 0

            def pick_block(b):
                if b < NBLK:
                    for i in tiles_of(b):
                        if b and i == 4 * b:
                            if early_rounds(b) < ROUNDS:
                                with dve.Fori(0, ROUNDS - early_rounds(b)):
                                    pick_round(slice(0, 128), row_of(i))
                            picked(row_of(i))
                            continue
                        late = LATE.get(b, {}).get(i, 0)
                        if i >= 2 and late < ROUNDS:
                            with dve.Fori(0, ROUNDS - late):
                                pick_round(slice(0, 128), row_of(i))
                            if not late:
                                picked(row_of(i))
                else:
                    with dve.Fori(0, (TOPK_S + 6) // 8):
                        pick_round(slice(0, 64), sscore)
                    picked(sscore)

            def late_picks(b):
                plan, start = {}, 0
                for i, rounds in LATE.get(b, {}).items():
                    units = range(start, HEADS * (i - 4 * b) - 1)
                    for n, u in enumerate(units):
                        plan.setdefault(u, []).append(
                            (i, rounds * (n + 1) // len(units) - rounds * n // len(units)))
                    start = units[-1] + 1
                return plan

            for nph, (kind, b) in enumerate(SCHED):
                NT = ntok(b)
                t0 = TOK * b
                if kind == "A":
                    a_start(dve, nph, b)
                elif kind == "I":
                    i_start(dve, nph, b)
                else:
                    phase_start(dve, nph)
                stored_before(dve, nph - (kind == "A" and b > 0))
                if kind == "B":
                    dve.wait_ge(S("consts_in"), 96)
                    v.memset(state[:, :, :], 0.0)
                    v.tensor_copy(relw[0:RB], relb[0:RB].unsqueeze(2).broadcast_to([RB, HEADS, 128])).then_inc(S("bias_wide"), 1)
                    for h in range(HEADS):
                        dve.wait_ge(S("bias_mm"), h + 1)
                        k = 3 * (h % 2)
                        v.tensor_scalar(row1[:, h, :], bank[k][:, 0:W1], Q_SCALE, None, ALU.mult)
                        v.tensor_copy(row2[:, h, 0:512], bank[k + 1][:, :])
                        v.tensor_copy(row2[:, h, 512:W2], bank[k + 2][:, 0:W2 - 512]).then_inc(S("bias_copied"), 1)
                    dve.drain().then_inc(S("bias_rows"), 1)
                    lows_ahead(nph)
                    dve.wait_ge(S("skew_dma"), 48)
                if kind == "P":
                    dve.wait_ge(S("p_root"), b + 1)
                    newton(*(n[:, 0:NT] for n in nP[b]), H_UP)
                    for k in range(KT):
                        v.scalar_tensor_tensor(hn[:, k, 0:NT], X[:, k, 0:NT], gvec[:, k:k + 1],
                                               nP[b][3][:, 0:NT], ALU.mult, ALU.mult)
                        dve.drain()
                        v.tensor_copy(H[:, 0, k, 0:NT], hn[:, k, 0:NT])
                        dve.drain()
                        v.tensor_tensor(H[:, 1, k, 0:NT], hn[:, k, 0:NT], H[:, 0, k, 0:NT], ALU.subtract
                                        ).then_inc(S("p_h"), 1)
                    C = CH if b < NBLK else TS
                    nc_ = NT // C

                    def gates_step(u):
                        if u == 5:
                            dve.wait_ge(S("g_mean"), b + 1)
                            v.scalar_tensor_tensor(ikc[:, 0:NT], bank[7][:, 0:NT], -1.0 / 128, ikx[:, 0:NT], ALU.mult, ALU.add)
                            dve.drain()
                            v.tensor_tensor(ikx[:, 0:NT], ikc[:, 0:NT], ikc[:, 0:NT], ALU.mult).then_inc(S("g_ikc"), 1)
                            dve.wait_ge(S("g_lsig"), b + 1)
                            v.scalar_tensor_tensor(la[:, :, 0:NT], la[:, :, 0:NT], 0.0, exa[:, :, 0:NT], ALU.min, ALU.subtract)
                            dve.wait_ge(S("g_rst"), b + 1)
                            dve.drain()
                            for j in range(2):
                                v.tensor_tensor_scan(cum[:, j, 0:NT], rst[:, 0:NT], la[:, j, 0:NT], 0.0, ALU.mult, ALU.add)
                            dve.drain()
                            for j in range(2):
                                def chunks(t):
                                    return t[:, j, 0:NT].rearrange("p (n c) -> p n c", c=C)
                                mid = chunks(cum)[:, :, C // 2 - 1:C // 2].broadcast_to([128, nc_, C])
                                end = chunks(cum)[:, :, C - 1:C].broadcast_to([128, nc_, C])
                                v.tensor_tensor(chunks(exa), chunks(cum), mid, ALU.subtract)
                                v.tensor_tensor(chunks(exb), end, chunks(cum), ALU.subtract)
                        if u == 9:
                            dve.wait_ge(S("g_ikr"), b + 1)
                            newton(nG[0][:, 0:NT], nG[1][:, 0:NT], nG[2][:, 0:NT], nG[3][:, 0:NT])
                            v.tensor_tensor(ikc[:, 0:NT], ikc[:, 0:NT], nG[3][:, 0:NT], ALU.mult)
                            dve.drain()
                            ik = ik32 if b < NBLK else ikTs[:, :]
                            v.tensor_scalar(ik, ikc[:, 0:NT], gates[:, 3:4], gates[:, 4:5], ALU.mult, ALU.add)
                            if b < NBLK:
                                dve.drain()
                                v.tensor_scalar(ikT[:, 0, t0:t0 + TOK], ik, I_UP, None, ALU.mult)
                                dve.drain()
                                v.scalar_tensor_tensor(ikT[:, 1, t0:t0 + TOK], ik, I_UP, ikT[:, 0, t0:t0 + TOK],
                                                       ALU.mult, ALU.subtract)
                            dve.drain().then_inc(S("g_cum"), 1)
                        if u == 14:
                            dve.wait_ge(S("g_ex"), b + 1)
                            dve.wait_ge(S("g_zero"), b + 1)
                            for e in range(2):
                                p = slice(64 * e, 64 * e + 64)
                                v.tensor_tensor(qgz[p, e::2, 0:NT], gq[p, :, 0:NT], exa[p, :, 0:NT], ALU.mult)
                                last = v.tensor_tensor(qiz[p, e::2, 0:NT], gq[p, :, 0:NT], la[p, :, 0:NT], ALU.mult)
                            last.then_inc(S("g_q"), 1)

                    back = 1.0 / (W_UP * H_UP)
                    for u, (what, j) in enumerate(TILES):
                        if b < NBLK and what in SPLIT:
                            dve.wait_ge(S("products"), base["P", b] + u + 1)
                            o = bank[u % 4]
                            if what == "k":
                                v.tensor_scalar(k32[:, j, :], o[:, :], back, None, ALU.mult)
                                v.tensor_scalar(kT[:, j, 0, t0:t0 + TOK], o[:, :], K_UP * back, None, ALU.mult)
                                dve.drain()
                                v.scalar_tensor_tensor(kT[:, j, 1, t0:t0 + TOK], o[:, :], K_UP * back,
                                                       kT[:, j, 0, t0:t0 + TOK], ALU.mult, ALU.subtract
                                                       ).then_inc(S("p_split"), 1)
                            else:
                                to, up = (iq, I_UP * back) if what == "iq" else (q, Q_UP * back)
                                for e in range(2):
                                    hi, lo = halves(e)
                                    v.tensor_scalar(to[hi, 2 * j + e, :], o[hi, :], up, None, ALU.mult)
                                dve.drain()
                                for e in range(2):
                                    hi, lo = halves(e)
                                    last = v.scalar_tensor_tensor(to[lo, 2 * j + e, :], o[hi, :], up,
                                                                  to[hi, 2 * j + e, :], ALU.mult, ALU.subtract)
                                last.then_inc(S("p_split"), 1)
                        if u + 4 < len(TILES):
                            lows(base["P", b] + u + 4)
                        gates_step(u)
                if kind == "G":
                    dve.wait_ge(S("g_zeros"), b + 1)
                    if b < NBLK:
                        for t in range(4):
                            T = 4 * b + t
                            dve.wait_ge(S("g_at"), T + 1)
                            if t >= 2:
                                dve.wait_ge(S("g_o"), 2 * T - 3)
                            for c in range(2):
                                p = slice(64 * c, 64 * c + 64)
                                last = v.tensor_tensor(
                                    att[p, t % 2, :, 64 * c:64 * c + 64],
                                    bank[2 + t % 2][p, 0:256].rearrange("p (h n) -> p h n", n=64),
                                    cst[p, C_TRI:C_TRI + 64].unsqueeze(1).broadcast_to([64, GH, 64]), ALU.mult)
                            last.then_inc(S("g_atm"), 1)
                            for c in range(2):
                                dve.wait_ge(S("g_o"), 2 * T + c + 1)
                                at = 128 * t + CH * c + CH - 1
                                for e in range(2):
                                    for j in range(2):
                                        p = slice(64 * e, 64 * e + 64)
                                        last = v.scalar_tensor_tensor(
                                            state[p, j, :], state[p, j, :], la[p, j, at:at + 1],
                                            bank[4 + c][p, j * 256 + e * 128:j * 256 + e * 128 + 128],
                                            ALU.mult, ALU.add)
                                last.then_inc(S("g_state"), 1)
                                dve.drain()
                    else:
                        dve.wait_ge(S("g_at"), 4 * NBLK + 1)
                        v.tensor_tensor(atts[0:NS], bank[2][0:NS, 0:256].rearrange("p (h n) -> p h n", n=64),
                                        cst[0:NS, C_TRI8:C_TRI8 + 64].unsqueeze(1).broadcast_to([NS, GH, 64]),
                                        ALU.mult).then_inc(S("g_atm"), 1)
                        dve.wait_ge(S("g_o"), 8 * NBLK + 1)
                        for s in range(DB):
                            dve.wait_ge(S("gs_u"), s + 1)
                            at = TS * s + TS - 1
                            for e in range(2):
                                for j in range(2):
                                    p = slice(64 * e, 64 * e + 64)
                                    last = v.scalar_tensor_tensor(
                                        sin[p, s, j, :], sin[p, s, j, :], la[p, j, at:at + 1],
                                        bank[4 + s % 2][p, j * 256 + e * 128:j * 256 + e * 128 + 128],
                                        ALU.mult, ALU.add)
                            last.then_inc(S("gs_new"), 1)
                if kind == "I" and b < NBLK:
                    for i in tiles_of(b):
                        if i < 2:
                            continue
                        row_at = score_at(i)
                        for c, (k0, kn) in enumerate(score_chunks(i)):
                            out = Sf[:, row_at + k0:row_at + k0 + kn]
                            for h in range(HEADS):
                                n = IN[i, c, h]
                                w = iw[:, i % 4, h:h + 1]
                                dve.wait_ge(S("i_relu"), n + 1)
                                if h == 0:
                                    v.tensor_scalar(out, relu[:, n % 4, 0:kn], w, None, ALU.mult).then_inc(S("i_added"), 1)
                                else:
                                    v.scalar_tensor_tensor(out, relu[:, n % 4, 0:kn], w, out, ALU.mult, ALU.add
                                                           ).then_inc(S("i_added"), 1)
                                dve.drain()
                if kind == "I" and b == NBLK:
                    dve.wait_ge(S("si_zero"), 1)
                    for h in range(HEADS):
                        e, j = h % 2, h // 2
                        p = slice(64 * e, 64 * e + 64)
                        last = v.tensor_copy(iqz[p, :, 8 * h:8 * h + 8], iqs[p, j, 0:NS].rearrange("p (s t) -> p s t", t=TS))
                    last.then_inc(S("si_iqz"), 1)
                    dve.wait_ge(S("rep_in"), 16)
                    for h in range(HEADS):
                        last = v.tensor_scalar(wrow[0:64, :, 8 * h:8 * h + 8], rep[0:64, :, 8 * h:8 * h + 8],
                                               iw[0:64, 0, h:h + 1], None, ALU.mult)
                    last.then_inc(S("si_wrow"), 1)
                    dve.wait_ge(S("si_sum"), DB)
                    v.tensor_tensor(sscore[:, PAST:LS], bank[7][0:64, 0:NS], cst[0:64, C_SEQ:C_SEQ + 64], ALU.add)
                if kind == "F":
                    if b == NBLK:
                        for t in range(4, KT + 4):
                            lows(base["O", b] + t)
                    if early_rounds(b + 1):
                        with dve.Fori(0, early_rounds(b + 1)):
                            pick_round(slice(0, 128), row_of(4 * b + 4))
                    dve.wait_ge(S("f_root"), b + 1)
                    newton(nF[0][:, 0:NT], nF[1][:, 0:NT], nF[2][:, 0:NT], nF[3][:, 0:NT], H_UP)
                    for k in range(KT):
                        dve.wait_ge(S("f_gained"), KT * b + k + 1)
                        v.tensor_tensor(hn[:, k, 0:NT], hn[:, k, 0:NT], nF[3][:, 0:NT], ALU.mult
                                        ).then_inc(S("f_scaled"), 1)
                if kind == "F" and b < NBLK:
                    pick_block(b + 1)
                if kind == "A" and b < NBLK:
                    def mask(i, h):
                        u = 8 * i + h
                        if u >= 2:
                            pi, ph = (u - 2) // 8, (u - 2) % 8
                            dve.wait_ge(S("a_pT"), TN[pi, ph, -(-(pi + 1) // 4) - 1] + 1)
                            dve.wait_ge(S("a_exp"), u - 1)
                        cs = near_chunks(i)
                        for c, (k0, kn, near) in enumerate(cs):
                            n = QN[i, h, c]
                            dve.wait_ge(S("a_logits"), n + 1)
                            if near:
                                dve.wait_ge(S("a_near"), u + 1)
                                m = nearm[:, u % 2, 0:kn]
                            else:
                                at = score_at(i) + k0
                                m = Sf[:, at:at + kn]
                            v.tensor_tensor_reduce(lg[:, u % 2, k0:k0 + kn], bank[n % 3][:, 0:kn], m, 1.0 / Q_SCALE, OUTSIDE,
                                                   ALU.add, ALU.max, mx[:, u % 2, c:c + 1]).then_inc(S("a_masked"), 1)
                        dve.drain()
                        v.tensor_reduce(nmax[:, u % 2:u % 2 + 1], mx[:, u % 2, 0:len(cs)], AX.X, ALU.max,
                                        negate=True).then_inc(S("a_max"), 1)

                    def scale(i, h):
                        u = 8 * i + h
                        dve.wait_ge(S("a_pv"), u + 1)
                        v.reciprocal(rden[:, u % 4:u % 4 + 1], den[:, u % 4:u % 4 + 1])
                        if h == 0 and i >= 2:
                            dve.wait_ge(S("a_oT"), i - 1)
                        dve.drain()
                        v.tensor_scalar(osb[:, i % 2, 64 * h:64 * h + 64], bank[5 + u % 2][:, 64 * (h // 4):64 * (h // 4) + 64],
                                        rden[:, u % 4:u % 4 + 1], None, ALU.mult).then_inc(S("a_scaled"), 1)

                    plan = late_picks(b)
                    units = [(i, h) for i in tiles_of(b) for h in range(HEADS)]
                    mask(*units[0])
                    for n in range(len(units)):
                        if n + 1 < len(units):
                            mask(*units[n + 1])
                        if n == 0:
                            lows_ahead(nph)
                        if n >= 2:
                            scale(*units[n - 2])
                        for i, rounds in plan.get(n, ()):
                            for _ in range(rounds):
                                pick_round(slice(0, 128), row_of(i))
                            if n == HEADS * (i - 4 * b) - 2:
                                picked(row_of(i))
                                dve.drain().then_inc(S("late_picked"), 1)
                    scale(*units[-2])
                    scale(*units[-1])
                if kind == "A" and b == NBLK:
                    dve.wait_ge(S("end_pe"), nph)
                    v.memset(qz, 0.0)
                    dve.drain()
                    for h in range(HEADS):
                        e, j = h % 2, h // 2
                        p = slice(64 * e, 64 * e + 64)
                        last = v.tensor_copy(qz[p, :, 8 * h:8 * h + 8], qs[p, j, 0:NS].rearrange("p (s t) -> p s t", t=TS))
                    last.then_inc(S("sa_qz"), 1)
                    dve.wait_ge(S("sbias_in"), 16)

                    def biased(s):
                        dve.wait_ge(S("sa_logits"), s + 1)
                        if s >= 2:
                            dve.wait_ge(S("sa_pT"), s - 1)
                        out = slg[0:64, s % 2, :]
                        past, new = bank[4 * (s % 2)], bank[4 * (s % 2) + 1]
                        v.tensor_tensor(out[:, 0:PAST], past[0:64, :], sbias[:, 0:PAST], ALU.add)
                        v.tensor_tensor(out[:, PAST:LS].rearrange("p (s t) -> p s t", t=TS),
                                        new[0:64, 0:NS].rearrange("p (s t) -> p s t", t=TS),
                                        sbias[:, PAST:PAST + TS].unsqueeze(1).broadcast_to([64, DB, TS]),
                                        ALU.add).then_inc(S("sa_added"), 1)
                        dve.drain()
                        v.tensor_reduce(nmax[0:64, s % 2:s % 2 + 1], out, AX.X, ALU.max, negate=True).then_inc(S("sa_max"), 1)

                    biased(0)
                    for s in range(DB):
                        dve.wait_ge(S("sa_exp"), s + 1)
                        out = slg[0:64, s % 2, :]
                        v.reciprocal(rden[0:64, s % 2:s % 2 + 1], den[0:64, s % 2:s % 2 + 1])
                        dve.drain()
                        v.tensor_scalar(out, out, rden[0:64, s % 2:s % 2 + 1], None, ALU.mult).then_inc(S("sa_probs"), 1)
                        if s + 1 < DB:
                            biased(s + 1)
                    lows_ahead(nph)
                    dve.wait_ge(S("sa_pv"), DB)
                    for h in range(HEADS):
                        e, j = h % 2, h // 2
                        src = bank[6][0:64, :].rearrange("p (s m) -> p s m", m=64)[:, :, 8 * h:8 * h + 8]
                        to = [mixA[64 * e:64 * e + 64, half, j, 0:NS].rearrange("p (s t) -> p s t", t=TS)
                              for half in range(2)]
                        v.tensor_scalar(to[0], src, M_UP, None, ALU.mult)
                        dve.drain()
                        v.scalar_tensor_tensor(to[1], src, M_UP, to[0], ALU.mult, ALU.subtract)
                if kind == "F" and b == NBLK:
                    with dve.Fori(0, NF // 2 - 1) as i:
                        for r in range(4):
                            lows(base["U", b] + 4 + r, i, 4)
                    for r in range(ND):
                        lows(base["D", b] + r, cols=128 * len(D_BLOCKS[r]))
                    with dve.Fori(0, KT - 1) as i:
                        for r in range(ND):
                            lows(base["D", b] + ND + r, i, ND, 128 * len(D_BLOCKS[r]))
                dve.drain().then_inc(S("end_dve"), 1)

        @block.gpsimd
        def _(pool):
            g = nc.gpsimd

            def newton(ms, r, tmp, out, up=1.0):
                g.tensor_tensor(tmp, r, r, ALU.mult)
                pool.drain()
                g.tensor_tensor(tmp, tmp, ms, ALU.mult)
                pool.drain()
                g.tensor_scalar(tmp, tmp, -0.5 * up, 1.5 * up, ALU.mult, ALU.add)
                pool.drain()
                g.tensor_tensor(out, tmp, r, ALU.mult)
                pool.drain()

            def lows(n, i=None, step=0, cols=WT):
                pool.wait_ge(S("w_high"), value(n + 1, i, step))
                g.tensor_tensor(ring[:, n % 4, 1, 0:cols], raw_at(n)[0][:, 0:cols], ring[:, n % 4, 0, 0:cols],
                                ALU.subtract).then_inc(S("w_split"), 1)

            for nph, (kind, b) in enumerate(SCHED):
                NT = ntok(b)
                if kind == "A":
                    a_start(pool, nph, b, waits_picks=True)
                elif kind == "I":
                    i_start(pool, nph, b)
                else:
                    phase_start(pool, nph)
                stored_before(pool, nph - (kind == "A" and b > 0))
                if kind == "B":
                    pool.wait_ge(S("consts_in"), 96)
                if kind == "P":
                    g.memset(rst[:, 0:NT], 1.0)
                    pool.drain()
                    g.memset(rst[:, 0:NT].rearrange("p (n c) -> p n c", c=CH if b < NBLK else TS)[:, :, 0:1], 0.0)
                    pool.drain().then_inc(S("g_rst"), 1)
                    g.memset(qgz[:, :, 0:NT], 0.0)
                    g.memset(qiz[:, :, 0:NT], 0.0)
                    pool.drain().then_inc(S("g_zero"), 1)
                    pool.wait_ge(S("g_ex"), b + 1)
                    g.tensor_tensor(kg[:, :, 0:NT], gk[:, :, 0:NT], kg[:, :, 0:NT], ALU.mult)
                    g.tensor_tensor(kh[:, :, 0:NT], gk[:, :, 0:NT], kh[:, :, 0:NT], ALU.mult)
                    pool.drain().then_inc(S("g_k"), 1)
                if kind == "G":
                    if b < NBLK:
                        g.memset(khz, 0.0)
                        g.memset(att, 0.0)
                    pool.drain().then_inc(S("g_zeros"), 1)
                    if b == NBLK:
                        for s in range(DB):
                            if s >= 2:
                                pool.wait_ge(S("gs_u"), s - 1)
                            g.tensor_scalar(gvz[0:NS, s % 2, :], gv[0:NS, 0, :], cst[0:NS, C_ROW + s:C_ROW + s + 1],
                                            None, ALU.mult).then_inc(S("gs_gvz"), 1)
                if kind == "G":
                    pool.wait_ge(S("g_root"), b + 1)
                    tmp = mixG[:, b % 2, :, :, :].rearrange("p s h n -> p (s h n)").bitcast(F32).rearrange(
                        "p (h n) -> p h n", n=TOK)[:, :, 0:NT]
                    out, r, gate = oT[:, :, 0:NT], oroot[:, :, 0:NT], gr[:, :, 0:NT]
                    high, low = (mixG[:, b % 2, half, :, 0:NT] for half in range(2))
                    newton(o2[:, :, 0:NT], r, tmp, r, M_UP)
                    g.tensor_tensor(out, out, r, ALU.mult)
                    pool.drain()
                    pool.wait_ge(S("g_silu"), b + 1)
                    g.tensor_tensor(out, out, gate, ALU.mult)
                    pool.drain()
                    g.tensor_copy(high, out)
                    pool.drain()
                    g.tensor_tensor(low, out, high, ALU.subtract)
                if kind == "I" and b == 0:
                    for i in range(2):
                        g.memset(Sf[:, score_at(i):score_at(i) + 128 * (i + 1)], 0.0)
                    pool.drain()
                if kind == "I" and b == NBLK:
                    g.memset(iqz, 0.0).then_inc(S("si_zero"), 1)
                    g.memset(sscore[:, LS:LS + 6], 3e38)
                tiles, low_by = first_tiles(nph)
                if low_by == "pool":
                    for n in tiles:
                        lows(n)
                if kind == "I" and b < NBLK:
                    for i in tiles_of(b):
                        if i >= 2:
                            pool.wait_ge(S("i_added"), IN[i, len(score_chunks(i)) - 1, HEADS - 1] + 1)
                        at = score_at(i) + 128 * i
                        diag = Sf[:, at:at + 128]
                        g.affine_select(out=diag, in_=diag, compare_op=ALU.is_ge, fill=OUTSIDE, base=0,
                                        pattern=[[-1, 128]], channel_multiplier=1)
                if kind == "A" and b < NBLK:
                    def mix_low(i):
                        cols = slice(128 * (i % 4), 128 * (i % 4) + 128)
                        pool.wait_ge(S("a_mix"), i + 1)
                        g.tensor_tensor(mixA[:, 1, :, cols], mix32, mixA[:, 0, :, cols], ALU.subtract
                                        ).then_inc(S("a_mix_low"), 1)

                    for i in tiles_of(b):
                        if i in LATE_TILES:
                            pool.wait_ge(S("late_picked"), LATE_TILES.index(i) + 1)
                        k0, kn, _near = near_chunks(i)[-1]
                        at = score_at(i) + k0
                        for h in range(HEADS):
                            u = 8 * i + h
                            if u >= 2:
                                pool.wait_ge(S("a_max"), u - 1)
                            g.tensor_tensor(nearm[:, u % 2, 0:kn], Sf[:, at:at + kn],
                                            near_bias[:, h, 256 - kn:256], ALU.add).then_inc(S("a_near"), 1)
                            if h == HEADS // 2 and i > 4 * b:
                                mix_low(i - 1)
                    mix_low(4 * b + 3)
                if kind == "F":
                    pool.wait_ge(S("x_in"), 16 * x_loads(nph))
                    by_pool = lows_by(kind, b) == "pool"
                    for dt in range(KT):
                        pool.wait_ge(S("o_copied"), KT * b + dt + 1)
                        g.tensor_tensor(X[:, dt, 0:NT], X[:, dt, 0:NT], outev[:, dt % 4, 0:NT], ALU.add
                                        ).then_inc(S("o_added"), 1)
                        if by_pool:
                            lows(base["O", b] + dt + 4)
                    for k in range(KT):
                        pool.wait_ge(S("f_high"), KT * b + k + 1)
                        last = g.tensor_tensor(H[:, 1, k, 0:NT], hn[:, k, 0:NT], H[:, 0, k, 0:NT], ALU.subtract)
                    last.then_inc(S("f_h"), 1)

                    def gated(c, i, ahead):
                        rows = (c - base["U", b]) // 2
                        for s in range(2):
                            if by_pool:
                                lows(c + 2 * s + 4, i, 4, 128 * len(D_BLOCKS[2 * s]) if ahead == "D" else WT)
                            pool.wait_ge(S("u_bank_free"), value(4 + 2 * NF * b + 2 * (rows + s) + 2, i, 4))
                            pool.sem_inc(S("pool_ticks"), 1)
                            gate, up = ffev[:, 2 * s, 0:NT], ffev[:, 2 * s + 1, 0:NT]
                            if i is None:
                                hi, lo = (U[:, rows + s, half, 0:NT] for half in range(2))
                            else:
                                hi, lo = (U[:, bass.ds(i * 2 + s, 1), half, 0:NT].rearrange("p a n -> p (a n)")
                                          for half in range(2))
                            g.tensor_tensor(hi, gate, up, ALU.mult)
                            pool.drain()
                            g.tensor_tensor(gate, gate, up, ALU.mult)
                            pool.drain()
                            g.tensor_tensor(lo, gate, hi, ALU.subtract).then_inc(S("u_pair_free"), 1)
                            if by_pool:
                                lows(c + 2 * s + 5, i, 4, 128 * len(D_BLOCKS[2 * s + 1]) if ahead == "D" else WT)

                    with pool.Fori(0, NF // 2 - 1) as i:
                        gated(base["U", b], i, "U")
                    gated(base["D", b] - 4, None, "D")

                    def added(c, i, ahead):
                        outs = (c - base["D", b]) // ND
                        for r in range(2 * ND):
                            if by_pool and r < ahead:
                                lows(c + r + 4, i, 2 * ND, 128 * len(D_BLOCKS[r % ND]))
                            if r % ND == ND - 1:
                                dt = r // ND
                                pool.wait_ge(S("d_bank_free"), value(2 + KT * b + outs + dt + 1, i, 2))
                                pool.sem_inc(S("pool_ticks"), 1)
                                x = (X[:, outs + dt, 0:NT] if i is None else
                                     X[:, bass.ds(i * 2 + dt, 1), 0:NT].rearrange("p a n -> p (a n)"))
                                g.tensor_tensor(x, x, ffev[:, dt, 0:NT], ALU.add).then_inc(S("d_buf_free"), 1)

                    with pool.Fori(0, KT // 2 - 1) as i:
                        added(base["D", b], i, 2 * ND)
                    added(base["D", b] + ND * (KT - 2), None, ND)
                    pool.wait_ge(S("y_root"), b + 1)
                    n = nY[b % 2]
                    newton(n[0][:, 0:NT], n[1][:, 0:NT], n[2][:, 0:NT], n[3][:, 0:NT])
                    for k in range(KT):
                        g.tensor_tensor(X[:, k, 0:NT], X[:, k, 0:NT], n[3][:, 0:NT], ALU.mult).then_inc(S("y_scaled"), 1)
                pool.drain().then_inc(S("end_pool"), 1)


def outputs_of():
    return {
        "o_y": (128, KT, ALLT), "o_k": (64, KVH, ALLT), "o_v": (ALLT, KVH * HD), "o_ik": (64, ALLT),
        "o_gp": (128, 2, DV), "o_gs": (128, DB, 2, DV),
    }


def laid_out(i):
    def tiles(w, cols):
        return w.reshape(KT, 128, cols).transpose(1, 0, 2).reshape(128, KT * cols)

    w = np.asarray(i["w_in"])[0]
    at = dict(q=0, k=512, v=640, iq=768, ik=1280, iw=1344, gq=1352, gk=1608, gv=1864, gr=2376, glr=2888)
    parts = []
    for what, j in TILES:
        if what == "k":
            c = w[:, at["k"] + 64 * j:at["k"] + 64 * j + 64]
            c = np.concatenate([c, c], 1)
        elif what == "ik":
            c = w[:, at["ik"]:at["ik"] + 64]
            c = np.concatenate([c, c], 1)
        elif what == "glr":
            c = np.concatenate([w[:, at["glr"]:at["glr"] + RANK], w[:, at["iw"]:at["iw"] + 8],
                                np.zeros((D, 128 - RANK - 8), w.dtype)], 1)
        else:
            c = w[:, at[what] + 128 * j:at[what] + 128 * j + 128]
        parts.append(tiles(c, 128))
    wo, wg, wu, wd = (np.asarray(i[n])[0] for n in ("w_out", "w_gate", "w_up", "w_down"))
    x = np.concatenate([np.asarray(i["x_prompt"])[0], np.asarray(i["x_sample"]).reshape(NS, D)], 0)
    ck, cv, ci = (np.asarray(i[n])[0] for n in ("cache_k", "cache_v", "cache_idx_k"))
    kt = ck.transpose(0, 3, 2, 1)
    kt = np.concatenate([kt, kt], 1).reshape(NPOOL, 128, 256)
    it = ci.transpose(0, 2, 1)
    cache = np.concatenate([kt, np.concatenate([it, it], 1), cv.reshape(NPOOL, 128, 128)], 2)
    cst, rep, hots = constants()

    def col(v):
        return np.asarray(v).reshape(-1, 128).T

    kn = [np.concatenate([np.asarray(i[n])[0]] * 2) for n in ("idx_knorm_g", "idx_knorm_b")]
    out = {
        "xT": x.T.reshape(KT, 128, ALLT).transpose(1, 0, 2),
        "w_in": np.stack(parts),
        "w_out": np.stack([tiles(wo[:, 128 * t:128 * t + 128], 128) for t in range(KT)]),
        "w_gu": np.stack([np.concatenate([tiles(m[:, 128 * f:128 * f + 128], 128) for m in (wg, wu)], 1)
                          for f in range(NF)]),
        "w_d": wd.reshape(NF, 128, KT, 128).transpose(2, 1, 0, 3).reshape(KT, 128, NF * 128),
        "cache": cache,
        "state": np.asarray(i["state_gla"])[0],
        "pages": np.asarray(i["page_table"]).reshape(1, DB * NPG),
        "gains": np.concatenate([col(i["attn_norm_g"]), col(i["ffn_norm_g"]), col(i["final_norm_g"])], 1),
        "gates": np.concatenate([col(i["gla_gate_b"]), col(i["gla_onorm_g"]), col(kn[0]), col(kn[1])], 1),
        "gate_up": np.asarray(i["gla_gate_up"])[0],
        "rel_bias": np.asarray(i["rel_bias"]),
        "consts": cst, "rep": rep, "hots": hots,
    }
    return {k: np.ascontiguousarray(v) for k, v in out.items()}


def returned(r):
    y = r["o_y"].transpose(1, 0, 2).reshape(D, ALLT).T
    k = r["o_k"].transpose(2, 1, 0)
    vv = r["o_v"].reshape(ALLT, KVH, HD)
    ik = r["o_ik"].T
    gp = r["o_gp"].reshape(2, 64, 2, DV).transpose(2, 0, 1, 3).reshape(1, 1, GH, DK, DV)
    gs = r["o_gs"].reshape(2, 64, DB, 2, DV).transpose(2, 3, 0, 1, 4).reshape(1, DB, GH, DK, DV)
    c = np.ascontiguousarray
    return (c(y[:SEQ].reshape(1, SEQ, D)), c(y[SEQ:].reshape(DB, TS, D)),
            c(k[:SEQ].reshape(1, 1, SEQ, KVH, HD)), c(vv[:SEQ].reshape(1, 1, SEQ, KVH, HD)),
            c(ik[:SEQ].reshape(1, 1, SEQ, HD)), c(gp),
            c(k[SEQ:].reshape(1, DB, TS, KVH, HD)), c(vv[SEQ:].reshape(1, DB, TS, KVH, HD)),
            c(ik[SEQ:].reshape(1, DB, TS, HD)), c(gs))


def kernel(**inputs):
    import concourse.bacc as bacc
    from concourse.bass_utils import run_bass_kernel_spmd

    arrays = {"in_" + n: v for n, v in laid_out(inputs).items()}
    nc = bacc.Bacc("TRN2", target_bir_lowering=False, num_devices=1)
    a = {n[3:]: nc.dram_tensor(n, v.shape, mybir.dt.from_np(v.dtype), kind="ExternalInput").ap()
         for n, v in arrays.items()}
    for n, shape in outputs_of().items():
        a[n] = nc.dram_tensor(n, shape, F32, kind="ExternalOutput").ap()
    layer(nc, a)
    r = run_bass_kernel_spmd(nc, [arrays], core_ids=[0])
    return returned(r.results[0])
```
